# Optimizing a Trainium2 kernel written in Bass

```python
import jax, jax.numpy as jnp
from jax import lax
import numpy as np

D_MODEL = 1024
BATCH = 1
SEQ = 1024
DEPTH = 1

ATTN_HEADS = 16
ATTN_KV_HEADS = 4
ATTN_HEAD_DIM = 64
ATTN_GROUPS = ATTN_HEADS // ATTN_KV_HEADS
ATTN_WIDTH = ATTN_HEADS * ATTN_HEAD_DIM
ATTN_KV_WIDTH = ATTN_KV_HEADS * ATTN_HEAD_DIM
WINDOW = 128
ATTN_BLOCK = 128

MLSTM_HEADS = 8
MLSTM_QK_DIM = 64
MLSTM_V_DIM = 128
MLSTM_QK_WIDTH = MLSTM_HEADS * MLSTM_QK_DIM
MLSTM_V_WIDTH = MLSTM_HEADS * MLSTM_V_DIM
MLSTM_CHUNK = 64
CONV_WIDTH = 4
FORGET_BIAS_LO = 3.0
FORGET_BIAS_HI = 6.0
M_INIT = -1e30

RMS_EPS = 1e-6

SPLIT_SIZES = (ATTN_WIDTH, ATTN_KV_WIDTH, ATTN_KV_WIDTH, ATTN_WIDTH,
               MLSTM_QK_WIDTH, MLSTM_QK_WIDTH, MLSTM_V_WIDTH, MLSTM_HEADS, MLSTM_HEADS,
               MLSTM_V_WIDTH, MLSTM_V_WIDTH, D_MODEL, D_MODEL)
SPLIT_IDX = tuple(sum(SPLIT_SIZES[:i + 1]) for i in range(len(SPLIT_SIZES) - 1))
PROJ_WIDTH = sum(SPLIT_SIZES)
F_GATE_OFFSET = sum(SPLIT_SIZES[:8])

kernel_name = 'hybrid_swa_sink_mlstm_gated_merge'

def rms_norm(x, w):
    xf = x.astype(jnp.float32)
    y = xf * lax.rsqrt(jnp.mean(xf * xf, axis=-1, keepdims=True) + RMS_EPS)
    return (y * w.astype(jnp.float32)).astype(x.dtype)

def head_rms_norm(h, w):
    y = h * lax.rsqrt(jnp.mean(h * h, axis=-1, keepdims=True) + RMS_EPS)
    return y * w.astype(jnp.float32).reshape(MLSTM_HEADS, MLSTM_V_DIM)

def sliding_window_sink_attention(q, k, v, sinks):
    B, T = q.shape[0], q.shape[1]
    nb = T // ATTN_BLOCK
    qb = q.reshape(B, nb, ATTN_BLOCK, ATTN_KV_HEADS, ATTN_GROUPS, ATTN_HEAD_DIM)
    kb = k.reshape(B, nb, ATTN_BLOCK, ATTN_KV_HEADS, ATTN_HEAD_DIM)
    vb = v.reshape(B, nb, ATTN_BLOCK, ATTN_KV_HEADS, ATTN_HEAD_DIM)

    def with_prev(t):
        prev = jnp.concatenate([jnp.zeros_like(t[:, :1]), t[:, :-1]], axis=1)
        return jnp.concatenate([prev, t], axis=2)

    kw, vw = with_prev(kb), with_prev(vb)
    scores = jnp.einsum('bnqkgd,bnskd->bnkgqs', qb, kw).astype(jnp.float32) * (ATTN_HEAD_DIM ** -0.5)
    blk = jnp.arange(nb)[:, None] * ATTN_BLOCK
    q_pos = blk + jnp.arange(ATTN_BLOCK)[None, :]
    k_pos = blk - ATTN_BLOCK + jnp.arange(2 * ATTN_BLOCK)[None, :]
    rel = q_pos[:, :, None] - k_pos[:, None, :]
    allowed = (rel >= 0) & (rel < WINDOW) & (k_pos[:, None, :] >= 0)
    scores = jnp.where(allowed[None, :, None, None], scores, -jnp.inf)
    sink = sinks.astype(jnp.float32).reshape(ATTN_KV_HEADS, ATTN_GROUPS)[None, None, :, :, None, None]
    sink = jnp.broadcast_to(sink, scores.shape[:-1] + (1,))
    probs = jax.nn.softmax(jnp.concatenate([scores, sink], axis=-1), axis=-1)[..., :-1]
    out = jnp.einsum('bnkgqs,bnskd->bnqkgd', probs.astype(v.dtype), vw)
    return out.reshape(B, T, ATTN_WIDTH)

def causal_depthwise_conv(u, w, b):
    out = lax.conv_general_dilated(u, w[:, None, :], window_strides=(1,),
                                   padding=[(CONV_WIDTH - 1, 0)],
                                   dimension_numbers=('NWC', 'WIO', 'NWC'),
                                   feature_group_count=u.shape[-1])
    return out + b

def mlstm_chunkwise(q, k, v, i_pre, f_pre):
    B, T, H, dk = q.shape
    dv = v.shape[-1]
    nc = T // MLSTM_CHUNK

    def chunked(t):
        return jnp.moveaxis(t.reshape((B, nc, MLSTM_CHUNK) + t.shape[2:]), 3, 1)

    q = chunked(q) * (dk ** -0.5)
    k = chunked(k)
    v = chunked(v)
    ig = chunked(i_pre)
    logf = jax.nn.log_sigmoid(chunked(f_pre))
    b = jnp.cumsum(logf, axis=-1)
    causal = jnp.tril(jnp.ones((MLSTM_CHUNK, MLSTM_CHUNK), dtype=bool))
    log_d = jnp.where(causal, b[..., :, None] - b[..., None, :] + ig[..., None, :], -jnp.inf)

    g = b[..., -1]
    a = g[..., None] - b + ig
    m_loc = jnp.max(a, axis=-1)
    wts = jnp.exp(a - m_loc[..., None])
    c_loc = jnp.einsum('bhcl,bhclv,bhclk->bhcvk', wts, v, k)
    n_loc = jnp.einsum('bhcl,bhclk->bhck', wts, k)

    def step(carry, inp):
        c, n, m = carry
        g_c, m_l, c_l, n_l = inp
        m_new = jnp.maximum(g_c + m, m_l)
        s_prev = jnp.exp(g_c + m - m_new)
        s_loc = jnp.exp(m_l - m_new)
        c_new = s_prev[..., None, None] * c + s_loc[..., None, None] * c_l
        n_new = s_prev[..., None] * n + s_loc[..., None] * n_l
        return (c_new, n_new, m_new), (c, n, m)

    init = (jnp.zeros((B, H, dv, dk), q.dtype), jnp.zeros((B, H, dk), q.dtype),
            jnp.full((B, H), M_INIT, q.dtype))
    xs = (jnp.moveaxis(g, 2, 0), jnp.moveaxis(m_loc, 2, 0),
          jnp.moveaxis(c_loc, 2, 0), jnp.moveaxis(n_loc, 2, 0))
    _, (c_prev, n_prev, m_prev) = lax.scan(step, init, xs)
    c_prev = jnp.moveaxis(c_prev, 0, 2)
    n_prev = jnp.moveaxis(n_prev, 0, 2)
    m_prev = jnp.moveaxis(m_prev, 0, 2)

    m_inter = b + m_prev[..., None]
    m_row = jnp.maximum(m_inter, jnp.max(log_d, axis=-1))
    s = jnp.einsum('bhclk,bhcsk->bhcls', q, k) * jnp.exp(log_d - m_row[..., None])
    inter = jnp.exp(m_inter - m_row)
    num = jnp.einsum('bhcls,bhcsv->bhclv', s, v) + inter[..., None] * jnp.einsum('bhcvk,bhclk->bhclv', c_prev, q)
    den = jnp.sum(s, axis=-1) + inter * jnp.einsum('bhck,bhclk->bhcl', n_prev, q)
    h = num / jnp.maximum(jnp.abs(den), jnp.exp(-m_row))[..., None]
    return jnp.moveaxis(h, 1, 3).reshape(B, T, H, dv)

def hybrid_layer(x, norm_w, w_in, b_in, attn_sinks, conv_w, conv_b, mlstm_norm_w,
                 w_branch_attn, w_branch_mlstm, w_out):
    B, T, _ = x.shape
    f32 = jnp.float32
    h = rms_norm(x, norm_w)
    proj = jnp.einsum('btd,de->bte', h, w_in) + b_in
    (a_q, a_k, a_v, a_z, m_q, m_k, m_v, m_i, m_f, m_o, m_z,
     g_attn, g_mlstm) = jnp.split(proj, SPLIT_IDX, axis=-1)

    attn = sliding_window_sink_attention(a_q.reshape(B, T, ATTN_HEADS, ATTN_HEAD_DIM),
                                         a_k.reshape(B, T, ATTN_KV_HEADS, ATTN_HEAD_DIM),
                                         a_v.reshape(B, T, ATTN_KV_HEADS, ATTN_HEAD_DIM),
                                         attn_sinks)
    branch_a = jnp.einsum('bte,ed->btd', attn * jax.nn.silu(a_z), w_branch_attn)

    qk = jax.nn.silu(causal_depthwise_conv(jnp.concatenate([m_q, m_k], axis=-1), conv_w, conv_b))
    mq, mk = jnp.split(qk, 2, axis=-1)
    h_tilde = mlstm_chunkwise(mq.reshape(B, T, MLSTM_HEADS, MLSTM_QK_DIM).astype(f32),
                              mk.reshape(B, T, MLSTM_HEADS, MLSTM_QK_DIM).astype(f32),
                              m_v.reshape(B, T, MLSTM_HEADS, MLSTM_V_DIM).astype(f32),
                              m_i.astype(f32), m_f.astype(f32))
    h_m = head_rms_norm(h_tilde, mlstm_norm_w).reshape(B, T, MLSTM_V_WIDTH).astype(x.dtype)
    h_m = jax.nn.sigmoid(m_o) * h_m * jax.nn.silu(m_z)
    branch_m = jnp.einsum('bte,ed->btd', h_m, w_branch_mlstm)

    merged = jax.nn.sigmoid(g_attn) * branch_a + jax.nn.sigmoid(g_mlstm) * branch_m
    return x + jnp.einsum('btd,de->bte', merged, w_out)

def setup_inputs(seed: int = 0) -> dict:
    key = jax.random.key(seed)
    ks = jax.random.split(key, 12)
    nrm = jax.random.normal
    x = nrm(ks[0], (BATCH, SEQ, D_MODEL), jnp.float32)
    norm_w = 1.0 + 0.02 * nrm(ks[1], (DEPTH, D_MODEL), jnp.float32)
    w_in = nrm(ks[2], (DEPTH, D_MODEL, PROJ_WIDTH), jnp.float32) * (D_MODEL ** -0.5)
    b_in = 0.01 * nrm(ks[3], (DEPTH, PROJ_WIDTH), jnp.float32)
    b_in = b_in.at[:, F_GATE_OFFSET:F_GATE_OFFSET + MLSTM_HEADS].add(
        jnp.linspace(FORGET_BIAS_LO, FORGET_BIAS_HI, MLSTM_HEADS, dtype=jnp.float32))
    attn_sinks = 0.5 * nrm(ks[4], (DEPTH, ATTN_HEADS), jnp.float32)
    conv_w = nrm(ks[5], (DEPTH, CONV_WIDTH, 2 * MLSTM_QK_WIDTH), jnp.float32) * (CONV_WIDTH ** -0.5)
    conv_b = 0.01 * nrm(ks[6], (DEPTH, 2 * MLSTM_QK_WIDTH), jnp.float32)
    mlstm_norm_w = 1.0 + 0.02 * nrm(ks[7], (DEPTH, MLSTM_V_WIDTH), jnp.float32)
    w_branch_attn = nrm(ks[8], (DEPTH, ATTN_WIDTH, D_MODEL), jnp.float32) * (ATTN_WIDTH ** -0.5)
    w_branch_mlstm = nrm(ks[9], (DEPTH, MLSTM_V_WIDTH, D_MODEL), jnp.float32) * (MLSTM_V_WIDTH ** -0.5)
    w_out = nrm(ks[10], (DEPTH, D_MODEL, D_MODEL), jnp.float32) * (D_MODEL ** -0.5)
    final_norm_w = 1.0 + 0.02 * nrm(ks[11], (D_MODEL,), jnp.float32)
    return {'x': x, 'norm_w': norm_w, 'w_in': w_in, 'b_in': b_in, 'attn_sinks': attn_sinks,
            'conv_w': conv_w, 'conv_b': conv_b, 'mlstm_norm_w': mlstm_norm_w,
            'w_branch_attn': w_branch_attn, 'w_branch_mlstm': w_branch_mlstm,
            'w_out': w_out, 'final_norm_w': final_norm_w}

def reference(x, norm_w, w_in, b_in, attn_sinks, conv_w, conv_b, mlstm_norm_w,
              w_branch_attn, w_branch_mlstm, w_out, final_norm_w):
    for layer in range(DEPTH):
        x = hybrid_layer(x, norm_w[layer], w_in[layer], b_in[layer], attn_sinks[layer],
                         conv_w[layer], conv_b[layer], mlstm_norm_w[layer],
                         w_branch_attn[layer], w_branch_mlstm[layer], w_out[layer])
    return rms_norm(x, final_norm_w)


_drawn_inputs = setup_inputs


def setup_inputs(seed=0):
    import zlib

    import numpy as np

    out = dict(_drawn_inputs(seed))
    spreads = {}
    factors = {'norm_w': 6.757,
     'attn_sinks': 200.0,
     'conv_b': 64.0,
     'mlstm_norm_w': 110.849,
     'final_norm_w': 22.621}
    for name, (base, spread) in spreads.items():
        noise = np.random.default_rng([zlib.crc32(name.encode()), seed]).standard_normal(out[name].shape)
        drawn = base * np.exp(spread * noise) if base else spread * noise
        out[name] = __import__('jax').numpy.asarray(drawn.astype(out[name].dtype))
    for name, factor in factors.items():
        out[name] = (out[name] * factor).astype(out[name].dtype)
    return out
```

```python
import concourse.bass as bass
from concourse import mybir
from contextlib import ExitStack

F32 = mybir.dt.float32
F32R = mybir.dt.float32r
BF16 = mybir.dt.bfloat16
I8 = mybir.dt.int8
ALU = mybir.AluOpType
ACT = mybir.ActivationFunctionType
AXX = mybir.AxisListType.X
ds = bass.ds

P = 128
D = 1024
T = 1024
KT = D // P
NB = T // P
HEADS, KV, HD = 16, 4, 64
GR = HEADS // KV
MH, MK, MV = 8, 64, 128
PAIRS = MH // 2
EPS = 1e-6
NEG = -1e30
BANK = 512

Q0, K0, V0, Z0 = 0, 1024, 1280, 1536
MQ0, MK0, MV0, MI0, MF0, MO0, MZ0, GA0, GM0 = 2560, 3072, 3584, 4608, 4616, 4624, 5648, 6672, 7696
R_Q, R_K, R_V, R_Z, R_MQ, R_MK, R_MV, R_O, R_MZ, R_GA, R_GM = 0, 8, 10, 12, 20, 24, 28, 36, 44, 52, 60
R_NORM, R_MNORM, R_CONVW, R_CONVB, ROWS = 68, 76, 84, 116, 124

S1, S2, S3, S4, S5 = 0, 5, 21, 37, 77
S6 = 85
TERMS = 3
MMS = 2 * KT * TERMS


def slot(t):
    return t % 2


def until(eng, sem, value):
    if isinstance(value, int) and value <= 0:
        return
    eng.wait_ge(sem, value)


def later(i):
    return not (isinstance(i, int) and i == 0)


def looped(eng, count, body):
    body(0)
    with eng.Fori(1, count) as i:
        body(i)


def build(nc, x, norm_w, w_in, b_in, sinks, conv_w, conv_b, mnorm_w, wba, wbm, w_out, fnorm_w, out):
    ctx = ExitStack()
    with ctx:
        def sb(name, shape, dt=F32, stack=None):
            return (stack or ctx).enter_context(nc.sbuf_tensor(name, shape, dt))

        def sem(name):
            return ctx.enter_context(nc.semaphore(name))

        hT_hi = sb("hT_hi", [P, KT, T], F32R)
        hT_lo = sb("hT_lo", [P, KT, T], F32R)
        w_raw = sb("w_raw", [P, 2, KT, P])
        w_hi = [sb(f"w_hi{s}", [P, KT, P], F32R) for s in range(2)]
        w_lo = [sb(f"w_lo{s}", [P, KT, P], F32R) for s in range(2)]
        ev = [sb(f"ev{s}", [P, T]) for s in range(2)]
        ident = sb("ident", [P, P])
        ident_b = sb("ident_b", [P, P], BF16)
        par = sb("par", [P, ROWS])
        par_half = sb("par_half", [P, ROWS])
        from_prev = sb("from_prev", [P, P], I8)
        cur_T = sb("cur_T", [P, P])
        prev_T = sb("prev_T", [P, P])
        causal = sb("causal", [P, P], BF16)
        ones_r = sb("ones_r", [40, P], F32R)
        head_col = sb("head_col", [40, MH])
        pair_mask = sb("pair_mask", [MH, PAIRS, NB])
        decay_rows = sb("decay_rows", [MH, PAIRS, NB])
        decay_tab = sb("decay_tab", [P, PAIRS, NB])
        gate_bias = sb("gate_bias", [40, 1])
        sink_tab = sb("sink_tab", [P, HEADS])
        zero_col = sb("zero_col", [P, 1])
        neg_col = sb("neg_col", [P, 1])
        sumsq = sb("sumsq", [P, 2 * NB])
        rstd = sb("rstd", [P, 2 * NB])
        m_before = sb("m_before", [MH, NB])
        decay = sb("decay", [MH, NB])
        row_max = sb("row_max", [P, GR])
        neg_max = sb("neg_max", [P, GR])
        sink_in = sb("sink_in", [P, GR])
        sink_exp = sb("sink_exp", [P, GR])
        row_sum = sb("row_sum", [P, GR])
        row_inv = sb("row_inv", [P, GR])
        tok_gate = sb("tok_gate", [P, NB, 4, 2])
        pair_decay = sb("pair_decay", [P, NB])
        pair_norm = sb("pair_norm", [P, 2])
        den = sb("den", [P, 2])
        den_inv = sb("den_inv", [P, NB, 2])

        def aliased(groups):
            made = []
            for g in groups:
                with ExitStack() as st:
                    made.append([sb(*a, stack=st) for a in g])
            return made

        (gate_T, c_split), (th_gm,) = aliased([
            [("gate_T", [P, NB, P]), ("c_split", [40, T])],
            [("th_gm", [P, 2, T])]])
        ctx.enter_context(nc.sbuf_tensor("hold_gates", [P, 2, T], F32))
        (xs,), gt, (U,), (wo_hi,) = aliased([
            [("xs", [P, NB, T])],
            [(f"gt{i}", [P, T]) for i in range(7)] + [("gt_r", [P, T], F32R)],
            [("U", [P, KT, T])],
            [("wo_hi", [P, KT, T], F32R)]])
        ctx.enter_context(nc.sbuf_tensor("hold_u", [P, KT, T], F32))
        att, (u_hi, u_lo), ml, (merged, wo_lo) = aliased([
            [("k_dup", [P, KV, T]), ("v_tok", [P, NB, KV * HD]), ("k_pad", [P, 2, T]), ("v_head", [P, NB, HD]),
             ("q_T", [P, 2, T]), ("attn_T", [P, 2, T]), ("silu_z", [P, 2, T]),
             ("probs0", [P, GR, P]), ("probs1", [P, GR, P]), ("pT_cur", [P, GR, P]), ("pT_prev", [P, GR, P])],
            [("u_hi", [P, KT, T], F32R), ("u_lo", [P, KT, T], F32R)],
            [("raw_q", [P, T + 3]), ("raw_k", [P, T + 3]), ("mq_pad", [P, 2, T]), ("mk_T", [P, T]),
             ("v1", [P, NB, 2, MV + 1]), ("h_tok", [P, NB, 2, MV + 1]), ("gates", [P, 2, T]), ("z_buf", [P, T]),
             ("tanh_buf", [P, T]), ("dmat", [P, 2, P]), ("s_T", [P, 2, P]), ("inter", [P, 2, MV + 1]),
             ("k_w", [P, 2, MK]), ("state", [P, MV + 1]), ("c_heads", [40, 2, T], F32R), ("junk", [P, MV])],
            [("merged", [P, KT, T]), ("wo_lo", [P, KT, T], F32R)]])
        k_dup, v_tok, k_pad, v_head, q_T, attn_T, silu_z, probs0, probs1, pT_cur, pT_prev = att
        probs = [probs0, probs1]
        param_rows = pT_prev[:, 0, :]
        ones8 = pT_cur[0:MH, 0, :]
        parity_sel = pT_cur[0:MH, 1, :]
        (raw_q, raw_k, mq_pad, mk_T, v1, h_tok, gates, z_buf, tanh_buf, dmat, s_T, inter, k_w, state,
         c_heads, junk) = ml
        g_i, g_f, g_t1, g_t2, g_t3, g_t4, g_t5 = gt[:7]
        c_hi = gt[7]

        ps = ctx.enter_context(nc.psum_tensor("ps", [P, 8, BANK], F32))
        X = [4, 5, 6, 7]

        def dense_ps(t):
            return ps[:, 2 * slot(t):2 * slot(t) + 2, :].rearrange("p b n -> p (b n)")

        scr_a = nc.dram_tensor("branch_a_scratch", [KT, P, T], F32).ap()
        scr_g = nc.dram_tensor("tanh_gm_scratch", [KT, P, T], F32).ap()

        params_in = sem("params_in")
        x_in = [sem(f"x_in{i}") for i in range(4)]
        gate_slot_clear = sem("gate_slot_clear")
        w_in_sem = [sem(f"w_landed{s}") for s in range(2)]
        w_split = sem("w_split")
        tile_done = sem("tile_done")
        tile_out = sem("tile_out")
        consts_made = sem("consts_made")
        params_T = sem("params_T")
        params_ready = sem("params_ready")
        x_sumsq = sem("x_sumsq")
        x_var = sem("x_var")
        x_root = sem("x_root")
        x_norm = sem("x_norm")
        x_turned = sem("x_turned")
        hT_hi_ready = sem("hT_hi_ready")
        hT_lo_ready = sem("hT_lo_ready")
        g_log = sem("g_log")
        g_rows = sem("g_rows")
        g_exp = sem("g_exp")
        g_turned = sem("g_turned")
        g_ready = sem("g_ready")
        v_turned = sem("v_turned")
        v_ready = sem("v_ready")
        kv_head_ready = sem("kv_head_ready")
        scores_done = sem("scores_done")
        cur_copied = sem("cur_copied")
        max_ready = sem("max_ready")
        exp_ready = sem("exp_ready")
        probs_ready = sem("probs_ready")
        probs_turned = sem("probs_turned")
        pT_ready = sem("pT_ready")
        pv_done = sem("pv_done")
        attn_ready = sem("attn_ready")
        z_tanh = sem("z_tanh")
        u_ready = sem("u_ready")
        u_hi_ready = sem("u_hi_ready")
        u_split = sem("u_split")
        branch_a = sem("branch_a")
        branch_a_out = sem("branch_a_out")
        m_clear = sem("m_clear")
        m_raw = sem("m_raw")
        m_conv = sem("m_conv")
        m_tanh = sem("m_tanh")
        m_qk = sem("m_qk")
        m_v_turned = sem("m_v_turned")
        m_v_ready = sem("m_v_ready")
        m_tabs = sem("m_tabs")
        m_scores = sem("m_scores")
        m_decay = sem("m_decay")
        m_inter = sem("m_inter")
        m_sT = sem("m_sT")
        m_prod = sem("m_prod")
        m_state = sem("m_state")
        m_den = sem("m_den")
        m_sumsq = sem("m_sumsq")
        m_var = sem("m_var")
        m_root = sem("m_root")
        m_h = sem("m_h")
        m_h_turned = sem("m_h_turned")
        mz_tanh = sem("mz_tanh")
        mz_used = sem("mz_used")
        gm_ready = sem("gm_ready")
        gm_out = [sem(f"gm_out{s}") for s in range(2)]
        merged_in = sem("merged_in")
        th_in = [sem(f"th_in{s}") for s in range(2)]
        merged_ready = sem("merged_ready")
        mt_hi_ready = sem("mt_hi_ready")
        mt_ready = sem("mt_ready")
        fn_in = sem("fn_in")
        x_again = [sem(f"x_again{s}") for s in range(2)]
        res_ready = sem("res_ready")
        res_sumsq = sem("res_sumsq")
        res_var = sem("res_var")
        res_root = sem("res_root")
        y_ready = sem("y_ready")
        y_out = [sem(f"y_out{s}") for s in range(2)]

        passed = sem("passed")
        sp_passed = sem("sp_passed")

        mt_hi = [hT_hi[:, s, :].rearrange("p (k n) -> p k n", k=KT) for s in range(2)]
        mt_lo = [hT_lo[:, s, :].rearrange("p (k n) -> p k n", k=KT) for s in range(2)]
        x_tile = th_gm
        fnw = w_raw[:, 0].rearrange("p k n -> p (k n)")
        squares = w_raw[:, 1].rearrange("p k n -> p (k n)")

        block = ctx.enter_context(nc.Block())

        w_cols = w_in.rearrange("(k p) n -> p k n", p=P)
        wba_cols = wba.rearrange("(k p) n -> p k n", p=P)
        wbm_cols = wbm.rearrange("(k p) n -> p k n", p=P)
        x_rows = x.rearrange("(t p) d -> p t d", p=P)
        out_rows = out.rearrange("(t p) d -> p t d", p=P)

        @block.sync
        def _(sp):
            for row, src in ((R_Q, b_in[0:MI0]), (R_O, b_in[MO0:GM0 + D]), (R_NORM, norm_w),
                             (R_MNORM, mnorm_w), (R_CONVB, conv_b)):
                rows = src.shape[0] // P
                sp.dma_start(param_rows[row:row + rows, :], src.rearrange("(r n) -> r n", n=P)).then_inc(params_in, 16)
            sp.dma_start(param_rows[R_CONVW:R_CONVW + 32, :],
                         conv_w.rearrange("j (r n) -> (j r) n", n=P)).then_inc(params_in, 16)
            sp.dma_start(gate_bias[0:8, :], b_in[MI0:MF0].rearrange("(h a) -> h a", a=1)).then_inc(params_in, 16)
            sp.dma_start(gate_bias[32:40, :], b_in[MF0:MO0].rearrange("(h a) -> h a", a=1)).then_inc(params_in, 16)
            sp.dma_start(sink_tab[:, :], sinks.partition_broadcast(P)).then_inc(params_in, 16)
            for i in range(4):
                sp.dma_start(xs[:, 2 * i:2 * i + 2, :], x_rows[:, 2 * i:2 * i + 2, :]).then_inc(x_in[i], 16)

            sp.wait_ge(gate_slot_clear, 1)
            sp.dma_start(w_raw[:, 0, :, 0:8], w_cols[:, :, MI0:MF0]).then_inc(w_in_sem[0], 16)
            sp.dma_start(w_raw[:, 0, :, 32:40], w_cols[:, :, MF0:MO0]).then_inc(w_in_sem[0], 16)

            def weights(t0, tiles):
                cols = [c if isinstance(c, int) else sp.snap(c) for _, _, c in tiles]
                need = [n if isinstance(n, int) else sp.snap(n) for n in (t0 + j - 1 for j, _, _ in tiles)]
                for (j, src, _), c, n in zip(tiles, cols, need):
                    until(sp, w_split, n)
                    sp.sem_inc(sp_passed, 1)
                    s = slot(S2 + j)
                    sp.dma_start(w_raw[:, s], src[:, :, ds(c, P)]).then_inc(w_in_sem[s], 16)

            for t, c in ((1, K0), (2, K0 + P), (3, V0), (4, V0 + P)):
                until(sp, w_split, t - 1)
                sp.dma_start(w_raw[:, slot(t)], w_cols[:, :, c:c + P]).then_inc(w_in_sem[slot(t)], 16)

            looped(sp, KV, lambda g: weights(S2 + 4 * g, [
                (0, w_cols, Q0 + 2 * P * g), (1, w_cols, Q0 + P + 2 * P * g),
                (2, w_cols, Z0 + 2 * P * g), (3, w_cols, Z0 + P + 2 * P * g)]))

            def branch_a_step(i):
                weights(S3 + 2 * i, [(0, w_cols, GA0 + P * i), (1, wba_cols, P * i)])

            looped(sp, KT, branch_a_step)

            looped(sp, PAIRS, lambda p: weights(S4 + 10 * p, [
                (0, w_cols, MQ0 + P * p), (1, w_cols, MK0 + P * p),
                (2, w_cols, MV0 + 2 * P * p), (3, w_cols, MV0 + P + 2 * P * p),
                (4, w_cols, MO0 + 2 * P * p), (5, w_cols, MO0 + P + 2 * P * p),
                (6, w_cols, MZ0 + 2 * P * p), (7, w_cols, MZ0 + P + 2 * P * p),
                (8, w_cols, GM0 + 2 * P * p), (9, w_cols, GM0 + P + 2 * P * p)]))

            def branch_m_step(i):
                weights(S5 + 2 * i, [(0, wbm_cols, 2 * P * i), (1, wbm_cols, P + 2 * P * i)])
                if not later(i):
                    sp.wait_ge(u_split, KT + 1)
                    sp.wait_ge(branch_a_out, 16 * KT)
                    sp.dma_start(merged[:], scr_a.rearrange("k p n -> p k n")).then_inc(merged_in, 16)
                rows = [2 * i + j if isinstance(i, int) else sp.snap(2 * i + j) for j in range(2)]
                used = [2 * i + j - 1 if isinstance(i, int) else sp.snap(2 * i + j - 1) for j in range(2)]
                for j in range(2):
                    if later(i):
                        sp.wait_ge(merged_ready, used[j])
                    else:
                        sp.wait_ge(gm_out[j], 16 * PAIRS)
                    sp.dma_start(th_gm[:, j, :], scr_g[ds(rows[j], 1)].rearrange("a p n -> p (a n)")).then_inc(th_in[j], 16)

            looped(sp, KT // 2, branch_m_step)
            for k in range(KT):
                t = S6 + k
                until(sp, w_split, t - 1)
                sp.dma_start(w_raw[:, slot(t)].rearrange("p k n -> p (k n)"),
                             w_out[k * P:(k + 1) * P, :]).then_inc(w_in_sem[slot(t)], 16)

            sp.wait_ge(w_split, S6 + KT)
            sp.dma_start(fnw, fnorm_w.partition_broadcast(P)).then_inc(fn_in, 16)

            sp.wait_ge(merged_ready, KT)
            for j in range(2):
                sp.dma_start(x_tile[:, j, :], x_rows[:, j, :]).then_inc(x_again[j], 16)

            def out_step(i):
                last = isinstance(i, int) and i == NB // 2 - 1
                value = lambda v: v if isinstance(v, int) else sp.snap(v)
                done = [value(2 * i + j + 1) for j in range(2)]
                rows = [value(2 * i + j) for j in range(2)]
                ahead = [value(2 * i + j + 2) for j in range(2)]
                if not last:
                    for j in range(2):
                        sp.wait_ge(res_ready, done[j])
                        sp.dma_start(x_tile[:, j, :], x_rows[:, ds(ahead[j], 1), :].rearrange("p a n -> p (a n)"))\
                            .then_inc(x_again[j], 16)
                for j in range(2):
                    sp.wait_ge(y_ready, done[j])
                    sp.dma_start(out_rows[:, ds(rows[j], 1), :].rearrange("p a n -> p (a n)"), ev[j][:])\
                        .then_inc(y_out[j], 16)

            out_step(0)
            with sp.Fori(1, NB // 2 - 1) as i:
                out_step(i)
            out_step(NB // 2 - 1)

            for s in range(2):
                sp.wait_ge(gm_out[s], 16 * PAIRS)
                sp.wait_ge(y_out[s], 16 * NB // 2)
            sp.wait_ge(branch_a_out, 16 * KT)

        @block.gpsimd
        def _(pool):
            raw0 = w_raw[:, 0]
            nc.gpsimd.memset(raw0, 0.0).then_inc(gate_slot_clear, 1)

            def triangle(dst, inside, outside, base, free_step, chan):
                nc.gpsimd.memset(dst, inside)
                pool.drain()
                nc.gpsimd.affine_select(out=dst, in_=dst, compare_op=ALU.is_ge, fill=outside, base=base,
                                        pattern=[[free_step, P]], channel_multiplier=chan)

            nc.gpsimd.memset(ident[:], 0.0)
            nc.gpsimd.memset(zero_col[:], 0.0)
            nc.gpsimd.memset(neg_col[:], NEG)
            pool.drain()
            nc.gpsimd.affine_select(out=ident[:], in_=ident[:], compare_op=ALU.not_equal, fill=1.0, base=0,
                                    pattern=[[-1, P]], channel_multiplier=1)
            triangle(from_prev[:], 1.0, 0.0, -1, 1, -1)
            triangle(cur_T[:], 1.0, 0.0, 0, 1, -1)
            triangle(prev_T[:], 1.0, 0.0, -1, -1, 1)
            triangle(causal[:], 0.0, NEG, 0, 1, -1)
            nc.gpsimd.tensor_copy(ident_b[:], ident[:])
            nc.gpsimd.memset(ones_r[:].bitcast(F32), 1.0)
            nc.gpsimd.memset(ones8, 1.0)
            nc.gpsimd.memset(head_col[:], 0.0)
            nc.gpsimd.memset(parity_sel, 0.0)
            nc.gpsimd.memset(pair_mask[:], 1.0)
            pool.drain()
            for first in (0, 32):
                nc.gpsimd.affine_select(out=head_col[:], in_=head_col[:], compare_op=ALU.not_equal, fill=1.0,
                                        base=-first, pattern=[[-1, MH]], channel_multiplier=1)
                pool.drain()
            for q in range(PAIRS):
                v = parity_sel.rearrange("h (r m) -> h r m", r=2)
                nc.gpsimd.affine_select(out=v, in_=v, compare_op=ALU.not_equal, fill=1.0, base=-2 * q,
                                        pattern=[[-1, 2], [0, MK]], channel_multiplier=1)
                pool.drain()
            nc.gpsimd.affine_select(out=pair_mask[:], in_=pair_mask[:], compare_op=ALU.is_ge, fill=0.0, base=0,
                                    pattern=[[-2, PAIRS], [0, NB]], channel_multiplier=1)
            pool.drain()
            nc.gpsimd.affine_select(out=pair_mask[:], in_=pair_mask[:], compare_op=ALU.is_ge, fill=0.0, base=1,
                                    pattern=[[2, PAIRS], [0, NB]], channel_multiplier=-1)
            pool.drain()
            nc.gpsimd.memset(sumsq[:], 0.0).then_inc(consts_made, 1)

            def split(src, hi, lo):
                nc.gpsimd.tensor_tensor(hi, src, zero_col[:].to_broadcast([P, D]), ALU.add)
                pool.drain()
                nc.gpsimd.tensor_tensor(lo, src, hi.bitcast(F32), ALU.subtract).then_inc(w_split, 1)

            def landed(t):
                return 16 * (t // 2 + 1) + (16 if slot(t) == 0 else 0)

            def flat(a):
                return a.rearrange("p k n -> p (k n)")

            def split_tiles(first, i, per):
                for j in range(per):
                    s, t = slot(first + j), first + per * i + j
                    pool.wait_ge(w_in_sem[s], landed(first + j) + 8 * per * i)
                    until(pool, tile_done, t - 1)
                    split(flat(w_raw[:, s]), flat(w_hi[s][:]), flat(w_lo[s][:]))

            for t in range(S1, S2):
                split_tiles(t, 0, 1)
            looped(pool, KV, lambda g: split_tiles(S2, g, 4))
            looped(pool, KT, lambda i: split_tiles(S3, i, 2))
            pool.wait_ge(tile_done, S4)
            nc.gpsimd.memset(raw_q[:, 0:3], 0.0)
            nc.gpsimd.memset(raw_k[:, 0:3], 0.0)
            for r in range(2):
                pool.drain()
                nc.gpsimd.memset(mq_pad[64 * (1 - r):64 * (1 - r) + 64, r, :], 0.0)
            pool.drain()
            nc.gpsimd.memset(v1[:, :, :, MV:MV + 1], 1.0).then_inc(m_clear, 1)
            looped(pool, PAIRS, lambda p: split_tiles(S4, p, 10))
            looped(pool, KT // 2, lambda i: split_tiles(S5, i, 2))
            for k in range(KT):
                t = S6 + k
                pool.wait_ge(w_in_sem[slot(t)], landed(t))
                if k == 0:
                    pool.wait_ge(u_split, 2 * KT)
                split(flat(w_raw[:, slot(t)]), wo_hi[:, k, :], wo_lo[:, k, :])

        @block.tensor
        def _(pe):
            def dense(t, s, lo, hi, rhs_hi=hT_hi, rhs_lo=hT_lo, gate=None):
                for m in range(lo, hi):
                    b, r = divmod(m, KT * TERMS)
                    k, term = divmod(r, TERMS)
                    if m == 0:
                        until(pe, w_split, t + 1)
                        until(pe, tile_out, t - 1)
                    if gate is not None and b == 0 and term == 0:
                        pe.wait_ge(gate, gate_from + k + 1)
                    w = (w_hi, w_hi, w_lo)[term][s]
                    r_ = (rhs_hi, rhs_lo, rhs_hi)[term]
                    mm = nc.tensor.matmul(ps[:, 2 * s + b, :], w[:, k, :], r_[:, k, b * BANK:(b + 1) * BANK],
                                          start=(r == 0), stop=(r == KT * TERMS - 1))
                if hi == MMS:
                    mm.then_inc(tile_done, 1)

            gate_from = 0

            pe.wait_ge(consts_made, 1)
            pe.wait_ge(params_in, 16 * 9)
            nc.tensor.transpose(ps[:, X[3], 0:ROWS], param_rows[0:ROWS, :], ident[0:ROWS, 0:ROWS]).then_inc(params_T, 1)
            for half in range(2):
                for k in range(KT):
                    if k == 0:
                        pe.wait_ge(x_norm, half + 1)
                    if half == 0 and k == X[3]:
                        pe.wait_ge(params_ready, 1)
                    if half == 1:
                        pe.wait_ge(hT_lo_ready, k + 1)
                    for j in range(4):
                        t = 4 * half + j
                        mm = nc.tensor.transpose(ps[:, k, j * P:(j + 1) * P], xs[:, t, k * P:(k + 1) * P], ident[:])
                    mm.then_inc(x_turned, 1)

            pe.wait_ge(hT_lo_ready, 2 * KT)
            for t in range(S1, S2):
                dense(t, slot(t), 0, MMS)
                if t == 2:
                    pe.wait_ge(g_exp, 1)
                    for c in range(NB):
                        mm = nc.tensor.transpose(ps[:, X[c // 4], (c % 4) * P:(c % 4 + 1) * P],
                                                 g_t4[:, c * P:(c + 1) * P], ident[:])
                    nc.tensor.matmul(ps[:, X[2], 0:PAIRS * NB], parity_sel,
                                     decay_rows[:].rearrange("h a b -> h (a b)"), start=True, stop=True)\
                        .then_inc(g_turned, 1)
            pe.wait_ge(g_ready, 1)
            pe.wait_ge(tile_out, S2 - 1)
            for n, (buf, t) in enumerate(((ev[1], 3), (ev[0], 4))):
                until(pe, tile_out, t + 1)
                for c in range(NB):
                    mm = nc.tensor.transpose(ps[:, X[2 * n + c // 4], (c % 4) * P:(c % 4 + 1) * P],
                                             buf[:, c * P:(c + 1) * P], ident[:])
                mm.then_inc(v_turned, 1)

            pe.wait_ge(v_ready, 2)

            def scores(n):
                for b, at in ((0, n), (1, n - 1)):
                    if at < 0:
                        continue
                    for j in range(2):
                        mm = nc.tensor.matmul(ps[:, X[b], 2 * j * P:2 * (j + 1) * P], q_T[:, j, n * P:(n + 1) * P],
                                              k_pad[:, :, at * P:(at + 1) * P], start=True, stop=True)
                return mm

            def attention_step(g):
                t0 = S2 + 4 * g
                dense(t0, 1, 0, MMS)
                dense(t0 + 1, 0, 0, MMS)
                slots = 2 * (NB + 1)
                done = [0]

                def z_tiles(k):
                    hi = 2 * MMS * (k + 1) // slots
                    lo = done[0]
                    for j in range(2):
                        a, b = max(lo, j * MMS), min(hi, (j + 1) * MMS)
                        if a < b:
                            dense(t0 + 2 + j, 1 - j, a - j * MMS, b - j * MMS)
                    done[0] = hi

                for n in range(NB + 1):
                    if n < NB:
                        if n == 0:
                            pe.wait_ge(kv_head_ready, g + 1)
                            pe.wait_ge(tile_out, t0 + 2)
                        else:
                            pe.wait_ge(cur_copied, NB * g + n)
                            pe.wait_ge(max_ready, NB * g + n)
                        scores(n).then_inc(scores_done, 1)
                    z_tiles(2 * n)
                    if n >= 1:
                        pe.wait_ge(probs_ready, NB * g + n)
                        for h in range(GR):
                            mm = nc.tensor.transpose(ps[:, X[2], h * P:(h + 1) * P], probs[(n - 1) % 2][:, h, :], ident[:])
                        mm.then_inc(probs_turned, 1)
                    z_tiles(2 * n + 1)
                    if n >= 1:
                        m = n - 1
                        pe.wait_ge(pT_ready, NB * g + n)
                        if m >= 1:
                            pe.wait_ge(attn_ready, NB * g + m)
                        for r in range(2):
                            o = ps[64 * r:64 * r + 64, X[3], 0:2 * P]
                            mm = nc.tensor.matmul(o, v_head[:, m, :], pT_cur[:, r:GR:2, :], start=True, stop=(m == 0))
                            if m:
                                mm = nc.tensor.matmul(o, v_head[:, m - 1, :], pT_prev[:, r:GR:2, :], start=False, stop=True)
                        mm.then_inc(pv_done, 1)

            looped(pe, KV, attention_step)

            def branch_a_step(i):
                dense(S3 + 2 * i, 1, 0, MMS)
                dense(S3 + 1 + 2 * i, 0, 0, MMS, u_hi, u_lo, gate=u_split)

            looped(pe, KT, branch_a_step)

            def mlstm_step(p):
                t0 = S4 + 10 * p
                for j in range(4):
                    dense(t0 + j, slot(S4 + j), 0, MMS)
                done = [0]

                def more(hi):
                    lo = done[0]
                    for j in range(6):
                        a, b = max(lo, j * MMS), min(hi, (j + 1) * MMS)
                        if a < b:
                            dense(t0 + 4 + j, slot(S4 + j), a - j * MMS, b - j * MMS)
                    done[0] = hi

                def turn_v(j):
                    pe.wait_ge(tile_out, t0 + 3 + j)
                    for c in range(NB):
                        mm = nc.tensor.transpose(ps[:, X[2 * j + c // 4], (c % 4) * P:(c % 4 + 1) * P],
                                                 ev[j][:, c * P:(c + 1) * P], ident[:])
                    mm.then_inc(m_v_turned, 1)

                if later(p):
                    pe.wait_ge(u_ready, KV + p)
                turn_v(0)
                more(12)
                turn_v(1)
                more(24)
                pe.wait_ge(m_qk, 2 * (p + 1))
                pe.wait_ge(m_tabs, p + 1)
                pe.wait_ge(m_v_ready, 2 * (p + 1))
                each = (5 * MMS - 24) // (2 * NB)
                for c in range(NB):
                    tok = slice(c * P, (c + 1) * P)
                    if c:
                        pe.wait_ge(m_inter, 7 * p + c - 1) if c > 1 else None
                        pe.wait_ge(m_decay, 8 * p + c)
                        pe.wait_ge(m_state, 8 * p + c)
                    nc.tensor.matmul(ps[:, X[0], 0:2 * P], ones_r[:], c_heads[:, :, tok], start=True, stop=False)
                    nc.tensor.matmul(ps[:, X[0], 0:2 * P], ident_b[:],
                                     causal[:].unsqueeze(1).to_broadcast([P, 2, P]), start=False, stop=True)
                    nc.tensor.matmul(ps[:, X[1], 0:2 * P], mk_T[:, tok], mq_pad[:, :, tok], start=True, stop=True)
                    mm = nc.tensor.transpose(ps[:, X[1], 2 * P:3 * P], mk_T[:, tok], ident[:])
                    if c:
                        for j in range(2):
                            mm = nc.tensor.matmul(ps[:, X[3], j * (MV + 1):(j + 1) * (MV + 1)], mq_pad[:, j, tok],
                                                  state[:], start=True, stop=True)
                    mm.then_inc(m_scores, 1)
                    more(24 + each * (2 * c + 1))
                    pe.wait_ge(m_sT, 8 * p + c + 1)
                    for j in range(2):
                        mm = nc.tensor.matmul(ps[:, X[2], j * (MV + 1):(j + 1) * (MV + 1)], s_T[:, j, :], v1[:, c, j, :],
                                              start=True, stop=True)
                    if c < NB - 1:
                        for j in range(2):
                            mm = nc.tensor.matmul(ps[64 * j:64 * j + 64, X[2], 2 * (MV + 1):3 * (MV + 1)], k_w[:, j, :],
                                                  v1[:, c, j, :], start=True, stop=True)
                    mm.then_inc(m_prod, 1)
                    more(24 + each * (2 * c + 2))
                more(6 * MMS)
                pe.wait_ge(m_h, p + 1)
                for j in range(2):
                    for c in range(NB):
                        mm = nc.tensor.transpose(ps[:, X[2 * j + c // 4], (c % 4) * P:(c % 4 + 1) * P],
                                                 h_tok[:, c, j, 0:MV], ident[:])
                mm.then_inc(m_h_turned, 1)

            looped(pe, PAIRS, mlstm_step)

            gate_from = KT

            def branch_m_step(i):
                dense(S5 + 2 * i, 1, 0, MMS, gate=u_split)
                dense(S5 + 1 + 2 * i, 0, 0, MMS)

            looped(pe, KT // 2, branch_m_step)

            pe.wait_ge(w_split, S6 + KT)

            def out_step(i):
                for j in range(2):
                    s = slot(S6 + j)
                    pe.wait_ge(mt_ready, 2 * i + j + 1)
                    pe.wait_ge(tile_out, S6 - 1 + 2 * i + j)
                    for b in range(2):
                        for k in range(KT):
                            for term in range(TERMS):
                                lhs = (mt_hi, mt_lo, mt_hi)[term][j]
                                rhs = (wo_hi, wo_hi, wo_lo)[term]
                                mm = nc.tensor.matmul(ps[:, 2 * s + b, :], lhs[:, k, :],
                                                      rhs[:, k, b * BANK:(b + 1) * BANK],
                                                      start=(k == 0 and term == 0), stop=(k == KT - 1 and term == TERMS - 1))
                    mm.then_inc(tile_done, 1)

            looped(pe, NB // 2, out_step)

        @block.scalar
        def _(act):
            A = nc.scalar.activation

            act.wait_ge(params_T, 1)
            A(par[:], ps[:, X[3], 0:ROWS], ACT.Copy)
            A(par_half[:], ps[:, X[3], 0:ROWS], ACT.Copy, scale=0.5).then_inc(params_ready, 1)
            for half in range(2):
                for j in range(4):
                    t = 4 * half + j
                    if j % 2 == 0:
                        act.wait_ge(x_in[t // 2], 16)
                    act.drain()
                    ins = A(ev[0][:], xs[:, t, :], ACT.Square, accum_out=sumsq[:, t:t + 1])
                ins.then_inc(x_sumsq, 1)
                act.wait_ge(x_var, half + 1)
                A(rstd[:, 4 * half:4 * half + 4], rstd[:, 4 * half:4 * half + 4], ACT.Sqrt).then_inc(x_root, 1)
            for half in range(2):
                for k in range(KT):
                    act.wait_ge(x_turned, KT * half + k + 1)
                    A(hT_hi[:, k, half * BANK:(half + 1) * BANK], ps[:, k, :], ACT.Copy,
                      scale=par[:, R_NORM + k:R_NORM + k + 1]).then_inc(hT_hi_ready, 1)

            act.wait_ge(tile_done, 1)
            A(g_i[0:8, :], dense_ps(0)[0:8, :], ACT.Identity, bias=gate_bias[0:8, :])
            A(g_f[0:8, :], dense_ps(0)[32:40, :], ACT.Identity, bias=gate_bias[32:40, :]).then_inc(tile_out, 1)
            act.drain()
            A(g_t1[0:8, :], g_f[0:8, :], ACT.Abs)
            act.drain()
            A(g_t1[0:8, :], g_t1[0:8, :], ACT.Exp, scale=-1.0)
            act.drain()
            A(g_t1[0:8, :], g_t1[0:8, :], ACT.Ln, bias=1.0).then_inc(g_log, 1)
            for t in (1, 2):
                act.wait_ge(tile_done, t + 1)
                for half in range(2):
                    g = 2 * (t - 1) + half
                    for r in range(2):
                        ins = A(k_dup[64 * r:64 * r + 64, g, :], dense_ps(t)[64 * half:64 * half + 64, :], ACT.Identity,
                                bias=par[64 * half:64 * half + 64, R_K + t - 1:R_K + t])
                ins.then_inc(tile_out, 1)
                if t == 1:
                    act.wait_ge(g_rows, 1)
                    A(g_t4[32:40, :], g_f[0:8, :], ACT.Exp)
                    A(g_t4[64:72, :], g_t2[0:8, :], ACT.Exp)
                    A(g_t4[96:104, :], g_t3[0:8, :], ACT.Exp, scale=-1.0)
                    A(decay[:], g_f[0:8, :].rearrange("h (c n) -> h c n", n=P)[:, :, P - 1], ACT.Exp)
                    act.drain()
                    for q in range(PAIRS):
                        ins = A(decay_rows[:, q, :], decay[:], ACT.Copy, scale=pair_mask[:, q, 0:1])
                    ins.then_inc(g_exp, 1)
            act.wait_ge(g_turned, 1)
            for b in range(2):
                A(gate_T[:, 4 * b:4 * b + 4, :].rearrange("p c n -> p (c n)"), ps[:, X[b], :], ACT.Copy)
            A(decay_tab[:].rearrange("p a b -> p (a b)"), ps[:, X[2], 0:PAIRS * NB], ACT.Copy).then_inc(g_ready, 1)
            for t in (3, 4):
                act.wait_ge(tile_done, t + 1)
                A(ev[t % 2][:], dense_ps(t), ACT.Identity, bias=par[:, R_V + t - 3:R_V + t - 2]).then_inc(tile_out, 1)

            def attention_step(g):
                t0 = S2 + 4 * g
                for j in range(2):
                    act.wait_ge(tile_done, t0 + 1 + j)
                    A(q_T[:, j, :], dense_ps(S2 + j), ACT.Identity, bias=par[:, ds(R_Q + j + 2 * g, 1)]).then_inc(tile_out, 1)

                def z_tile(j):
                    act.wait_ge(tile_done, t0 + 3 + j)
                    if later(g):
                        act.wait_ge(u_ready, g)
                    else:
                        act.wait_ge(v_turned, 2)
                    A(silu_z[:, j, :], dense_ps(S2 + j), ACT.Identity, bias=par[:, ds(R_Z + j + 2 * g, 1)]).then_inc(tile_out, 1)
                    act.drain()
                    A(ev[j][:], silu_z[:, j, :], ACT.Tanh, scale=0.5).then_inc(z_tanh, 1)

                for n in range(NB + 1):
                    if n < NB:
                        pr = probs[n % 2]
                        act.wait_ge(scores_done, NB * g + n + 1)
                        if n >= 2:
                            act.wait_ge(probs_turned, NB * g + n - 1)
                        A(pr[:].rearrange("p h n -> p (h n)"), ps[:, X[0], :], ACT.Copy).then_inc(cur_copied, 1)
                        act.wait_ge(max_ready, NB * g + n + 1)
                        for h in range(GR):
                            A(pr[:, h, :], pr[:, h, :], ACT.Exp, scale=HD ** -0.5, bias=neg_max[:, h:h + 1],
                              accum_out=row_sum[:, h:h + 1])
                        A(sink_exp[:], sink_in[:], ACT.Exp).then_inc(exp_ready, 1)
                    if n >= 1:
                        m = n - 1
                        act.wait_ge(pv_done, NB * g + n)
                        if m == 0 and later(g):
                            act.wait_ge(u_ready, g)
                        A(attn_T[:, :, m * P:(m + 1) * P], ps[:, X[3], 0:2 * P].rearrange("p (j n) -> p j n", j=2),
                          ACT.Copy).then_inc(attn_ready, 1)
                    if n == 5:
                        z_tile(0)
                z_tile(1)

            looped(act, KV, attention_step)

            act.wait_ge(u_ready, KV)
            act.wait_ge(pv_done, KV * NB)
            for k in range(KT):
                A(u_hi[:, k, :], U[:, k, :], ACT.Copy).then_inc(u_hi_ready, 1)

            def branch_a_step(i):
                t0 = S3 + 2 * i
                act.wait_ge(tile_done, t0 + 1)
                until(act, branch_a, i)
                A(ev[0][:], dense_ps(S3), ACT.Tanh, scale=0.5, bias=par_half[:, ds(R_GA + i, 1)]).then_inc(tile_out, 1)
                act.wait_ge(tile_done, t0 + 2)
                until(act, branch_a_out, 16 * i)
                A(ev[1][:], dense_ps(S3 + 1), ACT.Copy).then_inc(tile_out, 1)
                act.wait_ge(branch_a, i + 1)
                act.dma_start(scr_a[ds(i, 1)].rearrange("a p n -> p (a n)"), ev[1][:]).then_inc(branch_a_out, 16)

            looped(act, KT, branch_a_step)

            def mlstm_step(p):
                t0 = S4 + 10 * p
                for j, (raw, row) in enumerate(((raw_q, R_MQ), (raw_k, R_MK))):
                    act.wait_ge(tile_done, t0 + 1 + j)
                    if j == 0:
                        act.wait_ge(m_clear, 1)
                    A(raw[:, 3:], dense_ps(S4 + j), ACT.Identity, bias=par[:, ds(row + p, 1)]).then_inc(tile_out, 1)
                act.wait_ge(m_conv, 2 * p + 1)
                if later(p):
                    act.wait_ge(mz_used, 2 * p)
                A(tanh_buf[:], z_buf[:], ACT.Tanh, scale=0.5).then_inc(m_tanh, 1)

                def v_tile(j):
                    act.wait_ge(tile_done, t0 + 3 + j)
                    if not later(p):
                        act.wait_ge(branch_a_out, 16 * KT)
                    else:
                        act.wait_ge(gm_out[j], 16 * p)
                    A(ev[j][:], dense_ps(S4 + j), ACT.Identity, bias=par[:, ds(R_MV + j + 2 * p, 1)]).then_inc(tile_out, 1)

                v_tile(0)
                act.wait_ge(m_conv, 2 * p + 2)
                act.wait_ge(m_qk, 2 * p + 1)
                A(tanh_buf[:], mk_T[:], ACT.Tanh, scale=0.5).then_inc(m_tanh, 1)
                v_tile(1)

                def o_tile(j):
                    act.wait_ge(tile_done, t0 + 5 + j)
                    if later(p):
                        act.wait_ge(u_ready, KV + p)
                    A(gates[:, j, :], dense_ps(S4 + j), ACT.Tanh, scale=0.5,
                      bias=par_half[:, ds(R_O + j + 2 * p, 1)]).then_inc(tile_out, 1)

                def z_tile(j):
                    act.wait_ge(tile_done, t0 + 7 + j)
                    if j == 0:
                        act.wait_ge(m_qk, 2 * p + 2)
                    else:
                        act.wait_ge(mz_used, 2 * p + 1)
                    A(z_buf[:], dense_ps(S4 + j), ACT.Identity, bias=par[:, ds(R_MZ + j + 2 * p, 1)]).then_inc(tile_out, 1)
                    act.drain()
                    A(tanh_buf[:], z_buf[:], ACT.Tanh, scale=0.5).then_inc(mz_tanh, 1)

                def gm_tile(j):
                    act.wait_ge(tile_done, t0 + 9 + j)
                    act.wait_ge(m_v_turned, 2 * p + 1 + j)
                    A(ev[j][:], dense_ps(S4 + j), ACT.Tanh, scale=0.5,
                      bias=par_half[:, ds(R_GM + j + 2 * p, 1)]).then_inc(tile_out, 1)
                    act.drain()
                    act.dma_start(scr_g[ds(2 * p + j, 1)].rearrange("a p n -> p (a n)"), ev[j][:]).then_inc(gm_out[j], 16)

                def sum_squares(c):
                    act.drain()
                    act.wait_ge(m_den, 8 * p + c + 1)
                    for j in range(2):
                        if j:
                            act.drain()
                        ins = A(junk[:], h_tok[:, c, j, 0:MV], ACT.Square, scale=den_inv[:, c, j:j + 1],
                                accum_out=sumsq[:, 2 * c + j:2 * c + j + 1])
                    return ins

                for c in range(NB):
                    act.wait_ge(m_scores, 8 * p + c + 1)
                    if c >= 1:
                        act.wait_ge(m_sT, 8 * p + c)
                    for j in range(2):
                        ins = A(dmat[:, j, :], ps[:, X[0], j * P:(j + 1) * P], ACT.Exp, bias=tok_gate[:, c, 0, j:j + 1])
                    ins.then_inc(m_decay, 1)
                    if c:
                        act.wait_ge(m_state, 8 * p + c)
                        for j in range(2):
                            ins = A(inter[:, j, :], ps[:, X[3], j * (MV + 1):(j + 1) * (MV + 1)], ACT.Copy,
                                    scale=tok_gate[:, c, 1, j:j + 1])
                        ins.then_inc(m_inter, 1)
                        sum_squares(c - 1)
                    if c == 1:
                        o_tile(0)
                    if c == 3:
                        o_tile(1)
                    if c == 5:
                        z_tile(0)
                    if c == 7:
                        z_tile(1)
                gm_tile(0)
                sum_squares(NB - 1).then_inc(m_sumsq, 1)
                act.wait_ge(m_var, p + 1)
                A(rstd[:], rstd[:], ACT.Sqrt).then_inc(m_root, 1)
                gm_tile(1)

            looped(act, PAIRS, mlstm_step)

            act.wait_ge(tile_done, S5)
            for k in range(KT):
                act.wait_ge(u_ready, KV + (k // 2) + 1)
                A(hT_hi[:, k, :], U[:, k, :], ACT.Copy).then_inc(u_hi_ready, 1)

            def branch_m_step(i):
                for j in range(2):
                    act.wait_ge(tile_done, S5 + 1 + j + 2 * i)
                    if not later(i):
                        act.wait_ge(gm_out[j], 16 * PAIRS)
                    else:
                        act.wait_ge(merged_ready, 2 * i + j - 1)
                    A(ev[j][:], dense_ps(S5 + j), ACT.Copy).then_inc(tile_out, 1)

            looped(act, KT // 2, branch_m_step)

            act.wait_ge(merged_ready, KT)
            act.wait_ge(tile_done, S6)

            def token_tile(n, j):
                A(mt_hi[j], merged[:, :, ds(P * n, P)], ACT.Copy).then_inc(mt_hi_ready, 1)

            token_tile(0, 0)
            token_tile(1, 1)
            act.wait_ge(fn_in, 16)

            def out_step(i):
                for j in range(2):
                    act.wait_ge(tile_done, S6 + 1 + 2 * i + j)
                    if later(i):
                        act.wait_ge(y_out[j], 16 * i)
                    A(ev[j][:], dense_ps(S6 + j), ACT.Copy, scale=0.5).then_inc(tile_out, 1)
                    if not (isinstance(i, int) and i == NB // 2 - 1):
                        token_tile(2 * (i + 1) + j, j)
                    act.wait_ge(res_ready, 2 * i + j + 1)
                    A(squares, ev[j][:], ACT.Square, accum_out=sumsq[:, j:j + 1]).then_inc(res_sumsq, 1)
                    act.wait_ge(res_var, 2 * i + j + 1)
                    A(rstd[:, j:j + 1], rstd[:, j:j + 1], ACT.Sqrt).then_inc(res_root, 1)

            out_step(0)
            with act.Fori(1, NB // 2 - 1) as i:
                out_step(i)
            out_step(NB // 2 - 1)

        @block.vector
        def _(dve):
            V = nc.vector

            for half in range(2):
                cols = rstd[:, 4 * half:4 * half + 4]
                dve.wait_ge(x_sumsq, half + 1)
                V.tensor_scalar(cols, sumsq[:, 4 * half:4 * half + 4], 1.0 / D, EPS, ALU.mult, ALU.add).then_inc(x_var, 1)
                dve.wait_ge(x_root, half + 1)
                V.reciprocal(cols, cols)
                dve.drain()
                for j in range(4):
                    t = 4 * half + j
                    ins = V.tensor_scalar(xs[:, t, :], xs[:, t, :], rstd[:, t:t + 1], None, ALU.mult)
                ins.then_inc(x_norm, 1)
            for half in range(2):
                for k in range(KT):
                    part = slice(half * BANK, (half + 1) * BANK)
                    dve.wait_ge(hT_hi_ready, KT * half + k + 1)
                    V.scalar_tensor_tensor(hT_lo[:, k, part], ps[:, k, :], par[:, R_NORM + k:R_NORM + k + 1],
                                           hT_hi[:, k, part].bitcast(F32), ALU.mult, ALU.subtract).then_inc(hT_lo_ready, 1)

            i_, f_ = g_i[0:8, :], g_f[0:8, :]
            chunks = lambda a: a.rearrange("h (c n) -> h c n", n=P)
            logf, m_, b_ = g_t2[0:8, :], g_t3[0:8, :], g_t5[0:8, :]
            dve.wait_ge(g_log, 1)
            V.tensor_scalar(logf, f_, 0.0, None, ALU.min)
            V.memset(g_t4[:], 0.0)
            V.memset(c_split[:], 0.0)
            V.memset(m_before[:], NEG)
            dve.drain()
            V.tensor_tensor(logf, logf, g_t1[0:8, :], ALU.subtract)
            dve.drain()
            V.tensor_tensor_scan(m_, logf, i_, NEG, ALU.add, ALU.max)
            for c in range(NB):
                V.tensor_tensor_scan(b_[:, c * P:(c + 1) * P], ones8, logf[:, c * P:(c + 1) * P], 0.0, ALU.mult, ALU.add)
            dve.drain()
            V.tensor_tensor(g_t4[0:8, :], i_, b_, ALU.subtract)
            V.tensor_tensor(b_, b_, m_, ALU.subtract)
            V.tensor_copy(m_before[:, 1:NB], chunks(m_)[:, 0:NB - 1, P - 1])
            dve.drain()
            V.tensor_tensor(chunks(f_), chunks(b_), m_before[:].unsqueeze(2).to_broadcast([MH, NB, P]), ALU.add)
            V.tensor_tensor(chunks(logf), chunks(g_t4[0:8, :]),
                            chunks(b_)[:, :, P - 1:P].to_broadcast([MH, NB, P]), ALU.add).then_inc(g_rows, 1)
            V.tensor_copy(c_hi[0:8, :], b_)
            dve.drain()
            V.tensor_tensor(c_split[32:40, :], b_, c_hi[0:8, :].bitcast(F32), ALU.subtract)
            V.tensor_copy(c_split[0:8, :], c_hi[0:8, :].bitcast(F32))
            for n in range(2):
                dve.wait_ge(v_turned, n + 1)
                for b in range(2):
                    ins = V.tensor_copy(v_tok[:, 4 * b:4 * b + 4, n * P:(n + 1) * P],
                                        ps[:, X[2 * n + b], :].rearrange("p (c n) -> p c n", n=P))
                ins.then_inc(v_ready, 1)

            def attention_step(g):
                dve.drain()
                until(dve, pv_done, NB * g)
                for r in range(2):
                    V.tensor_copy(k_pad[64 * r:64 * r + 64, r, :],
                                  k_dup[64 * r:64 * r + 64, ds(g, 1), :].rearrange("p a n -> p (a n)"))
                V.tensor_copy(v_head[:], v_tok[:, :, ds(HD * g, HD)]).then_inc(kv_head_ready, 1)

                def combine(n):
                    pr = probs[n % 2]
                    dve.wait_ge(cur_copied, NB * g + n + 1)
                    dve.sem_inc(passed, 1)
                    if n:
                        V.copy_predicated(pr[:], from_prev[:].unsqueeze(1).to_broadcast([P, GR, P]),
                                          ps[:, X[1], :].rearrange("p (h n) -> p h n", n=P))
                    else:
                        V.copy_predicated(pr[:], from_prev[:].unsqueeze(1).to_broadcast([P, GR, P]),
                                          neg_col[:].unsqueeze(1).to_broadcast([P, GR, P]))
                    dve.drain()
                    V.tensor_reduce(row_max[:], pr[:], AXX, ALU.max)
                    dve.drain()
                    sink = sink_tab[:, ds(GR * g, GR)]
                    V.scalar_tensor_tensor(row_max[:], row_max[:], HD ** -0.5, sink, ALU.mult, ALU.max)
                    dve.drain()
                    V.tensor_tensor(sink_in[:], sink, row_max[:], ALU.subtract)
                    V.tensor_scalar(neg_max[:], row_max[:], -1.0, None, ALU.mult).then_inc(max_ready, 1)

                def normalise(n):
                    pr = probs[n % 2]
                    dve.wait_ge(exp_ready, NB * g + n + 1)
                    V.tensor_tensor(row_inv[:], row_sum[:], sink_exp[:], ALU.add)
                    dve.drain()
                    V.tensor_scalar(row_inv[:], row_inv[:], 2.0, None, ALU.mult)
                    dve.drain()
                    V.reciprocal(row_inv[:], row_inv[:])
                    dve.drain()
                    V.tensor_tensor(pr[:], pr[:], row_inv[:].unsqueeze(2).to_broadcast([P, GR, P]), ALU.mult)\
                        .then_inc(probs_ready, 1)

                def select(n):
                    dve.wait_ge(probs_turned, NB * g + n + 1)
                    if n:
                        dve.wait_ge(pv_done, NB * g + n)
                    src = ps[:, X[2], :].rearrange("p (h n) -> p h n", n=P)
                    ins = V.tensor_tensor(pT_cur[:], src, cur_T[:].unsqueeze(1).to_broadcast([P, GR, P]), ALU.mult)
                    if n:
                        ins = V.tensor_tensor(pT_prev[:], src, prev_T[:].unsqueeze(1).to_broadcast([P, GR, P]), ALU.mult)
                    ins.then_inc(pT_ready, 1)

                for n in range(NB + 1):
                    if n < NB:
                        combine(n)
                    if n >= 1:
                        select(n - 1)
                    if n < NB:
                        normalise(n)
                for j in range(2):
                    dve.wait_ge(z_tanh, 2 * g + j + 1)
                    V.scalar_tensor_tensor(silu_z[:, j, :], ev[j][:], 1.0, silu_z[:, j, :], ALU.add, ALU.mult)
                dve.drain()
                dve.wait_ge(attn_ready, NB * (g + 1))
                for j in range(2):
                    ins = V.tensor_tensor(U[:, ds(j + 2 * g, 1), :].rearrange("p a n -> p (a n)"), attn_T[:, j, :],
                                          silu_z[:, j, :], ALU.mult)
                ins.then_inc(u_ready, 1)

            for r in range(2):
                V.memset(k_pad[64 * (1 - r):64 * (1 - r) + 64, r, :], 0.0)
            looped(dve, KV, attention_step)

            dve.drain()
            for k in range(KT):
                dve.wait_ge(u_hi_ready, k + 1)
                V.tensor_tensor(u_lo[:, k, :], U[:, k, :], u_hi[:, k, :].bitcast(F32), ALU.subtract).then_inc(u_split, 1)

            def branch_a_step(i):
                dve.wait_ge(tile_out, S3 + 2 + 2 * i)
                V.scalar_tensor_tensor(ev[1][:], ev[0][:], 1.0, ev[1][:], ALU.add, ALU.mult).then_inc(branch_a, 1)

            looped(dve, KT, branch_a_step)

            def mlstm_step(p):
                t0 = S4 + 10 * p
                dve.drain()
                dve.wait_ge(tile_out, t0 + 1)
                gate_v = gate_T[:].rearrange("p c (q h) -> p c q h", h=32)
                V.tensor_copy(tok_gate[:], gate_v[:, :, :, ds(2 * p, 2)])
                V.tensor_copy(pair_decay[:], decay_tab[:, ds(p, 1), :].rearrange("p a c -> p (a c)"))
                V.tensor_copy(pair_norm[:], par[:, ds(R_MNORM + 2 * p, 2)])
                for j in range(2):
                    V.tensor_scalar(c_heads[:, j, :], c_split[:], head_col[:, ds(2 * p + j, 1)], None, ALU.mult)
                dve.drain()
                V.tensor_scalar(tok_gate[:, :, 1, :], tok_gate[:, :, 1, :], 0.5 * MK ** -0.5, None, ALU.mult)
                V.tensor_scalar(pair_norm[:], pair_norm[:], 0.25, None, ALU.mult).then_inc(m_tabs, 1)
                for j, (raw, dst) in enumerate(((raw_q, z_buf), (raw_k, mk_T))):
                    dve.wait_ge(tile_out, t0 + 1 + j)
                    tap = lambda n: par[:, ds(R_CONVW + 8 * n + 4 * j + p, 1)]
                    V.tensor_scalar(dst[:], raw[:, 3:T + 3], tap(3), par[:, ds(R_CONVB + 4 * j + p, 1)], ALU.mult, ALU.add)
                    for n in range(3):
                        dve.drain()
                        ins = V.scalar_tensor_tensor(dst[:], raw[:, n:T + n], tap(n), dst[:], ALU.mult, ALU.add)
                    ins.then_inc(m_conv, 1)
                    dve.wait_ge(m_tanh, 2 * p + j + 1)
                    if j == 0:
                        for r in range(2):
                            rows = slice(64 * r, 64 * r + 64)
                            ins = V.scalar_tensor_tensor(mq_pad[rows, r, :], tanh_buf[rows, :], 1.0, z_buf[rows, :],
                                                         ALU.add, ALU.mult)
                    else:
                        ins = V.scalar_tensor_tensor(mk_T[:], tanh_buf[:], 1.0, mk_T[:], ALU.add, ALU.mult)
                    ins.then_inc(m_qk, 1)
                for j in range(2):
                    dve.wait_ge(m_v_turned, 2 * p + j + 1)
                    if not later(p):
                        dve.wait_ge(m_clear, 1)
                    for b in range(2):
                        ins = V.tensor_copy(v1[:, 4 * b:4 * b + 4, j, 0:MV],
                                            ps[:, X[2 * j + b], :].rearrange("p (c n) -> p c n", n=P))
                    ins.then_inc(m_v_ready, 1)

                def z_part(j):
                    dve.wait_ge(mz_tanh, 2 * p + j + 1)
                    V.scalar_tensor_tensor(gates[:, j, :], gates[:, j, :], 1.0, z_buf[:], ALU.add, ALU.mult)
                    dve.drain()
                    V.scalar_tensor_tensor(gates[:, j, :], tanh_buf[:], 1.0, gates[:, j, :], ALU.add, ALU.mult)\
                        .then_inc(mz_used, 1)

                for c in range(NB):
                    dve.wait_ge(m_decay, 8 * p + c + 1)
                    for j in range(2):
                        V.scalar_tensor_tensor(s_T[:, j, :], ps[:, X[1], j * P:(j + 1) * P], 0.25 * MK ** -0.5,
                                               dmat[:, j, :], ALU.mult, ALU.mult)
                    for j in range(2):
                        ins = V.tensor_scalar(k_w[:, j, :], ps[:, X[1], 2 * P + MK * j:2 * P + MK * (j + 1)],
                                              tok_gate[:, c, 2, j:j + 1], 0.5, ALU.mult, ALU.mult)
                    ins.then_inc(m_sT, 1)
                    dve.wait_ge(m_prod, 8 * p + c + 1)
                    num = ps[:, X[2], 0:2 * (MV + 1)]
                    h_c = h_tok[:, c].rearrange("p j n -> p (j n)")
                    new = ps[:, X[2], 2 * (MV + 1):3 * (MV + 1)]
                    if c == 0:
                        V.tensor_copy(h_c, num)
                        V.tensor_copy(state[:], new).then_inc(m_state, 1)
                    else:
                        if c < NB - 1:
                            V.scalar_tensor_tensor(state[:], state[:], pair_decay[:, c:c + 1], new, ALU.mult, ALU.add)
                        dve.wait_ge(m_inter, 7 * p + c)
                        V.tensor_tensor(h_c, num, inter[:].rearrange("p j n -> p (j n)"), ALU.add).then_inc(m_state, 1)
                    dve.drain()
                    d = h_tok[:, c, :, MV]
                    V.scalar_tensor_tensor(den[:], d, -1.0, d, ALU.mult, ALU.max)
                    dve.drain()
                    V.tensor_tensor(den[:], den[:], tok_gate[:, c, 3, :], ALU.max)
                    dve.drain()
                    V.reciprocal(den_inv[:, c, :], den[:]).then_inc(m_den, 1)
                    if c == 6:
                        z_part(0)
                z_part(1)
                dve.wait_ge(m_sumsq, p + 1)
                V.tensor_scalar(rstd[:], sumsq[:], 1.0 / MV, EPS, ALU.mult, ALU.add).then_inc(m_var, 1)
                dve.wait_ge(m_root, p + 1)
                V.reciprocal(rstd[:], rstd[:])
                dve.drain()
                V.tensor_tensor(rstd[:], rstd[:], den_inv[:].rearrange("p c j -> p (c j)"), ALU.mult)
                dve.drain()
                hv = h_tok[:].rearrange("p c j n -> p (c j) n")[:, :, 0:MV]
                V.tensor_tensor(hv, hv, rstd[:].unsqueeze(2).to_broadcast([P, 2 * NB, MV]), ALU.mult).then_inc(m_h, 1)
                dve.wait_ge(m_h_turned, p + 1)
                for j in range(2):
                    for b in range(2):
                        part = slice(b * BANK, (b + 1) * BANK)
                        ins = V.scalar_tensor_tensor(U[:, ds(j + 2 * p, 1), part].rearrange("p a n -> p (a n)"),
                                                     ps[:, X[2 * j + b], :], pair_norm[:, j:j + 1], gates[:, j, part],
                                                     ALU.mult, ALU.mult)
                ins.then_inc(u_ready, 1)

            looped(dve, PAIRS, mlstm_step)

            dve.drain()
            for k in range(KT):
                dve.wait_ge(u_hi_ready, KT + k + 1)
                V.tensor_tensor(hT_lo[:, k, :], U[:, k, :], hT_hi[:, k, :].bitcast(F32), ALU.subtract).then_inc(u_split, 1)
            dve.wait_ge(merged_in, 16)

            def branch_m_step(i):
                for j in range(2):
                    dve.wait_ge(th_in[j], 16 * (i + 1))
                    dve.wait_ge(tile_out, S5 + 1 + 2 * i + j)
                    V.scalar_tensor_tensor(ev[j][:], th_gm[:, j, :], 1.0, ev[j][:], ALU.add, ALU.mult)
                    dve.drain()
                    row = merged[:, ds(2 * i + j, 1), :].rearrange("p a n -> p (a n)")
                    V.tensor_tensor(row, row, ev[j][:], ALU.add).then_inc(merged_ready, 1)

            looped(dve, KT // 2, branch_m_step)

            def token_tile(n, j):
                dve.wait_ge(mt_hi_ready, n + 1)
                V.tensor_tensor(mt_lo[j], merged[:, :, ds(P * n, P)], mt_hi[j].bitcast(F32), ALU.subtract).then_inc(mt_ready, 1)

            token_tile(0, 0)
            token_tile(1, 1)
            dve.wait_ge(fn_in, 16)

            def out_step(i):
                for j in range(2):
                    dve.wait_ge(x_again[j], 16 * (i + 1))
                    dve.wait_ge(tile_out, S6 + 1 + 2 * i + j)
                    V.tensor_tensor(ev[j][:], ev[j][:], x_tile[:, j, :], ALU.add).then_inc(res_ready, 1)
                    if not (isinstance(i, int) and i == NB // 2 - 1):
                        token_tile(2 * (i + 1) + j, j)
                    r = rstd[:, j:j + 1]
                    dve.wait_ge(res_sumsq, 2 * i + j + 1)
                    V.tensor_scalar(r, sumsq[:, j:j + 1], 1.0 / D, EPS, ALU.mult, ALU.add).then_inc(res_var, 1)
                    dve.wait_ge(res_root, 2 * i + j + 1)
                    V.reciprocal(r, r)
                    dve.drain()
                    V.scalar_tensor_tensor(ev[j][:], ev[j][:], r, fnw, ALU.mult, ALU.mult).then_inc(y_ready, 1)

            out_step(0)
            with dve.Fori(1, NB // 2 - 1) as i:
                out_step(i)
            out_step(NB // 2 - 1)


def kernel(x, norm_w, w_in, b_in, attn_sinks, conv_w, conv_b, mlstm_norm_w, w_branch_attn, w_branch_mlstm,
           w_out, final_norm_w):
    import numpy as np
    import concourse.bacc as bacc
    from concourse.bass_utils import run_bass_kernel_spmd

    ins = {"x": x[0], "norm_w": norm_w[0], "w_in": w_in[0], "b_in": b_in[0], "attn_sinks": attn_sinks[0],
           "conv_w": conv_w[0], "conv_b": conv_b[0], "mlstm_norm_w": mlstm_norm_w[0],
           "w_branch_attn": w_branch_attn[0], "w_branch_mlstm": w_branch_mlstm[0], "w_out": w_out[0],
           "final_norm_w": final_norm_w}
    nc = bacc.Bacc("TRN2", target_bir_lowering=False, num_devices=1)
    arrays, args = {}, []
    for name, a in ins.items():
        a = np.ascontiguousarray(a)
        arrays[f"in_{name}"] = a
        args.append(nc.dram_tensor(f"in_{name}", a.shape, mybir.dt.from_np(a.dtype), kind="ExternalInput").ap())
    args.append(nc.dram_tensor("out", (T, D), F32, kind="ExternalOutput").ap())
    build(nc, *args)
    r = run_bass_kernel_spmd(nc, [arrays], core_ids=[0])
    return r.results[0]["out"].reshape(1, T, D)
```

```python
import concourse.bass as bass
from concourse import mybir
from contextlib import ExitStack

F32 = mybir.dt.float32
F32R = mybir.dt.float32r
BF16 = mybir.dt.bfloat16
I8 = mybir.dt.int8
ALU = mybir.AluOpType
ACT = mybir.ActivationFunctionType
AXX = mybir.AxisListType.X
ds = bass.ds

P = 128
D = 1024
T = 1024
KT = D // P
NB = T // P
HEADS, KV, HD = 16, 4, 64
GR = HEADS // KV
MH, MK, MV = 8, 64, 128
PAIRS = MH // 2
EPS = 1e-6
NEG = -1e30
BANK = 512

Q0, K0, V0, Z0 = 0, 1024, 1280, 1536
MQ0, MK0, MV0, MI0, MF0, MO0, MZ0, GA0, GM0 = 2560, 3072, 3584, 4608, 4616, 4624, 5648, 6672, 7696
R_Q, R_K, R_V, R_Z, R_MQ, R_MK, R_MV, R_O, R_MZ, R_GA, R_GM = 0, 8, 10, 12, 20, 24, 28, 36, 44, 52, 60
R_NORM, R_MNORM, R_CONVW, R_CONVB, ROWS = 68, 76, 84, 116, 124

S1, S2, S3, S4, S5 = 0, 5, 29, 37, 77
S6 = 85
TERMS = 3
MMS = 2 * KT * TERMS
COPIED = 5


def slot(t):
    return t % 2


def until(eng, sem, value):
    if isinstance(value, int) and value <= 0:
        return
    eng.wait_ge(sem, value)


def later(i):
    return not (isinstance(i, int) and i == 0)


def looped(eng, count, body):
    body(0)
    with eng.Fori(1, count) as i:
        body(i)


def build(nc, x, norm_w, w_in, b_in, sinks, conv_w, conv_b, mnorm_w, wba, wbm, w_out, fnorm_w, out):
    ctx = ExitStack()
    with ctx:
        def sb(name, shape, dt=F32, stack=None):
            return (stack or ctx).enter_context(nc.sbuf_tensor(name, shape, dt))

        def sem(name):
            return ctx.enter_context(nc.semaphore(name))

        hT_hi = sb("hT_hi", [P, KT, T], F32R)
        hT_lo = sb("hT_lo", [P, KT, T], F32R)
        w_raw = sb("w_raw", [P, 2, KT, P])
        w_hi = [sb(f"w_hi{s}", [P, KT, P], F32R) for s in range(2)]
        w_lo = [sb(f"w_lo{s}", [P, KT, P], F32R) for s in range(2)]
        ev = [sb(f"ev{s}", [P, T]) for s in range(2)]
        ident = sb("ident", [P, P])
        ident_b = sb("ident_b", [P, P], BF16)
        par = sb("par", [P, ROWS])
        par_half = sb("par_half", [P, ROWS])
        from_prev = sb("from_prev", [P, P], I8)
        cur_T = sb("cur_T", [P, P])
        prev_T = sb("prev_T", [P, P])
        causal = sb("causal", [P, P], BF16)
        ones_r = sb("ones_r", [40, P], F32R)
        head_col = sb("head_col", [40, MH])
        pair_mask = sb("pair_mask", [MH, PAIRS, NB])
        decay_rows = sb("decay_rows", [MH, PAIRS, NB])
        decay_tab = sb("decay_tab", [P, PAIRS, NB])
        gate_bias = sb("gate_bias", [40, 1])
        sink_tab = sb("sink_tab", [P, HEADS])
        zero_col = sb("zero_col", [P, 1])
        neg_col = sb("neg_col", [P, 1])
        sumsq = sb("sumsq", [P, 2 * NB])
        rstd = sb("rstd", [P, 2 * NB])
        m_before = sb("m_before", [MH, NB])
        decay = sb("decay", [MH, NB])
        row_max = sb("row_max", [P, GR])
        neg_max = sb("neg_max", [P, GR])
        sink_in = sb("sink_in", [P, GR])
        sink_exp = sb("sink_exp", [P, GR])
        row_sum = sb("row_sum", [P, GR])
        row_inv = sb("row_inv", [P, GR])
        tok_gate = sb("tok_gate", [P, NB, 4, 2])
        pair_decay = sb("pair_decay", [P, NB])
        pair_norm = sb("pair_norm", [P, 2])
        den = sb("den", [P, 2])
        den_inv = sb("den_inv", [P, NB, 2])

        def aliased(groups):
            made = []
            for g in groups:
                with ExitStack() as st:
                    made.append([sb(*a, stack=st) for a in g])
            return made

        (gate_T, c_split), (th0,) = aliased([
            [("gate_T", [P, NB, 4, MH]), ("c_split", [40, T])],
            [("th0", [P, T])]])
        ctx.enter_context(nc.sbuf_tensor("hold_gates", [P, 5, 2 * P], F32))
        (xs,), gt, (U,), (wo_hi,) = aliased([
            [("xs", [P, NB, T])],
            [(f"gt{i}", [P, T]) for i in range(7)] + [("gt_r", [P, T], F32R)],
            [("U", [P, KT, T])],
            [("wo_hi", [P, KT, T], F32R)]])
        ctx.enter_context(nc.sbuf_tensor("hold_u", [P, KT, T], F32))
        att, (u_hi, u_lo), ml, (merged, wo_lo, th1), (_, wo_raw) = aliased([
            [("k_dup", [P, KV, T]), ("v_tok", [P, NB, KV * HD]), ("k_hi", [P, T], F32R), ("k_lo", [P, T], F32R), ("v_head", [P, NB, HD]),
             ("q_split", [P, GR, T], F32R), ("silu_z", [P, 2, T]),
             ("probs0", [P, GR, P]), ("probs1", [P, GR, P]), ("pT_cur", [P, GR, P]), ("pT_prev", [P, GR, P])],
            [("u_hi", [P, KT, T], F32R), ("u_lo", [P, KT, T], F32R)],
            [("raw_q", [P, T + 3]), ("raw_k", [P, T + 3]), ("mq_pad", [P, 2, T]), ("mk_T", [P, T]),
             ("v1", [P, NB, 2, MV + 1]), ("h_tok", [P, NB, 2, MV + 1]), ("gates", [P, 2, T]), ("z_buf", [P, T]),
             ("tanh_buf", [P, T]), ("dmat", [P, 2, P]), ("s_T", [P, 2, P]), ("inter", [P, 2, MV + 1]),
             ("k_w", [P, 2, MK]), ("state", [P, MV + 1]), ("c_heads", [40, 2, T], F32R), ("junk", [P, MV])],
            [("merged", [P, KT, T]), ("wo_lo", [P, KT, T], F32R), ("th1", [P, T])],
            [("under_merged", [P, KT, T]), ("wo_raw", [P, KT, T])]])
        k_dup, v_tok, k_hi, k_lo, v_head, q_split, silu_z, probs0, probs1, pT_cur, pT_prev = att
        probs = [probs0, probs1]
        param_rows = pT_prev[:, 0, :]
        ones8 = pT_cur[0:MH, 0, :]
        parity_sel = pT_cur[0:MH, 1, :]
        (raw_q, raw_k, mq_pad, mk_T, v1, h_tok, gates, z_buf, tanh_buf, dmat, s_T, inter, k_w, state,
         c_heads, junk) = ml
        g_i, g_f, g_t1, g_t2, g_t3, g_t4, g_t5 = gt[:7]
        c_hi = gt[7]

        ps = ctx.enter_context(nc.psum_tensor("ps", [P, 8, BANK], F32))
        X = [4, 5, 6, 7]

        def dense_ps(t):
            return ps[:, 2 * slot(t):2 * slot(t) + 2, :].rearrange("p b n -> p (b n)")

        scr_a = nc.dram_tensor("branch_a_scratch", [KT, P, T], F32).ap()
        scr_g = nc.dram_tensor("tanh_gm_scratch", [KT, P, T], F32).ap()

        params_in = sem("params_in")
        x_in = [sem(f"x_in{i}") for i in range(4)]
        gate_slot_clear = sem("gate_slot_clear")
        w_in_sem = [sem(f"w_landed{s}") for s in range(2)]
        w_split = sem("w_split")
        tile_done = sem("tile_done")
        tile_out = sem("tile_out")
        consts_made = sem("consts_made")
        params_T = sem("params_T")
        params_ready = sem("params_ready")
        x_sumsq = sem("x_sumsq")
        x_var = sem("x_var")
        x_root = sem("x_root")
        x_norm = sem("x_norm")
        x_turned = sem("x_turned")
        hT_hi_ready = sem("hT_hi_ready")
        hT_lo_ready = sem("hT_lo_ready")
        g_log = sem("g_log")
        g_rows = sem("g_rows")
        g_exp = sem("g_exp")
        g_turned = sem("g_turned")
        g_ready = sem("g_ready")
        v_turned = sem("v_turned")
        v_ready = sem("v_ready")
        q_hi_ready = sem("q_hi_ready")
        q_split_ready = sem("q_split_ready")
        kv_head_ready = sem("kv_head_ready")
        scores_done = sem("scores_done")
        cur_copied = sem("cur_copied")
        max_ready = sem("max_ready")
        exp_ready = sem("exp_ready")
        probs_ready = sem("probs_ready")
        probs_turned = sem("probs_turned")
        pT_ready = sem("pT_ready")
        pv_done = sem("pv_done")
        attn_ready = sem("attn_ready")
        z_tanh = sem("z_tanh")
        z_used = sem("z_used")
        attn_gated = sem("attn_gated")
        ga_out = [sem(f"ga_out{s}") for s in range(2)]
        ga_in = [sem(f"ga_in{s}") for s in range(2)]
        u_ready = sem("u_ready")
        u_hi_ready = sem("u_hi_ready")
        u_split = sem("u_split")
        branch_a = sem("branch_a")
        branch_a_out = [sem(f"branch_a_out{s}") for s in range(2)]
        m_raw = sem("m_raw")
        m_conv = sem("m_conv")
        m_tanh = sem("m_tanh")
        m_qk = sem("m_qk")
        m_v_turned = sem("m_v_turned")
        m_v_ready = sem("m_v_ready")
        m_tabs = sem("m_tabs")
        m_scores = sem("m_scores")
        m_decay = sem("m_decay")
        m_inter = sem("m_inter")
        m_sT = sem("m_sT")
        m_prod = sem("m_prod")
        m_state = sem("m_state")
        m_den = sem("m_den")
        m_sumsq = sem("m_sumsq")
        m_var = sem("m_var")
        m_root = sem("m_root")
        m_h = sem("m_h")
        m_h_turned = sem("m_h_turned")
        mz_tanh = sem("mz_tanh")
        mz_used = sem("mz_used")
        gm_ready = sem("gm_ready")
        gm_out = [sem(f"gm_out{s}") for s in range(2)]
        wo_in = [sem(f"wo_in{s}") for s in range(2)]
        wo_hi_ready = sem("wo_hi_ready")
        wo_split = sem("wo_split")
        merged_in = [sem(f"merged_in{s}") for s in range(2)]
        th_in = [sem(f"th_in{s}") for s in range(2)]
        merged_ready = sem("merged_ready")
        mt_hi_ready = sem("mt_hi_ready")
        mt_ready = sem("mt_ready")
        fn_in = sem("fn_in")
        x_again = [sem(f"x_again{s}") for s in range(2)]
        res_ready = sem("res_ready")
        res_sumsq = sem("res_sumsq")
        res_var = sem("res_var")
        res_root = sem("res_root")
        y_ready = sem("y_ready")
        y_out = [sem(f"y_out{s}") for s in range(2)]

        passed = sem("passed")
        sp_passed = sem("sp_passed")

        mt_hi = [hT_hi[:, s, :].rearrange("p (k n) -> p k n", k=KT) for s in range(2)]
        mt_lo = [hT_lo[:, s, :].rearrange("p (k n) -> p k n", k=KT) for s in range(2)]
        th_gm = [th0, th1]
        fnw = w_raw[:, 0].rearrange("p k n -> p (k n)")
        squares = w_raw[:, 1].rearrange("p k n -> p (k n)")

        both_blocks = ps[:, X[0]:X[1] + 1, :].rearrange("p b (h w n) -> p (b h) w n", h=2, w=2)

        block = ctx.enter_context(nc.Block())

        w_cols = w_in.rearrange("(k p) n -> p k n", p=P)
        wba_cols = wba.rearrange("(k p) n -> p k n", p=P)
        wbm_cols = wbm.rearrange("(k p) n -> p k n", p=P)
        x_rows = x.rearrange("(t p) d -> p t d", p=P)
        wo_rows = w_out.rearrange("(k p) n -> p k n", p=P)
        out_rows = out.rearrange("(t p) d -> p t d", p=P)

        @block.sync
        def _(sp):
            for row, src in ((R_Q, b_in[0:MI0]), (R_O, b_in[MO0:GM0 + D]), (R_NORM, norm_w),
                             (R_MNORM, mnorm_w), (R_CONVB, conv_b)):
                rows = src.shape[0] // P
                sp.dma_start(param_rows[row:row + rows, :], src.rearrange("(r n) -> r n", n=P)).then_inc(params_in, 16)
            sp.dma_start(param_rows[R_CONVW:R_CONVW + 32, :],
                         conv_w.rearrange("j (r n) -> (j r) n", n=P)).then_inc(params_in, 16)
            sp.dma_start(gate_bias[0:8, :], b_in[MI0:MF0].rearrange("(h a) -> h a", a=1)).then_inc(params_in, 16)
            sp.dma_start(gate_bias[32:40, :], b_in[MF0:MO0].rearrange("(h a) -> h a", a=1)).then_inc(params_in, 16)
            sp.dma_start(sink_tab[:, :], sinks.partition_broadcast(P)).then_inc(params_in, 16)
            for i in range(4):
                sp.dma_start(xs[:, 2 * i:2 * i + 2, :], x_rows[:, 2 * i:2 * i + 2, :]).then_inc(x_in[i], 16)

            sp.wait_ge(gate_slot_clear, 1)
            sp.dma_start(w_raw[:, 0, :, 0:8], w_cols[:, :, MI0:MF0]).then_inc(w_in_sem[0], 16)
            sp.dma_start(w_raw[:, 0, :, 32:40], w_cols[:, :, MF0:MO0]).then_inc(w_in_sem[0], 16)

            def weights(t0, tiles):
                cols = [c if isinstance(c, int) else sp.snap(c) for _, _, c in tiles]
                need = [n if isinstance(n, int) else sp.snap(n) for n in (t0 + j - 1 for j, _, _ in tiles)]
                for (j, src, _), c, n in zip(tiles, cols, need):
                    until(sp, w_split, n)
                    sp.sem_inc(sp_passed, 1)
                    s = slot(S2 + j)
                    sp.dma_start(w_raw[:, s], src[:, :, ds(c, P)]).then_inc(w_in_sem[s], 16)

            for t, c in ((1, K0), (2, K0 + P), (3, V0), (4, V0 + P)):
                until(sp, w_split, t - 1)
                sp.dma_start(w_raw[:, slot(t)], w_cols[:, :, c:c + P]).then_inc(w_in_sem[slot(t)], 16)

            looped(sp, KV, lambda g: weights(S2 + 6 * g, [
                (0, w_cols, Q0 + 2 * P * g), (1, w_cols, Q0 + P + 2 * P * g),
                (2, w_cols, Z0 + 2 * P * g), (3, w_cols, Z0 + P + 2 * P * g),
                (4, w_cols, GA0 + 2 * P * g), (5, w_cols, GA0 + P + 2 * P * g)]))

            looped(sp, KT // 2, lambda i: weights(S3 + 2 * i, [
                (0, wba_cols, 2 * P * i), (1, wba_cols, P + 2 * P * i)]))

            looped(sp, PAIRS, lambda p: weights(S4 + 10 * p, [
                (0, w_cols, MQ0 + P * p), (1, w_cols, MK0 + P * p),
                (2, w_cols, MV0 + 2 * P * p), (3, w_cols, MV0 + P + 2 * P * p),
                (4, w_cols, MO0 + 2 * P * p), (5, w_cols, MO0 + P + 2 * P * p),
                (6, w_cols, MZ0 + 2 * P * p), (7, w_cols, MZ0 + P + 2 * P * p),
                (8, w_cols, GM0 + 2 * P * p), (9, w_cols, GM0 + P + 2 * P * p)]))

            def branch_m_step(i):
                weights(S5 + 2 * i, [(0, wbm_cols, 2 * P * i), (1, wbm_cols, P + 2 * P * i)])
                if not later(i):
                    sp.wait_ge(u_split, KT + 1)
                    for s in range(2):
                        sp.wait_ge(branch_a_out[s], 16 * (KT // 2))
                rows = [2 * i + j if isinstance(i, int) else sp.snap(2 * i + j) for j in range(2)]
                used = [2 * i + j - 1 if isinstance(i, int) else sp.snap(2 * i + j - 1) for j in range(2)]
                for j in range(2):
                    if later(i):
                        sp.wait_ge(wo_split, used[j])
                    else:
                        sp.wait_ge(gm_out[j], 16 * PAIRS)
                    sp.dma_start(th_gm[j][:], scr_g[ds(rows[j], 1)].rearrange("a p n -> p (a n)")).then_inc(th_in[j], 16)
                    row = ds(rows[j], 1)
                    sp.dma_start(merged[:, row, :], scr_a[row].rearrange("a p n -> p a n")).then_inc(merged_in[j], 16)
                    sp.dma_start(wo_raw[:, row, :], wo_rows[:, row, :]).then_inc(wo_in[j], 16)

            looped(sp, KT // 2, branch_m_step)
            sp.wait_ge(w_split, S6)
            sp.dma_start(fnw, fnorm_w.partition_broadcast(P)).then_inc(fn_in, 16)

            sp.wait_ge(merged_ready, KT)
            for j in range(2):
                sp.dma_start(th_gm[j][:], x_rows[:, j, :]).then_inc(x_again[j], 16)

            def out_step(i):
                last = isinstance(i, int) and i == NB // 2 - 1
                value = lambda v: v if isinstance(v, int) else sp.snap(v)
                done = [value(2 * i + j + 1) for j in range(2)]
                rows = [value(2 * i + j) for j in range(2)]
                ahead = [value(2 * i + j + 2) for j in range(2)]
                if not last:
                    for j in range(2):
                        sp.wait_ge(res_ready, done[j])
                        sp.dma_start(th_gm[j][:], x_rows[:, ds(ahead[j], 1), :].rearrange("p a n -> p (a n)"))\
                            .then_inc(x_again[j], 16)
                for j in range(2):
                    sp.wait_ge(y_ready, done[j])
                    sp.dma_start(out_rows[:, ds(rows[j], 1), :].rearrange("p a n -> p (a n)"), ev[j][:])\
                        .then_inc(y_out[j], 16)

            out_step(0)
            with sp.Fori(1, NB // 2 - 1) as i:
                out_step(i)
            out_step(NB // 2 - 1)

            for s in range(2):
                sp.wait_ge(gm_out[s], 16 * PAIRS)
                sp.wait_ge(y_out[s], 16 * NB // 2)
                sp.wait_ge(ga_out[s], 16 * KV)
                sp.wait_ge(branch_a_out[s], 16 * (KT // 2))

        @block.gpsimd
        def _(pool):
            raw0 = w_raw[:, 0]
            nc.gpsimd.memset(raw0, 0.0).then_inc(gate_slot_clear, 1)

            def triangle(dst, inside, outside, base, free_step, chan):
                nc.gpsimd.memset(dst, inside)
                pool.drain()
                nc.gpsimd.affine_select(out=dst, in_=dst, compare_op=ALU.is_ge, fill=outside, base=base,
                                        pattern=[[free_step, P]], channel_multiplier=chan)

            nc.gpsimd.memset(ident[:], 0.0)
            nc.gpsimd.memset(zero_col[:], 0.0)
            nc.gpsimd.memset(neg_col[:], NEG)
            pool.drain()
            nc.gpsimd.affine_select(out=ident[:], in_=ident[:], compare_op=ALU.not_equal, fill=1.0, base=0,
                                    pattern=[[-1, P]], channel_multiplier=1)
            triangle(from_prev[:], 1.0, 0.0, -1, 1, -1)
            triangle(cur_T[:], 1.0, 0.0, 0, 1, -1)
            triangle(prev_T[:], 1.0, 0.0, -1, -1, 1)
            triangle(causal[:], 0.0, NEG, 0, 1, -1)
            nc.gpsimd.tensor_copy(ident_b[:], ident[:])
            nc.gpsimd.memset(ones_r[:].bitcast(F32), 1.0)
            nc.gpsimd.memset(ones8, 1.0)
            nc.gpsimd.memset(head_col[:], 0.0)
            nc.gpsimd.memset(parity_sel, 0.0)
            nc.gpsimd.memset(pair_mask[:], 1.0)
            pool.drain()
            for first in (0, 32):
                nc.gpsimd.affine_select(out=head_col[:], in_=head_col[:], compare_op=ALU.not_equal, fill=1.0,
                                        base=-first, pattern=[[-1, MH]], channel_multiplier=1)
                pool.drain()
            for q in range(PAIRS):
                v = parity_sel.rearrange("h (r m) -> h r m", r=2)
                nc.gpsimd.affine_select(out=v, in_=v, compare_op=ALU.not_equal, fill=1.0, base=-2 * q,
                                        pattern=[[-1, 2], [0, MK]], channel_multiplier=1)
                pool.drain()
            nc.gpsimd.affine_select(out=pair_mask[:], in_=pair_mask[:], compare_op=ALU.is_ge, fill=0.0, base=0,
                                    pattern=[[-2, PAIRS], [0, NB]], channel_multiplier=1)
            pool.drain()
            nc.gpsimd.affine_select(out=pair_mask[:], in_=pair_mask[:], compare_op=ALU.is_ge, fill=0.0, base=1,
                                    pattern=[[2, PAIRS], [0, NB]], channel_multiplier=-1)
            pool.drain()
            nc.gpsimd.memset(sumsq[:], 0.0).then_inc(consts_made, 1)

            def split(src, hi, lo):
                nc.gpsimd.tensor_tensor(hi, src, zero_col[:].to_broadcast([P, D]), ALU.add)
                pool.drain()
                nc.gpsimd.tensor_tensor(lo, src, hi.bitcast(F32), ALU.subtract).then_inc(w_split, 1)

            def landed(t):
                return 16 * (t // 2 + 1) + (16 if slot(t) == 0 else 0)

            def flat(a):
                return a.rearrange("p k n -> p (k n)")

            def split_tiles(first, i, per):
                for j in range(per):
                    s, t = slot(first + j), first + per * i + j
                    pool.wait_ge(w_in_sem[s], landed(first + j) + 8 * per * i)
                    until(pool, tile_done, t - 1)
                    split(flat(w_raw[:, s]), flat(w_hi[s][:]), flat(w_lo[s][:]))

            for t in range(S1, S2):
                split_tiles(t, 0, 1)
            looped(pool, KV, lambda g: split_tiles(S2, g, 6))
            looped(pool, KT // 2, lambda i: split_tiles(S3, i, 2))
            looped(pool, PAIRS, lambda p: split_tiles(S4, p, 10))
            looped(pool, KT // 2, lambda i: split_tiles(S5, i, 2))

        @block.tensor
        def _(pe):
            def dense(t, s, lo, hi, rhs_hi=hT_hi, rhs_lo=hT_lo, gate=None):
                for m in range(lo, hi):
                    b, r = divmod(m, KT * TERMS)
                    k, term = divmod(r, TERMS)
                    if m == 0:
                        until(pe, w_split, t + 1)
                        until(pe, tile_out, t - 1)
                    if gate is not None and b == 0 and term == 0:
                        pe.wait_ge(gate, gate_from + k + 1)
                    w = (w_hi, w_hi, w_lo)[term][s]
                    r_ = (rhs_hi, rhs_lo, rhs_hi)[term]
                    mm = nc.tensor.matmul(ps[:, 2 * s + b, :], w[:, k, :], r_[:, k, b * BANK:(b + 1) * BANK],
                                          start=(r == 0), stop=(r == KT * TERMS - 1))
                if hi == MMS:
                    mm.then_inc(tile_done, 1)

            gate_from = 0

            pe.wait_ge(consts_made, 1)
            pe.wait_ge(params_in, 16 * 9)
            nc.tensor.transpose(ps[:, X[3], 0:ROWS], param_rows[0:ROWS, :], ident[0:ROWS, 0:ROWS]).then_inc(params_T, 1)
            for half in range(2):
                for k in range(KT):
                    if k == 0:
                        pe.wait_ge(x_norm, half + 1)
                    if half == 0 and k == X[3]:
                        pe.wait_ge(params_ready, 1)
                    if half == 1:
                        pe.wait_ge(hT_lo_ready, k + 1)
                    for j in range(4):
                        t = 4 * half + j
                        mm = nc.tensor.transpose(ps[:, k, j * P:(j + 1) * P], xs[:, t, k * P:(k + 1) * P], ident[:])
                    mm.then_inc(x_turned, 1)

            pe.wait_ge(hT_lo_ready, 2 * KT)
            for t in range(S1, S2):
                dense(t, slot(t), 0, MMS)
            pe.wait_ge(g_exp, 1)
            for c in range(NB):
                mm = nc.tensor.transpose(ps[:, X[c // 4], (c % 4) * P:(c % 4 + 1) * P],
                                         g_t4[:, c * P:(c + 1) * P], ident[:])
            nc.tensor.matmul(ps[:, X[2], 0:PAIRS * NB], parity_sel,
                             decay_rows[:].rearrange("h a b -> h (a b)"), start=True, stop=True)\
                .then_inc(g_turned, 1)
            pe.wait_ge(g_ready, 1)
            pe.wait_ge(tile_out, S2 - 1)
            for n, (buf, t) in enumerate(((ev[1], 3), (ev[0], 4))):
                until(pe, tile_out, t + 1)
                for c in range(NB):
                    mm = nc.tensor.transpose(ps[:, X[2 * n + c // 4], (c % 4) * P:(c % 4 + 1) * P],
                                             buf[:, c * P:(c + 1) * P], ident[:])
                mm.then_inc(v_turned, 1)

            pe.wait_ge(v_ready, 2)

            def scores(n):
                first = max(n - 1, 0)
                for h in range(GR):
                    o = ps[:, X[h // 2], (h % 2) * 2 * P + (P if n == 0 else 0):(h % 2 + 1) * 2 * P]
                    for part in (k_hi, k_lo):
                        mm = nc.tensor.matmul(o, q_split[:, h, n * P:(n + 1) * P], part[:, first * P:(n + 1) * P],
                                              start=(part is k_hi), stop=(part is k_lo))
                return mm

            def attention_step(g):
                t0 = S2 + 6 * g
                dense(t0, 1, 0, MMS)
                dense(t0 + 1, 0, 0, MMS)
                done = [0]

                def more(hi):
                    lo = done[0]
                    for j in range(4):
                        a, b = max(lo, j * MMS), min(hi, (j + 1) * MMS)
                        if a < b:
                            dense(t0 + 2 + j, slot(S2 + j), a - j * MMS, b - j * MMS)
                    done[0] = hi

                more(lead)
                for n in range(NB + 2):
                    if n < NB:
                        if n == 0:
                            pe.wait_ge(kv_head_ready, g + 1)
                            pe.wait_ge(tile_out, t0 + 2)
                        else:
                            pe.wait_ge(cur_copied, NB * g + n)
                            pe.wait_ge(max_ready, NB * g + n)
                        scores(n).then_inc(scores_done, 1)
                    if n >= 2:
                        m = n - 2
                        pe.wait_ge(pT_ready, NB * g + m + 1)
                        if 1 <= m <= COPIED:
                            pe.wait_ge(attn_ready, COPIED * g + m)
                        if m > COPIED:
                            pe.wait_ge(attn_gated, (NB - 1 - COPIED) * g + m - COPIED)
                        for r in range(2):
                            o = ps[64 * r:64 * r + 64, X[3], 0:2 * P]
                            mm = nc.tensor.matmul(o, v_head[:, m, :], pT_cur[:, r:GR:2, :], start=True, stop=(m == 0))
                            if m:
                                mm = nc.tensor.matmul(o, v_head[:, m - 1, :], pT_prev[:, r:GR:2, :], start=False, stop=True)
                        mm.then_inc(pv_done, 1)
                    if 1 <= n <= NB:
                        pe.wait_ge(probs_ready, NB * g + n)
                        for h in range(GR):
                            mm = nc.tensor.transpose(ps[:, X[2], h * P:(h + 1) * P], probs[(n - 1) % 2][:, h, :], ident[:])
                        mm.then_inc(probs_turned, 1)
                    if n <= NB:
                        more(lead + (4 * MMS - lead - tail) * (n + 1) // (NB + 1))
                more(4 * MMS)

            lead = 16
            tail = 28
            looped(pe, KV, attention_step)

            def branch_a_step(i):
                for j in range(2):
                    dense(S3 + j + 2 * i, slot(S3 + j), 0, MMS, u_hi, u_lo, gate=u_split if j == 0 else None)

            looped(pe, KT // 2, branch_a_step)

            def mlstm_step(p):
                t0 = S4 + 10 * p
                for j in range(4):
                    dense(t0 + j, slot(S4 + j), 0, MMS)
                done = [0]

                def more(hi):
                    lo = done[0]
                    for j in range(6):
                        a, b = max(lo, j * MMS), min(hi, (j + 1) * MMS)
                        if a < b:
                            dense(t0 + 4 + j, slot(S4 + j), a - j * MMS, b - j * MMS)
                    done[0] = hi

                def turn_v(j):
                    pe.wait_ge(tile_out, t0 + 3 + j)
                    for c in range(NB):
                        mm = nc.tensor.transpose(ps[:, X[2 * j + c // 4], (c % 4) * P:(c % 4 + 1) * P],
                                                 ev[j][:, c * P:(c + 1) * P], ident[:])
                    mm.then_inc(m_v_turned, 1)

                if later(p):
                    pe.wait_ge(u_ready, KV + p)
                turn_v(0)
                more(12)
                turn_v(1)
                more(24)
                pe.wait_ge(m_qk, 2 * (p + 1))
                pe.wait_ge(m_tabs, p + 1)
                pe.wait_ge(m_v_ready, 2 * (p + 1))
                each = (5 * MMS - 24) // (2 * NB)
                for c in range(NB):
                    tok = slice(c * P, (c + 1) * P)
                    if c:
                        pe.wait_ge(m_inter, 7 * p + c - 1) if c > 1 else None
                        pe.wait_ge(m_decay, 8 * p + c)
                        pe.wait_ge(m_state, 8 * p + c)
                    nc.tensor.matmul(ps[:, X[0], 0:2 * P], ones_r[:], c_heads[:, :, tok], start=True, stop=False)
                    nc.tensor.matmul(ps[:, X[0], 0:2 * P], ident_b[:],
                                     causal[:].unsqueeze(1).to_broadcast([P, 2, P]), start=False, stop=True)
                    nc.tensor.matmul(ps[:, X[1], 0:2 * P], mk_T[:, tok], mq_pad[:, :, tok], start=True, stop=True)
                    mm = nc.tensor.transpose(ps[:, X[1], 2 * P:3 * P], mk_T[:, tok], ident[:])
                    if c:
                        for j in range(2):
                            mm = nc.tensor.matmul(ps[:, X[3], j * (MV + 1):(j + 1) * (MV + 1)], mq_pad[:, j, tok],
                                                  state[:], start=True, stop=True)
                    mm.then_inc(m_scores, 1)
                    more(24 + each * (2 * c + 1))
                    pe.wait_ge(m_sT, 8 * p + c + 1)
                    for j in range(2):
                        mm = nc.tensor.matmul(ps[:, X[2], j * (MV + 1):(j + 1) * (MV + 1)], s_T[:, j, :], v1[:, c, j, :],
                                              start=True, stop=True)
                    if c < NB - 1:
                        for j in range(2):
                            mm = nc.tensor.matmul(ps[64 * j:64 * j + 64, X[2], 2 * (MV + 1):3 * (MV + 1)], k_w[:, j, :],
                                                  v1[:, c, j, :], start=True, stop=True)
                    mm.then_inc(m_prod, 1)
                    more(24 + each * (2 * c + 2))
                more(6 * MMS)
                pe.wait_ge(m_h, p + 1)
                for j in range(2):
                    for c in range(NB):
                        mm = nc.tensor.transpose(ps[:, X[2 * j + c // 4], (c % 4) * P:(c % 4 + 1) * P],
                                                 h_tok[:, c, j, 0:MV], ident[:])
                mm.then_inc(m_h_turned, 1)

            looped(pe, PAIRS, mlstm_step)

            gate_from = KT

            def branch_m_step(i):
                dense(S5 + 2 * i, 1, 0, MMS, gate=u_split)
                dense(S5 + 1 + 2 * i, 0, 0, MMS)

            looped(pe, KT // 2, branch_m_step)

            pe.wait_ge(wo_split, KT)

            def out_step(i):
                for j in range(2):
                    s = slot(S6 + j)
                    pe.wait_ge(mt_ready, 2 * i + j + 1)
                    pe.wait_ge(tile_out, S6 - 1 + 2 * i + j)
                    for b in range(2):
                        for k in range(KT):
                            for term in range(TERMS):
                                lhs = (mt_hi, mt_lo, mt_hi)[term][j]
                                rhs = (wo_hi, wo_hi, wo_lo)[term]
                                mm = nc.tensor.matmul(ps[:, 2 * s + b, :], lhs[:, k, :],
                                                      rhs[:, k, b * BANK:(b + 1) * BANK],
                                                      start=(k == 0 and term == 0), stop=(k == KT - 1 and term == TERMS - 1))
                    mm.then_inc(tile_done, 1)

            looped(pe, NB // 2, out_step)

        @block.scalar
        def _(act):
            A = nc.scalar.activation

            act.wait_ge(params_T, 1)
            A(par[:], ps[:, X[3], 0:ROWS], ACT.Copy)
            A(par_half[:], ps[:, X[3], 0:ROWS], ACT.Copy, scale=0.5).then_inc(params_ready, 1)
            for half in range(2):
                for j in range(4):
                    t = 4 * half + j
                    if j % 2 == 0:
                        act.wait_ge(x_in[t // 2], 16)
                    act.drain()
                    ins = A(ev[0][:], xs[:, t, :], ACT.Square, accum_out=sumsq[:, t:t + 1])
                ins.then_inc(x_sumsq, 1)
                act.wait_ge(x_var, half + 1)
                A(rstd[:, 4 * half:4 * half + 4], rstd[:, 4 * half:4 * half + 4], ACT.Sqrt).then_inc(x_root, 1)
            for half in range(2):
                for k in range(KT):
                    act.wait_ge(x_turned, KT * half + k + 1)
                    A(hT_hi[:, k, half * BANK:(half + 1) * BANK], ps[:, k, :], ACT.Copy,
                      scale=par[:, R_NORM + k:R_NORM + k + 1]).then_inc(hT_hi_ready, 1)

            act.wait_ge(tile_done, 1)
            A(g_i[0:8, :], dense_ps(0)[0:8, :], ACT.Identity, bias=gate_bias[0:8, :])
            A(g_f[0:8, :], dense_ps(0)[32:40, :], ACT.Identity, bias=gate_bias[32:40, :]).then_inc(tile_out, 1)
            act.drain()
            A(g_t1[0:8, :], g_f[0:8, :], ACT.Abs)
            act.drain()
            A(g_t1[0:8, :], g_t1[0:8, :], ACT.Exp, scale=-1.0)
            act.drain()
            A(g_t1[0:8, :], g_t1[0:8, :], ACT.Ln, bias=1.0).then_inc(g_log, 1)
            for t in (1, 2):
                act.wait_ge(tile_done, t + 1)
                for half in range(2):
                    g = 2 * (t - 1) + half
                    for r in range(2):
                        ins = A(k_dup[64 * r:64 * r + 64, g, :], dense_ps(t)[64 * half:64 * half + 64, :], ACT.Identity,
                                bias=par[64 * half:64 * half + 64, R_K + t - 1:R_K + t])
                ins.then_inc(tile_out, 1)
                if t == 1:
                    act.wait_ge(g_rows, 1)
                    A(g_t4[32:40, :], g_f[0:8, :], ACT.Exp)
                    A(g_t4[64:72, :], g_t2[0:8, :], ACT.Exp)
                    A(g_t4[96:104, :], g_t3[0:8, :], ACT.Exp, scale=-1.0)
                    A(decay[:], g_f[0:8, :].rearrange("h (c n) -> h c n", n=P)[:, :, P - 1], ACT.Exp)
                    act.drain()
                    for q in range(PAIRS):
                        ins = A(decay_rows[:, q, :], decay[:], ACT.Copy, scale=pair_mask[:, q, 0:1])
                    ins.then_inc(g_exp, 1)
            act.wait_ge(g_turned, 1)
            for b in range(2):
                for c in range(4):
                    A(gate_T[:, 4 * b + c], ps[:, X[b], c * P:(c + 1) * P].rearrange("p (q h) -> p q h", h=32)[:, :, 0:MH],
                      ACT.Copy)
            A(decay_tab[:].rearrange("p a b -> p (a b)"), ps[:, X[2], 0:PAIRS * NB], ACT.Copy).then_inc(g_ready, 1)
            for t in (3, 4):
                act.wait_ge(tile_done, t + 1)
                A(ev[t % 2][:], dense_ps(t), ACT.Identity, bias=par[:, R_V + t - 3:R_V + t - 2]).then_inc(tile_out, 1)

            def ga_tile(g, j):
                act.wait_ge(tile_done, S2 + 5 + j + 6 * g)
                act.wait_ge(z_used, 2 * g + j + 1)
                A(ev[j][:], dense_ps(S2 + j), ACT.Tanh, scale=0.5, bias=par_half[:, ds(R_GA + j + 2 * g, 1)])\
                    .then_inc(tile_out, 1)
                act.drain()
                act.dma_start(scr_a[ds(2 * g + j, 1)].rearrange("a p n -> p (a n)"), ev[j][:]).then_inc(ga_out[j], 16)

            def attention_step(g):
                t0 = S2 + 6 * g
                if later(g):
                    ga_tile(g - 1, 1)
                for j in range(2):
                    act.wait_ge(tile_done, t0 + 1 + j)
                    for r in range(2):
                        rows = slice(64 * r, 64 * r + 64)
                        A(q_split[0:64, 2 * j + r, :], dense_ps(S2 + j)[rows, :], ACT.Identity,
                          bias=par[rows, ds(R_Q + j + 2 * g, 1)]).then_inc(q_hi_ready, 1)
                    act.wait_ge(q_split_ready, GR * g + 2 * j + 2)
                    act.sem_inc(tile_out, 1)

                def z_tile(j):
                    act.wait_ge(tile_done, t0 + 3 + j)
                    if later(g):
                        act.wait_ge(u_ready, g)
                        act.wait_ge(ga_out[j], 16 * g)
                    else:
                        act.wait_ge(v_turned, 2)
                    A(silu_z[:, j, :], dense_ps(S2 + j), ACT.Identity, bias=par[:, ds(R_Z + j + 2 * g, 1)]).then_inc(tile_out, 1)
                    act.drain()
                    A(ev[j][:], silu_z[:, j, :], ACT.Tanh, scale=0.5).then_inc(z_tanh, 1)

                for n in range(NB + 2):
                    if n < NB:
                        pr = probs[n % 2]
                        act.wait_ge(scores_done, NB * g + n + 1)
                        if n >= 2:
                            act.wait_ge(probs_turned, NB * g + n - 1)
                        A(pr[:], both_blocks[:, :, 1, :], ACT.Copy).then_inc(cur_copied, 1)
                        act.wait_ge(max_ready, NB * g + n + 1)
                        for h in range(GR):
                            A(pr[:, h, :], pr[:, h, :], ACT.Exp, scale=HD ** -0.5, bias=neg_max[:, h:h + 1],
                              accum_out=row_sum[:, h:h + 1])
                        A(sink_exp[:], sink_in[:], ACT.Exp).then_inc(exp_ready, 1)
                    if 2 <= n < COPIED + 2:
                        m = n - 2
                        act.wait_ge(pv_done, NB * g + m + 1)
                        A(U[:, ds(2 * g, 2), m * P:(m + 1) * P], ps[:, X[3], 0:2 * P].rearrange("p (j n) -> p j n", j=2),
                          ACT.Copy).then_inc(attn_ready, 1)
                    if n == 2:
                        z_tile(0)
                    if n == 5:
                        z_tile(1)
                ga_tile(g, 0)

            looped(act, KV, attention_step)

            act.wait_ge(pv_done, KV * NB)
            for k in range(KT):
                if k % 2 == 0:
                    act.wait_ge(u_ready, k // 2 + 1)
                A(u_hi[:, k, :], U[:, k, :], ACT.Copy).then_inc(u_hi_ready, 1)
            ga_tile(KV - 1, 1)

            def branch_a_step(i):
                for j in range(2):
                    if later(i):
                        act.wait_ge(branch_a_out[j], 16 * i)
                    else:
                        act.wait_ge(ga_out[j], 16 * KV)
                    act.dma_start(ev[j][:], scr_a[ds(2 * i + j, 1)].rearrange("a p n -> p (a n)")).then_inc(ga_in[j], 16)
                for j in range(2):
                    act.wait_ge(branch_a, 2 * i + j + 1)
                    act.sem_inc(tile_out, 1)
                    act.dma_start(scr_a[ds(2 * i + j, 1)].rearrange("a p n -> p (a n)"), ev[j][:])\
                        .then_inc(branch_a_out[j], 16)

            looped(act, KT // 2, branch_a_step)

            def mlstm_step(p):
                t0 = S4 + 10 * p
                for j, (raw, row) in enumerate(((raw_q, R_MQ), (raw_k, R_MK))):
                    act.wait_ge(tile_done, t0 + 1 + j)
                    A(raw[:, 3:], dense_ps(S4 + j), ACT.Identity, bias=par[:, ds(row + p, 1)]).then_inc(tile_out, 1)
                act.wait_ge(m_conv, 2 * p + 1)
                if later(p):
                    act.wait_ge(mz_used, 2 * p)
                A(tanh_buf[:], z_buf[:], ACT.Tanh, scale=0.5).then_inc(m_tanh, 1)

                def v_tile(j):
                    act.wait_ge(tile_done, t0 + 3 + j)
                    if not later(p):
                        act.wait_ge(branch_a_out[j], 16 * (KT // 2))
                    else:
                        act.wait_ge(gm_out[j], 16 * p)
                    A(ev[j][:], dense_ps(S4 + j), ACT.Identity, bias=par[:, ds(R_MV + j + 2 * p, 1)]).then_inc(tile_out, 1)

                v_tile(0)
                act.wait_ge(m_conv, 2 * p + 2)
                act.wait_ge(m_qk, 2 * p + 1)
                A(tanh_buf[:], mk_T[:], ACT.Tanh, scale=0.5).then_inc(m_tanh, 1)
                v_tile(1)

                def o_tile(j):
                    act.wait_ge(tile_done, t0 + 5 + j)
                    if later(p):
                        act.wait_ge(u_ready, KV + p)
                    A(gates[:, j, :], dense_ps(S4 + j), ACT.Tanh, scale=0.5,
                      bias=par_half[:, ds(R_O + j + 2 * p, 1)]).then_inc(tile_out, 1)

                def z_tile(j):
                    act.wait_ge(tile_done, t0 + 7 + j)
                    if j == 0:
                        act.wait_ge(m_qk, 2 * p + 2)
                    else:
                        act.wait_ge(mz_used, 2 * p + 1)
                    A(z_buf[:], dense_ps(S4 + j), ACT.Identity, bias=par[:, ds(R_MZ + j + 2 * p, 1)]).then_inc(tile_out, 1)
                    act.drain()
                    A(tanh_buf[:], z_buf[:], ACT.Tanh, scale=0.5).then_inc(mz_tanh, 1)

                def gm_tile(j):
                    act.wait_ge(tile_done, t0 + 9 + j)
                    act.wait_ge(m_v_turned, 2 * p + 1 + j)
                    A(ev[j][:], dense_ps(S4 + j), ACT.Tanh, scale=0.5,
                      bias=par_half[:, ds(R_GM + j + 2 * p, 1)]).then_inc(tile_out, 1)
                    act.drain()
                    act.dma_start(scr_g[ds(2 * p + j, 1)].rearrange("a p n -> p (a n)"), ev[j][:]).then_inc(gm_out[j], 16)

                def sum_squares(c):
                    act.drain()
                    act.wait_ge(m_den, 8 * p + c + 1)
                    for j in range(2):
                        if j:
                            act.drain()
                        ins = A(junk[:], h_tok[:, c, j, 0:MV], ACT.Square, scale=den_inv[:, c, j:j + 1],
                                accum_out=sumsq[:, 2 * c + j:2 * c + j + 1])
                    return ins

                for c in range(NB):
                    act.wait_ge(m_scores, 8 * p + c + 1)
                    if c >= 1:
                        act.wait_ge(m_sT, 8 * p + c)
                    for j in range(2):
                        ins = A(dmat[:, j, :], ps[:, X[0], j * P:(j + 1) * P], ACT.Exp, bias=tok_gate[:, c, 0, j:j + 1])
                    ins.then_inc(m_decay, 1)
                    if c:
                        act.wait_ge(m_state, 8 * p + c)
                        for j in range(2):
                            ins = A(inter[:, j, :], ps[:, X[3], j * (MV + 1):(j + 1) * (MV + 1)], ACT.Copy,
                                    scale=tok_gate[:, c, 1, j:j + 1])
                        ins.then_inc(m_inter, 1)
                        sum_squares(c - 1)
                    if c == 1:
                        o_tile(0)
                    if c == 3:
                        o_tile(1)
                    if c == 5:
                        z_tile(0)
                    if c == 7:
                        z_tile(1)
                gm_tile(0)
                sum_squares(NB - 1).then_inc(m_sumsq, 1)
                act.wait_ge(m_var, p + 1)
                A(rstd[:], rstd[:], ACT.Sqrt).then_inc(m_root, 1)
                gm_tile(1)

            looped(act, PAIRS, mlstm_step)

            act.wait_ge(tile_done, S5)
            for k in range(KT):
                act.wait_ge(u_ready, KV + (k // 2) + 1)
                A(hT_hi[:, k, :], U[:, k, :], ACT.Copy).then_inc(u_hi_ready, 1)

            def branch_m_step(i):
                for j in range(2):
                    act.wait_ge(tile_done, S5 + 1 + j + 2 * i)
                    if not later(i):
                        act.wait_ge(gm_out[j], 16 * PAIRS)
                    else:
                        act.wait_ge(merged_ready, 2 * i + j - 1)
                    A(ev[j][:], dense_ps(S5 + j), ACT.Copy).then_inc(tile_out, 1)
                    if not later(i) and j == 0:
                        act.wait_ge(u_split, 2 * KT)
                    act.wait_ge(wo_in[j], 16 * (i + 1))
                    row = ds(2 * i + j, 1)
                    A(wo_hi[:, row, :], wo_raw[:, row, :], ACT.Copy).then_inc(wo_hi_ready, 1)

            looped(act, KT // 2, branch_m_step)

            act.wait_ge(merged_ready, KT)
            act.wait_ge(tile_done, S6)

            def token_tile(n, j):
                A(mt_hi[j], merged[:, :, ds(P * n, P)], ACT.Copy).then_inc(mt_hi_ready, 1)

            token_tile(0, 0)
            token_tile(1, 1)
            act.wait_ge(fn_in, 16)

            def out_step(i):
                for j in range(2):
                    act.wait_ge(tile_done, S6 + 1 + 2 * i + j)
                    if later(i):
                        act.wait_ge(y_out[j], 16 * i)
                    A(ev[j][:], dense_ps(S6 + j), ACT.Copy, scale=0.5).then_inc(tile_out, 1)
                    if not (isinstance(i, int) and i == NB // 2 - 1):
                        token_tile(2 * (i + 1) + j, j)
                    act.wait_ge(res_ready, 2 * i + j + 1)
                    A(squares, ev[j][:], ACT.Square, accum_out=sumsq[:, j:j + 1]).then_inc(res_sumsq, 1)
                    act.wait_ge(res_var, 2 * i + j + 1)
                    A(rstd[:, j:j + 1], rstd[:, j:j + 1], ACT.Sqrt).then_inc(res_root, 1)

            out_step(0)
            with act.Fori(1, NB // 2 - 1) as i:
                out_step(i)
            out_step(NB // 2 - 1)

        @block.vector
        def _(dve):
            V = nc.vector

            for half in range(2):
                cols = rstd[:, 4 * half:4 * half + 4]
                dve.wait_ge(x_sumsq, half + 1)
                V.tensor_scalar(cols, sumsq[:, 4 * half:4 * half + 4], 1.0 / D, EPS, ALU.mult, ALU.add).then_inc(x_var, 1)
                dve.wait_ge(x_root, half + 1)
                V.reciprocal(cols, cols)
                dve.drain()
                for j in range(4):
                    t = 4 * half + j
                    ins = V.tensor_scalar(xs[:, t, :], xs[:, t, :], rstd[:, t:t + 1], None, ALU.mult)
                ins.then_inc(x_norm, 1)
            for half in range(2):
                for k in range(KT):
                    part = slice(half * BANK, (half + 1) * BANK)
                    dve.wait_ge(hT_hi_ready, KT * half + k + 1)
                    V.scalar_tensor_tensor(hT_lo[:, k, part], ps[:, k, :], par[:, R_NORM + k:R_NORM + k + 1],
                                           hT_hi[:, k, part].bitcast(F32), ALU.mult, ALU.subtract).then_inc(hT_lo_ready, 1)

            i_, f_ = g_i[0:8, :], g_f[0:8, :]
            chunks = lambda a: a.rearrange("h (c n) -> h c n", n=P)
            logf, m_, b_ = g_t2[0:8, :], g_t3[0:8, :], g_t5[0:8, :]
            dve.wait_ge(g_log, 1)
            V.tensor_scalar(logf, f_, 0.0, None, ALU.min)
            V.memset(g_t4[:], 0.0)
            V.memset(c_split[:], 0.0)
            V.memset(m_before[:], NEG)
            dve.drain()
            V.tensor_tensor(logf, logf, g_t1[0:8, :], ALU.subtract)
            dve.drain()
            V.tensor_tensor_scan(m_, logf, i_, NEG, ALU.add, ALU.max)
            for c in range(NB):
                V.tensor_tensor_scan(b_[:, c * P:(c + 1) * P], ones8, logf[:, c * P:(c + 1) * P], 0.0, ALU.mult, ALU.add)
            dve.drain()
            V.tensor_tensor(g_t4[0:8, :], i_, b_, ALU.subtract)
            V.tensor_tensor(b_, b_, m_, ALU.subtract)
            V.tensor_copy(m_before[:, 1:NB], chunks(m_)[:, 0:NB - 1, P - 1])
            dve.drain()
            V.tensor_tensor(chunks(f_), chunks(b_), m_before[:].unsqueeze(2).to_broadcast([MH, NB, P]), ALU.add)
            V.tensor_tensor(chunks(logf), chunks(g_t4[0:8, :]),
                            chunks(b_)[:, :, P - 1:P].to_broadcast([MH, NB, P]), ALU.add).then_inc(g_rows, 1)
            V.tensor_copy(c_hi[0:8, :], b_)
            dve.drain()
            V.tensor_tensor(c_split[32:40, :], b_, c_hi[0:8, :].bitcast(F32), ALU.subtract)
            V.tensor_copy(c_split[0:8, :], c_hi[0:8, :].bitcast(F32))
            for n in range(2):
                dve.wait_ge(v_turned, n + 1)
                for b in range(2):
                    ins = V.tensor_copy(v_tok[:, 4 * b:4 * b + 4, n * P:(n + 1) * P],
                                        ps[:, X[2 * n + b], :].rearrange("p (c n) -> p c n", n=P))
                ins.then_inc(v_ready, 1)

            def attention_step(g):
                dve.drain()
                until(dve, pv_done, NB * g)
                k_g = k_dup[:, ds(g, 1), :].rearrange("p a n -> p (a n)")
                V.tensor_copy(k_hi[:], k_g)
                dve.drain()
                V.tensor_tensor(k_lo[:], k_g, k_hi[:].bitcast(F32), ALU.subtract)
                V.tensor_copy(v_head[:], v_tok[:, :, ds(HD * g, HD)]).then_inc(kv_head_ready, 1)

                for h in range(GR):
                    j, r = divmod(h, 2)
                    rows = slice(64 * r, 64 * r + 64)
                    dve.wait_ge(q_hi_ready, GR * g + h + 1)
                    V.scalar_tensor_tensor(q_split[64:128, h, :], dense_ps(S2 + j)[rows, :], par[rows, ds(R_Q + j + 2 * g, 1)],
                                           q_split[0:64, h, :].bitcast(F32), ALU.add, ALU.subtract).then_inc(q_split_ready, 1)

                def combine(n):
                    pr = probs[n % 2]
                    dve.wait_ge(cur_copied, NB * g + n + 1)
                    dve.sem_inc(passed, 1)
                    if n:
                        V.copy_predicated(pr[:], from_prev[:].unsqueeze(1).to_broadcast([P, GR, P]),
                                          both_blocks[:, :, 0, :])
                    else:
                        V.copy_predicated(pr[:], from_prev[:].unsqueeze(1).to_broadcast([P, GR, P]),
                                          neg_col[:].unsqueeze(1).to_broadcast([P, GR, P]))
                    dve.drain()
                    V.tensor_reduce(row_max[:], pr[:], AXX, ALU.max)
                    dve.drain()
                    sink = sink_tab[:, ds(GR * g, GR)]
                    V.scalar_tensor_tensor(row_max[:], row_max[:], HD ** -0.5, sink, ALU.mult, ALU.max)
                    dve.drain()
                    V.tensor_tensor(sink_in[:], sink, row_max[:], ALU.subtract)
                    V.tensor_scalar(neg_max[:], row_max[:], -1.0, None, ALU.mult).then_inc(max_ready, 1)

                def normalise(n):
                    pr = probs[n % 2]
                    dve.wait_ge(exp_ready, NB * g + n + 1)
                    V.tensor_tensor(row_inv[:], row_sum[:], sink_exp[:], ALU.add)
                    dve.drain()
                    V.tensor_scalar(row_inv[:], row_inv[:], 2.0, None, ALU.mult)
                    dve.drain()
                    V.reciprocal(row_inv[:], row_inv[:])
                    dve.drain()
                    V.tensor_tensor(pr[:], pr[:], row_inv[:].unsqueeze(2).to_broadcast([P, GR, P]), ALU.mult)\
                        .then_inc(probs_ready, 1)

                def select(n):
                    dve.wait_ge(probs_turned, NB * g + n + 1)
                    if n:
                        dve.wait_ge(pv_done, NB * g + n)
                    src = ps[:, X[2], :].rearrange("p (h n) -> p h n", n=P)
                    ins = V.tensor_tensor(pT_cur[:], src, cur_T[:].unsqueeze(1).to_broadcast([P, GR, P]), ALU.mult)
                    if n:
                        ins = V.tensor_tensor(pT_prev[:], src, prev_T[:].unsqueeze(1).to_broadcast([P, GR, P]), ALU.mult)
                    ins.then_inc(pT_ready, 1)

                def silu(j):
                    dve.wait_ge(z_tanh, 2 * g + j + 1)
                    V.scalar_tensor_tensor(silu_z[:, j, :], ev[j][:], 1.0, silu_z[:, j, :], ALU.add, ALU.mult)\
                        .then_inc(z_used, 1)

                for n in range(NB + 2):
                    if n < NB:
                        combine(n)
                    if 1 <= n <= NB:
                        select(n - 1)
                    if n >= COPIED + 2:
                        m = n - 2
                        dve.wait_ge(pv_done, NB * g + m + 1)
                        ins = V.tensor_tensor(U[:, ds(2 * g, 2), m * P:(m + 1) * P],
                                              ps[:, X[3], 0:2 * P].rearrange("p (j n) -> p j n", j=2),
                                              silu_z[:, :, m * P:(m + 1) * P], ALU.mult)
                        ins.then_inc(u_ready if m == NB - 1 else attn_gated, 1)
                    if n < NB:
                        normalise(n)
                    if n == 3:
                        silu(0)
                    if n == COPIED + 1:
                        silu(1)
                        dve.drain()
                    if n == NB:
                        dve.wait_ge(attn_ready, COPIED * (g + 1))
                        copied = U[:, ds(2 * g, 2), 0:COPIED * P]
                        V.tensor_tensor(copied, copied, silu_z[:, :, 0:COPIED * P], ALU.mult)

            looped(dve, KV, attention_step)

            dve.drain()
            for k in range(KT):
                dve.wait_ge(u_hi_ready, k + 1)
                V.tensor_tensor(u_lo[:, k, :], U[:, k, :], u_hi[:, k, :].bitcast(F32), ALU.subtract).then_inc(u_split, 1)

            def branch_a_step(i):
                for j in range(2):
                    dve.wait_ge(ga_in[j], 16 * (i + 1))
                    dve.wait_ge(tile_done, S3 + 1 + j + 2 * i)
                    V.scalar_tensor_tensor(ev[j][:], ev[j][:], 1.0, dense_ps(S3 + j), ALU.add, ALU.mult)\
                        .then_inc(branch_a, 1)

            looped(dve, KT // 2, branch_a_step)

            dve.wait_ge(tile_done, S4)
            V.memset(v1[:, :, :, MV:MV + 1], 1.0)
            for raw in (raw_q, raw_k):
                V.memset(raw[:, 0:3], 0.0)
            for r in range(2):
                V.memset(mq_pad[64 * (1 - r):64 * (1 - r) + 64, r, :], 0.0)

            def mlstm_step(p):
                t0 = S4 + 10 * p
                dve.drain()
                dve.wait_ge(tile_out, t0 + 1)
                V.tensor_copy(tok_gate[:], gate_T[:, :, :, ds(2 * p, 2)])
                V.tensor_copy(pair_decay[:], decay_tab[:, ds(p, 1), :].rearrange("p a c -> p (a c)"))
                V.tensor_copy(pair_norm[:], par[:, ds(R_MNORM + 2 * p, 2)])
                for j in range(2):
                    V.tensor_scalar(c_heads[:, j, :], c_split[:], head_col[:, ds(2 * p + j, 1)], None, ALU.mult)
                dve.drain()
                V.tensor_scalar(tok_gate[:, :, 1, :], tok_gate[:, :, 1, :], 0.5 * MK ** -0.5, None, ALU.mult)
                V.tensor_scalar(pair_norm[:], pair_norm[:], 0.25, None, ALU.mult).then_inc(m_tabs, 1)
                for j, (raw, dst) in enumerate(((raw_q, z_buf), (raw_k, mk_T))):
                    dve.wait_ge(tile_out, t0 + 1 + j)
                    tap = lambda n: par[:, ds(R_CONVW + 8 * n + 4 * j + p, 1)]
                    V.tensor_scalar(dst[:], raw[:, 3:T + 3], tap(3), par[:, ds(R_CONVB + 4 * j + p, 1)], ALU.mult, ALU.add)
                    for n in range(3):
                        dve.drain()
                        ins = V.scalar_tensor_tensor(dst[:], raw[:, n:T + n], tap(n), dst[:], ALU.mult, ALU.add)
                    ins.then_inc(m_conv, 1)
                    dve.wait_ge(m_tanh, 2 * p + j + 1)
                    if j == 0:
                        for r in range(2):
                            rows = slice(64 * r, 64 * r + 64)
                            ins = V.scalar_tensor_tensor(mq_pad[rows, r, :], tanh_buf[rows, :], 1.0, z_buf[rows, :],
                                                         ALU.add, ALU.mult)
                    else:
                        ins = V.scalar_tensor_tensor(mk_T[:], tanh_buf[:], 1.0, mk_T[:], ALU.add, ALU.mult)
                    ins.then_inc(m_qk, 1)
                for j in range(2):
                    dve.wait_ge(m_v_turned, 2 * p + j + 1)
                    for b in range(2):
                        ins = V.tensor_copy(v1[:, 4 * b:4 * b + 4, j, 0:MV],
                                            ps[:, X[2 * j + b], :].rearrange("p (c n) -> p c n", n=P))
                    ins.then_inc(m_v_ready, 1)

                def z_part(j):
                    dve.wait_ge(mz_tanh, 2 * p + j + 1)
                    V.scalar_tensor_tensor(gates[:, j, :], gates[:, j, :], 1.0, z_buf[:], ALU.add, ALU.mult)
                    dve.drain()
                    V.scalar_tensor_tensor(gates[:, j, :], tanh_buf[:], 1.0, gates[:, j, :], ALU.add, ALU.mult)\
                        .then_inc(mz_used, 1)

                for c in range(NB):
                    dve.wait_ge(m_decay, 8 * p + c + 1)
                    for j in range(2):
                        V.scalar_tensor_tensor(s_T[:, j, :], ps[:, X[1], j * P:(j + 1) * P], 0.25 * MK ** -0.5,
                                               dmat[:, j, :], ALU.mult, ALU.mult)
                    for j in range(2):
                        ins = V.tensor_scalar(k_w[:, j, :], ps[:, X[1], 2 * P + MK * j:2 * P + MK * (j + 1)],
                                              tok_gate[:, c, 2, j:j + 1], 0.5, ALU.mult, ALU.mult)
                    ins.then_inc(m_sT, 1)
                    dve.wait_ge(m_prod, 8 * p + c + 1)
                    num = ps[:, X[2], 0:2 * (MV + 1)]
                    h_c = h_tok[:, c].rearrange("p j n -> p (j n)")
                    new = ps[:, X[2], 2 * (MV + 1):3 * (MV + 1)]
                    if c == 0:
                        V.tensor_copy(h_c, num)
                        V.tensor_copy(state[:], new).then_inc(m_state, 1)
                    else:
                        if c < NB - 1:
                            V.scalar_tensor_tensor(state[:], state[:], pair_decay[:, c:c + 1], new, ALU.mult, ALU.add)
                        dve.wait_ge(m_inter, 7 * p + c)
                        V.tensor_tensor(h_c, num, inter[:].rearrange("p j n -> p (j n)"), ALU.add).then_inc(m_state, 1)
                    dve.drain()
                    d = h_tok[:, c, :, MV]
                    V.scalar_tensor_tensor(den[:], d, -1.0, d, ALU.mult, ALU.max)
                    dve.drain()
                    V.tensor_tensor(den[:], den[:], tok_gate[:, c, 3, :], ALU.max)
                    dve.drain()
                    V.reciprocal(den_inv[:, c, :], den[:]).then_inc(m_den, 1)
                    if c == 6:
                        z_part(0)
                z_part(1)
                dve.wait_ge(m_sumsq, p + 1)
                V.tensor_scalar(rstd[:], sumsq[:], 1.0 / MV, EPS, ALU.mult, ALU.add).then_inc(m_var, 1)
                dve.wait_ge(m_root, p + 1)
                V.reciprocal(rstd[:], rstd[:])
                dve.drain()
                V.tensor_tensor(rstd[:], rstd[:], den_inv[:].rearrange("p c j -> p (c j)"), ALU.mult)
                dve.drain()
                hv = h_tok[:].rearrange("p c j n -> p (c j) n")[:, :, 0:MV]
                V.tensor_tensor(hv, hv, rstd[:].unsqueeze(2).to_broadcast([P, 2 * NB, MV]), ALU.mult).then_inc(m_h, 1)
                dve.wait_ge(m_h_turned, p + 1)
                for j in range(2):
                    for b in range(2):
                        part = slice(b * BANK, (b + 1) * BANK)
                        ins = V.scalar_tensor_tensor(U[:, ds(j + 2 * p, 1), part].rearrange("p a n -> p (a n)"),
                                                     ps[:, X[2 * j + b], :], pair_norm[:, j:j + 1], gates[:, j, part],
                                                     ALU.mult, ALU.mult)
                ins.then_inc(u_ready, 1)

            looped(dve, PAIRS, mlstm_step)

            dve.drain()
            for k in range(KT):
                dve.wait_ge(u_hi_ready, KT + k + 1)
                V.tensor_tensor(hT_lo[:, k, :], U[:, k, :], hT_hi[:, k, :].bitcast(F32), ALU.subtract).then_inc(u_split, 1)

            def branch_m_step(i):
                for j in range(2):
                    dve.wait_ge(th_in[j], 16 * (i + 1))
                    dve.wait_ge(merged_in[j], 16 * (i + 1))
                    dve.wait_ge(tile_out, S5 + 1 + 2 * i + j)
                    V.scalar_tensor_tensor(ev[j][:], th_gm[j][:], 1.0, ev[j][:], ALU.add, ALU.mult)
                    dve.drain()
                    row = merged[:, ds(2 * i + j, 1), :].rearrange("p a n -> p (a n)")
                    V.tensor_tensor(row, row, ev[j][:], ALU.add).then_inc(merged_ready, 1)
                    row = ds(2 * i + j, 1)
                    dve.wait_ge(wo_hi_ready, 2 * i + j + 1)
                    V.tensor_tensor(wo_lo[:, row, :], wo_raw[:, row, :], wo_hi[:, row, :].bitcast(F32), ALU.subtract)\
                        .then_inc(wo_split, 1)

            looped(dve, KT // 2, branch_m_step)

            def token_tile(n, j):
                dve.wait_ge(mt_hi_ready, n + 1)
                V.tensor_tensor(mt_lo[j], merged[:, :, ds(P * n, P)], mt_hi[j].bitcast(F32), ALU.subtract).then_inc(mt_ready, 1)

            token_tile(0, 0)
            token_tile(1, 1)
            dve.wait_ge(fn_in, 16)

            def out_step(i):
                for j in range(2):
                    dve.wait_ge(x_again[j], 16 * (i + 1))
                    dve.wait_ge(tile_out, S6 + 1 + 2 * i + j)
                    V.tensor_tensor(ev[j][:], ev[j][:], th_gm[j][:], ALU.add).then_inc(res_ready, 1)
                    if not (isinstance(i, int) and i == NB // 2 - 1):
                        token_tile(2 * (i + 1) + j, j)
                    r = rstd[:, j:j + 1]
                    dve.wait_ge(res_sumsq, 2 * i + j + 1)
                    V.tensor_scalar(r, sumsq[:, j:j + 1], 1.0 / D, EPS, ALU.mult, ALU.add).then_inc(res_var, 1)
                    dve.wait_ge(res_root, 2 * i + j + 1)
                    V.reciprocal(r, r)
                    dve.drain()
                    V.scalar_tensor_tensor(ev[j][:], ev[j][:], r, fnw, ALU.mult, ALU.mult).then_inc(y_ready, 1)

            out_step(0)
            with dve.Fori(1, NB // 2 - 1) as i:
                out_step(i)
            out_step(NB // 2 - 1)


def kernel(x, norm_w, w_in, b_in, attn_sinks, conv_w, conv_b, mlstm_norm_w, w_branch_attn, w_branch_mlstm,
           w_out, final_norm_w):
    import numpy as np
    import concourse.bacc as bacc
    from concourse.bass_utils import run_bass_kernel_spmd

    ins = {"x": x[0], "norm_w": norm_w[0], "w_in": w_in[0], "b_in": b_in[0], "attn_sinks": attn_sinks[0],
           "conv_w": conv_w[0], "conv_b": conv_b[0], "mlstm_norm_w": mlstm_norm_w[0],
           "w_branch_attn": w_branch_attn[0], "w_branch_mlstm": w_branch_mlstm[0], "w_out": w_out[0],
           "final_norm_w": final_norm_w}
    nc = bacc.Bacc("TRN2", target_bir_lowering=False, num_devices=1)
    arrays, args = {}, []
    for name, a in ins.items():
        a = np.ascontiguousarray(a)
        arrays[f"in_{name}"] = a
        args.append(nc.dram_tensor(f"in_{name}", a.shape, mybir.dt.from_np(a.dtype), kind="ExternalInput").ap())
    args.append(nc.dram_tensor("out", (T, D), F32, kind="ExternalOutput").ap())
    build(nc, *args)
    r = run_bass_kernel_spmd(nc, [arrays], core_ids=[0])
    return r.results[0]["out"].reshape(1, T, D)
```

```python
import concourse.bass as bass
from concourse import mybir
from contextlib import ExitStack

F32 = mybir.dt.float32
F32R = mybir.dt.float32r
BF16 = mybir.dt.bfloat16
I8 = mybir.dt.int8
ALU = mybir.AluOpType
ACT = mybir.ActivationFunctionType
AXX = mybir.AxisListType.X
ds = bass.ds

P = 128
D = 1024
T = 1024
KT = D // P
NB = T // P
HEADS, KV, HD = 16, 4, 64
GR = HEADS // KV
MH, MK, MV = 8, 64, 128
PAIRS = MH // 2
EPS = 1e-6
NEG = -1e30
BANK = 512

Q0, K0, V0, Z0 = 0, 1024, 1280, 1536
MQ0, MK0, MV0, MI0, MF0, MO0, MZ0, GA0, GM0 = 2560, 3072, 3584, 4608, 4616, 4624, 5648, 6672, 7696
R_Q, R_K, R_V, R_Z, R_MQ, R_MK, R_MV, R_O, R_MZ, R_GA, R_GM = 0, 8, 10, 12, 20, 24, 28, 36, 44, 52, 60
R_NORM, R_MNORM, R_CONVW, R_CONVB, ROWS = 68, 76, 84, 116, 124

S1, S2, S3, S4, S5 = 0, 5, 29, 37, 77
S6 = 85
GATES = 1
TERMS = 3
MMS = 2 * KT * TERMS
COPIED = 5


def slot(t):
    return t % 2


def until(eng, sem, value):
    if isinstance(value, int) and value <= 0:
        return
    eng.wait_ge(sem, value)


def later(i):
    return not (isinstance(i, int) and i == 0)


def looped(eng, count, body):
    body(0)
    with eng.Fori(1, count) as i:
        body(i)


def build(nc, x, norm_w, w_in, b_in, sinks, conv_w, conv_b, mnorm_w, wba, wbm, w_out, fnorm_w, out):
    ctx = ExitStack()
    with ctx:
        def sb(name, shape, dt=F32, stack=None):
            return (stack or ctx).enter_context(nc.sbuf_tensor(name, shape, dt))

        def sem(name):
            return ctx.enter_context(nc.semaphore(name))

        hT_hi = sb("hT_hi", [P, KT, T], F32R)
        hT_lo = sb("hT_lo", [P, KT, T], F32R)
        w_raw = sb("w_raw", [P, 2, KT, P])
        w_hi = [sb(f"w_hi{s}", [P, KT, P], F32R) for s in range(2)]
        w_lo = [sb(f"w_lo{s}", [P, KT, P], F32R) for s in range(2)]
        ev = [sb(f"ev{s}", [P, T]) for s in range(2)]
        ident = sb("ident", [P, P])
        ident_b = sb("ident_b", [P, P], BF16)
        par = sb("par", [P, ROWS])
        par_half = sb("par_half", [P, ROWS])
        from_prev = sb("from_prev", [P, P], I8)
        cur_T = sb("cur_T", [P, P])
        prev_T = sb("prev_T", [P, P])
        causal = sb("causal", [P, P], BF16)
        ones_r = sb("ones_r", [40, P], F32R)
        head_col = sb("head_col", [40, MH])
        pair_mask = sb("pair_mask", [MH, PAIRS, NB])
        decay_rows = sb("decay_rows", [MH, PAIRS, NB])
        decay_tab = sb("decay_tab", [P, PAIRS, NB])
        gate_bias = sb("gate_bias", [40, 1])
        sink_tab = sb("sink_tab", [P, HEADS])
        zero_col = sb("zero_col", [P, 1])
        neg_col = sb("neg_col", [P, 1])
        sumsq = sb("sumsq", [P, 2 * NB])
        rstd = sb("rstd", [P, 2 * NB])
        m_before = sb("m_before", [MH, NB])
        decay = sb("decay", [MH, NB])
        row_max = sb("row_max", [P, GR])
        neg_max = sb("neg_max", [P, GR])
        sink_in = sb("sink_in", [P, GR])
        sink_exp = sb("sink_exp", [P, GR])
        row_sum = sb("row_sum", [P, GR])
        row_inv = sb("row_inv", [P, GR])
        tok_gate = sb("tok_gate", [P, NB, 4, 2])
        pair_decay = sb("pair_decay", [P, NB])
        pair_norm = sb("pair_norm", [P, 2])
        den = sb("den", [P, 2])
        den_inv = sb("den_inv", [P, NB, 2])

        def aliased(groups):
            made = []
            for g in groups:
                with ExitStack() as st:
                    made.append([sb(*a, stack=st) for a in g])
            return made

        (gate_T, c_split), (th0,) = aliased([
            [("gate_T", [P, NB, 4, MH]), ("c_split", [40, T])],
            [("th0", [P, T])]])
        ctx.enter_context(nc.sbuf_tensor("hold_gates", [P, 5, 2 * P], F32))
        (xs,), gt, (U,), (wo_hi,) = aliased([
            [("xs", [P, NB, T])],
            [(f"gt{i}", [P, T]) for i in range(7)] + [("gt_r", [P, T], F32R)],
            [("U", [P, KT, T])],
            [("wo_hi", [P, KT, T], F32R)]])
        ctx.enter_context(nc.sbuf_tensor("hold_u", [P, KT, T], F32))
        att, (u_hi, u_lo), ml, (merged, wo_lo, th1), (_, wo_raw) = aliased([
            [("k_dup", [P, KV, T]), ("v_tok", [P, NB, KV * HD]), ("k_hi", [P, T], F32R), ("k_lo", [P, T], F32R), ("v_head", [P, NB, HD]),
             ("q_split", [P, GR, T], F32R), ("silu_z", [P, 2, T]),
             ("probs0", [P, GR, P]), ("probs1", [P, GR, P]), ("pT_cur", [P, GR, P]), ("pT_prev", [P, GR, P])],
            [("u_hi", [P, KT, T], F32R), ("u_lo", [P, KT, T], F32R)],
            [("raw_q", [P, T + 3]), ("raw_k", [P, T + 3]), ("mq_pad", [P, 2, T]), ("mk_T", [P, T]),
             ("v1", [P, NB, 2, MV + 1]), ("h_tok", [P, NB, 2, MV + 1]), ("gates", [P, 2, T]), ("z_buf", [P, T]),
             ("tanh_buf", [P, T]), ("dmat", [P, 2, P]), ("s_T", [P, 2, P]), ("inter", [P, 2, MV + 1]),
             ("k_w", [P, 2, MK]), ("state", [P, MV + 1]), ("c_heads", [40, 2, T], F32R), ("junk", [P, MV])],
            [("merged", [P, KT, T]), ("wo_lo", [P, KT, T], F32R), ("th1", [P, T])],
            [("under_merged", [P, KT, T]), ("wo_raw", [P, KT, T])]])
        k_dup, v_tok, k_hi, k_lo, v_head, q_split, silu_z, probs0, probs1, pT_cur, pT_prev = att
        probs = [probs0, probs1]
        param_rows = pT_prev[:, 0, :]
        ones8 = pT_cur[0:MH, 0, :]
        parity_sel = pT_cur[0:MH, 1, :]
        (raw_q, raw_k, mq_pad, mk_T, v1, h_tok, gates, z_buf, tanh_buf, dmat, s_T, inter, k_w, state,
         c_heads, junk) = ml
        g_i, g_f, g_t1, g_t2, g_t3, g_t4, g_t5 = gt[:7]
        c_hi = gt[7]

        ps = ctx.enter_context(nc.psum_tensor("ps", [P, 8, BANK], F32))
        BANKS = [[0, 2, 4, 5, 6, 7, 1, 3], [4, 5, 1, 3, 6, 7, 4, 5]]
        FRESH = 6
        X = [4, 5, 6, 7]

        def dense_ps(t):
            return ps[:, 2 * slot(t):2 * slot(t) + 2, :].rearrange("p b n -> p (b n)")

        scr_a = nc.dram_tensor("branch_a_scratch", [KT, P, T], F32).ap()
        scr_g = nc.dram_tensor("tanh_gm_scratch", [KT, P, T], F32).ap()

        params_in = sem("params_in")
        bias_in = sem("bias_in")
        x_in = [sem(f"x_in{t}") for t in range(NB)]
        gate_slot_clear = sem("gate_slot_clear")
        w_in_sem = [sem(f"w_landed{s}") for s in range(2)]
        w_split = sem("w_split")
        tile_done = sem("tile_done")
        tile_out = sem("tile_out")
        consts_made = sem("consts_made")
        params_T = sem("params_T")
        params_ready = sem("params_ready")
        x_sumsq = sem("x_sumsq")
        x_var = sem("x_var")
        x_root = sem("x_root")
        x_norm = sem("x_norm")
        x_turned = sem("x_turned")
        hT_hi_ready = sem("hT_hi_ready")
        hT_lo_ready = sem("hT_lo_ready")
        g_parts = sem("g_parts")
        g_sum = sem("g_sum")
        g_log = sem("g_log")
        g_rows = sem("g_rows")
        g_exp = sem("g_exp")
        g_turned = sem("g_turned")
        g_ready = sem("g_ready")
        v_turned = sem("v_turned")
        v_ready = sem("v_ready")
        q_hi_ready = sem("q_hi_ready")
        q_split_ready = sem("q_split_ready")
        kv_head_ready = sem("kv_head_ready")
        scores_done = sem("scores_done")
        cur_copied = sem("cur_copied")
        max_ready = sem("max_ready")
        exp_ready = sem("exp_ready")
        probs_ready = sem("probs_ready")
        probs_turned = sem("probs_turned")
        pT_ready = sem("pT_ready")
        pv_done = sem("pv_done")
        attn_ready = sem("attn_ready")
        z_tanh = sem("z_tanh")
        z_used = sem("z_used")
        attn_gated = sem("attn_gated")
        ga_out = [sem(f"ga_out{s}") for s in range(2)]
        ga_in = [sem(f"ga_in{s}") for s in range(2)]
        u_ready = sem("u_ready")
        u_hi_ready = sem("u_hi_ready")
        u_split = sem("u_split")
        branch_a = sem("branch_a")
        branch_a_out = [sem(f"branch_a_out{s}") for s in range(2)]
        m_raw = sem("m_raw")
        m_conv = sem("m_conv")
        m_tanh = sem("m_tanh")
        m_qk = sem("m_qk")
        m_v_turned = sem("m_v_turned")
        m_v_ready = sem("m_v_ready")
        m_tabs = sem("m_tabs")
        m_scores = sem("m_scores")
        m_decay = sem("m_decay")
        m_inter = sem("m_inter")
        m_sT = sem("m_sT")
        m_prod = sem("m_prod")
        m_state = sem("m_state")
        m_den = sem("m_den")
        m_sumsq = sem("m_sumsq")
        m_var = sem("m_var")
        m_root = sem("m_root")
        m_h = sem("m_h")
        m_h_turned = sem("m_h_turned")
        mz_tanh = sem("mz_tanh")
        mz_used = sem("mz_used")
        gm_ready = sem("gm_ready")
        gm_out = [sem(f"gm_out{s}") for s in range(2)]
        wo_in = [sem(f"wo_in{s}") for s in range(2)]
        wo_hi_ready = sem("wo_hi_ready")
        wo_split = sem("wo_split")
        merged_in = [sem(f"merged_in{s}") for s in range(2)]
        th_in = [sem(f"th_in{s}") for s in range(2)]
        branch_m = sem("branch_m")
        merged_ready = sem("merged_ready")
        merged_rest = sem("merged_rest")
        h_half_used = sem("h_half_used")
        half_done = sem("half_done")
        mt_hi_ready = sem("mt_hi_ready")
        mt_ready = sem("mt_ready")
        fn_in = sem("fn_in")
        x_again = [sem(f"x_again{s}") for s in range(2)]
        res_ready = sem("res_ready")
        res_sumsq = sem("res_sumsq")
        res_var = sem("res_var")
        res_root = sem("res_root")
        y_ready = sem("y_ready")
        y_out = [sem(f"y_out{s}") for s in range(2)]

        passed = sem("passed")
        sp_passed = sem("sp_passed")

        mt_hi = [w_hi[slot(S6 + s)][:] for s in range(2)]
        mt_lo = [w_lo[slot(S6 + s)][:] for s in range(2)]
        th_gm = [th0, th1]
        fnw = w_raw[:, 0].rearrange("p k n -> p (k n)")
        squares = w_raw[:, 1].rearrange("p k n -> p (k n)")

        both_blocks = ps[:, X[0]:X[1] + 1, :].rearrange("p b (h w n) -> p (b h) w n", h=2, w=2)

        block = ctx.enter_context(nc.Block())

        w_cols = w_in.rearrange("(k p) n -> p k n", p=P)
        wba_cols = wba.rearrange("(k p) n -> p k n", p=P)
        wbm_cols = wbm.rearrange("(k p) n -> p k n", p=P)
        x_rows = x.rearrange("(t p) d -> p t d", p=P)
        wo_rows = w_out.rearrange("(k p) n -> p k n", p=P)
        out_rows = out.rearrange("(t p) d -> p t d", p=P)

        @block.sync
        def _(sp):
            for t in range(4):
                sp.dma_start(xs[:, t, :], x_rows[:, t, :]).then_inc(x_in[t], 16)
            for row, src in ((R_Q, b_in[0:MI0]), (R_O, b_in[MO0:GM0 + D]), (R_NORM, norm_w),
                             (R_MNORM, mnorm_w), (R_CONVB, conv_b)):
                rows = src.shape[0] // P
                sp.dma_start(param_rows[row:row + rows, :], src.rearrange("(r n) -> r n", n=P)).then_inc(params_in, 16)
            sp.dma_start(param_rows[R_CONVW:R_CONVW + 32, :],
                          conv_w.rearrange("j (r n) -> (j r) n", n=P)).then_inc(params_in, 16)
            sp.dma_start(w_raw[:, slot(0)], w_cols[:, :, K0:K0 + P]).then_inc(w_in_sem[slot(0)], 16)
            sp.wait_ge(gate_slot_clear, 1)
            sp.dma_start(w_raw[:, slot(GATES), :, 0:8], w_cols[:, :, MI0:MF0]).then_inc(w_in_sem[slot(GATES)], 16)
            sp.dma_start(w_raw[:, slot(GATES), :, 32:40], w_cols[:, :, MF0:MO0]).then_inc(w_in_sem[slot(GATES)], 16)
            for t in range(4, NB):
                sp.dma_start(xs[:, t, :], x_rows[:, t, :]).then_inc(x_in[t], 16)
            sp.dma_start(gate_bias[0:8, :], b_in[MI0:MF0].rearrange("(h a) -> h a", a=1)).then_inc(bias_in, 16)
            sp.dma_start(gate_bias[32:40, :], b_in[MF0:MO0].rearrange("(h a) -> h a", a=1)).then_inc(bias_in, 16)
            sp.dma_start(sink_tab[:, :], sinks.partition_broadcast(P)).then_inc(bias_in, 16)

            def weights(t0, tiles):
                cols = [c if isinstance(c, int) else sp.snap(c) for _, _, c in tiles]
                need = [n if isinstance(n, int) else sp.snap(n) for n in (t0 + j - 1 for j, _, _ in tiles)]
                for (j, src, _), c, n in zip(tiles, cols, need):
                    until(sp, w_split, n)
                    sp.sem_inc(sp_passed, 1)
                    s = slot(S2 + j)
                    sp.dma_start(w_raw[:, s], src[:, :, ds(c, P)]).then_inc(w_in_sem[s], 16)

            for t, c in ((2, K0 + P), (3, V0), (4, V0 + P)):
                until(sp, w_split, t - 1)
                sp.dma_start(w_raw[:, slot(t)], w_cols[:, :, c:c + P]).then_inc(w_in_sem[slot(t)], 16)

            looped(sp, KV, lambda g: weights(S2 + 6 * g, [
                (0, w_cols, Q0 + 2 * P * g), (1, w_cols, Q0 + P + 2 * P * g),
                (2, w_cols, Z0 + 2 * P * g), (3, w_cols, Z0 + P + 2 * P * g),
                (4, w_cols, GA0 + 2 * P * g), (5, w_cols, GA0 + P + 2 * P * g)]))

            looped(sp, KT // 2, lambda i: weights(S3 + 2 * i, [
                (0, wba_cols, 2 * P * i), (1, wba_cols, P + 2 * P * i)]))

            looped(sp, PAIRS, lambda p: weights(S4 + 10 * p, [
                (0, w_cols, MQ0 + P * p), (1, w_cols, MK0 + P * p),
                (2, w_cols, MV0 + 2 * P * p), (3, w_cols, MV0 + P + 2 * P * p),
                (4, w_cols, MO0 + 2 * P * p), (5, w_cols, MO0 + P + 2 * P * p),
                (6, w_cols, MZ0 + 2 * P * p), (7, w_cols, MZ0 + P + 2 * P * p),
                (8, w_cols, GM0 + 2 * P * p), (9, w_cols, GM0 + P + 2 * P * p)]))

            def branch_m_step(i):
                weights(S5 + 2 * i, [(0, wbm_cols, 2 * P * i), (1, wbm_cols, P + 2 * P * i)])
                if not later(i):
                    sp.wait_ge(u_split, KT + 1)
                    for s in range(2):
                        sp.wait_ge(branch_a_out[s], 16 * (KT // 2))
                rows = [2 * i + j if isinstance(i, int) else sp.snap(2 * i + j) for j in range(2)]
                stored = 16 if isinstance(i, int) else sp.snap(16 * i + 16)
                used = [2 * i + j - 1 if isinstance(i, int) else sp.snap(2 * i + j - 1) for j in range(2)]
                for j in range(2):
                    if later(i):
                        sp.wait_ge(wo_split, used[j])
                    sp.wait_ge(gm_out[j], stored)
                    sp.dma_start(th_gm[j][:], scr_g[ds(rows[j], 1)].rearrange("a p n -> p (a n)")).then_inc(th_in[j], 16)
                    row = ds(rows[j], 1)
                    sp.dma_start(merged[:, row, :], scr_a[row].rearrange("a p n -> p a n")).then_inc(merged_in[j], 16)
                    sp.dma_start(wo_raw[:, row, :], wo_rows[:, row, :]).then_inc(wo_in[j], 16)

            looped(sp, KT // 2, branch_m_step)
            sp.wait_ge(w_split, S6)
            sp.dma_start(fnw, fnorm_w.partition_broadcast(P)).then_inc(fn_in, 16)

            sp.wait_ge(merged_rest, 1)
            for j in range(2):
                sp.dma_start(th_gm[j][:], x_rows[:, j, :]).then_inc(x_again[j], 16)

            def out_step(i):
                last = isinstance(i, int) and i == NB // 2 - 1
                value = lambda v: v if isinstance(v, int) else sp.snap(v)
                done = [value(2 * i + j + 1) for j in range(2)]
                summed = [value(4 * i + 2 * j + 2) for j in range(2)]
                rows = [value(2 * i + j) for j in range(2)]
                ahead = [value(2 * i + j + 2) for j in range(2)]
                if not last:
                    for j in range(2):
                        sp.wait_ge(res_ready, summed[j])
                        sp.dma_start(th_gm[j][:], x_rows[:, ds(ahead[j], 1), :].rearrange("p a n -> p (a n)"))\
                            .then_inc(x_again[j], 16)
                for j in range(2):
                    sp.wait_ge(y_ready, done[j])
                    part = slice(0, BANK) if last and j == 1 else slice(0, D)
                    sp.dma_start(out_rows[:, ds(rows[j], 1), part].rearrange("p a n -> p (a n)"), ev[j][:, part])\
                        .then_inc(y_out[j], 16)
                if last:
                    sp.wait_ge(y_ready, NB + 1)
                    sp.dma_start(out_rows[:, NB - 1, BANK:D], ev[1][:, BANK:D]).then_inc(y_out[1], 16)

            out_step(0)
            with sp.Fori(1, NB // 2 - 1) as i:
                out_step(i)
            out_step(NB // 2 - 1)

            for s in range(2):
                sp.wait_ge(gm_out[s], 16 * PAIRS)
                sp.wait_ge(y_out[s], 16 * (NB // 2 + s))
                sp.wait_ge(ga_out[s], 16 * KV)
                sp.wait_ge(branch_a_out[s], 16 * (KT // 2))

        @block.gpsimd
        def _(pool):
            gate_raw = w_raw[:, slot(GATES), :, 0:P // 2]
            nc.gpsimd.memset(sumsq[:], 0.0)
            nc.gpsimd.memset(gate_raw, 0.0).then_inc(gate_slot_clear, 1)

            def triangle(dst, inside, outside, base, free_step, chan):
                nc.gpsimd.memset(dst, inside)
                pool.drain()
                nc.gpsimd.affine_select(out=dst, in_=dst, compare_op=ALU.is_ge, fill=outside, base=base,
                                        pattern=[[free_step, P]], channel_multiplier=chan)

            nc.gpsimd.memset(ident[:], 0.0)
            nc.gpsimd.memset(zero_col[:], 0.0)
            nc.gpsimd.memset(neg_col[:], NEG)
            pool.drain()
            nc.gpsimd.affine_select(out=ident[:], in_=ident[:], compare_op=ALU.not_equal, fill=1.0, base=0,
                                    pattern=[[-1, P]], channel_multiplier=1)
            triangle(from_prev[:], 1.0, 0.0, -1, 1, -1)
            triangle(cur_T[:], 1.0, 0.0, 0, 1, -1)
            triangle(prev_T[:], 1.0, 0.0, -1, -1, 1)
            triangle(causal[:], 0.0, NEG, 0, 1, -1)
            nc.gpsimd.tensor_copy(ident_b[:], ident[:])
            nc.gpsimd.memset(ones_r[:].bitcast(F32), 1.0)
            nc.gpsimd.memset(ones8, 1.0)
            nc.gpsimd.memset(head_col[:], 0.0)
            nc.gpsimd.memset(parity_sel, 0.0)
            nc.gpsimd.memset(pair_mask[:], 1.0)
            pool.drain()
            for first in (0, 32):
                nc.gpsimd.affine_select(out=head_col[:], in_=head_col[:], compare_op=ALU.not_equal, fill=1.0,
                                        base=-first, pattern=[[-1, MH]], channel_multiplier=1)
                pool.drain()
            for q in range(PAIRS):
                v = parity_sel.rearrange("h (r m) -> h r m", r=2)
                nc.gpsimd.affine_select(out=v, in_=v, compare_op=ALU.not_equal, fill=1.0, base=-2 * q,
                                        pattern=[[-1, 2], [0, MK]], channel_multiplier=1)
                pool.drain()
            nc.gpsimd.affine_select(out=pair_mask[:], in_=pair_mask[:], compare_op=ALU.is_ge, fill=0.0, base=0,
                                    pattern=[[-2, PAIRS], [0, NB]], channel_multiplier=1)
            pool.drain()
            nc.gpsimd.affine_select(out=pair_mask[:], in_=pair_mask[:], compare_op=ALU.is_ge, fill=0.0, base=1,
                                    pattern=[[2, PAIRS], [0, NB]], channel_multiplier=-1).then_inc(consts_made, 1)

            def split(src, hi, lo):
                nc.gpsimd.tensor_tensor(hi, src, zero_col[:].to_broadcast(list(src.shape)), ALU.add)
                pool.drain()
                nc.gpsimd.tensor_tensor(lo, src, hi.bitcast(F32), ALU.subtract).then_inc(w_split, 1)

            def landed(t):
                return 16 * (t // 2 + 1) + (16 if t >= GATES and slot(t) == slot(GATES) else 0)

            def flat(a):
                return a.rearrange("p k n -> p (k n)")

            def split_tiles(first, i, per):
                for j in range(per):
                    s, t = slot(first + j), first + per * i + j
                    pool.wait_ge(w_in_sem[s], landed(first + j) + 8 * per * i)
                    until(pool, tile_done, t - 1)
                    if isinstance(t, int) and t == GATES:
                        split(gate_raw, w_hi[s][:, :, 0:P // 2], w_hi[s][:, :, P // 2:P])
                    else:
                        split(flat(w_raw[:, s]), flat(w_hi[s][:]), flat(w_lo[s][:]))

            for t in range(S1, S2):
                split_tiles(t, 0, 1)
            looped(pool, KV, lambda g: split_tiles(S2, g, 6))
            looped(pool, KT // 2, lambda i: split_tiles(S3, i, 2))
            looped(pool, PAIRS, lambda p: split_tiles(S4, p, 10))
            looped(pool, KT // 2, lambda i: split_tiles(S5, i, 2))

        @block.tensor
        def _(pe):
            def dense(t, s, lo, hi, rhs_hi=hT_hi, rhs_lo=hT_lo, gate=None, halves=False, half_way=None):
                for m in range(lo, hi):
                    b, r = divmod(m, KT * TERMS)
                    k, term = divmod(r, TERMS)
                    if m == 0:
                        until(pe, w_split, t + 1)
                        until(pe, tile_out, t - 1)
                    if gate is not None and term == 0 and (b == 0 or halves):
                        pe.wait_ge(gate, gate_from + KT * b + k + 1)
                    w = (w_hi, w_hi, w_lo)[term][s]
                    r_ = (rhs_hi, rhs_lo, rhs_hi)[term]
                    mm = nc.tensor.matmul(ps[:, 2 * s + b, :], w[:, k, :], r_[:, k, b * BANK:(b + 1) * BANK],
                                          start=(r == 0), stop=(r == KT * TERMS - 1))
                    if half_way is not None and m == MMS // 2 - 1:
                        mm.then_inc(half_way, 1)
                if hi == MMS:
                    mm.then_inc(tile_done, 1)

            gate_from = 0

            pe.wait_ge(consts_made, 1)
            pe.wait_ge(params_in, 16 * 6)
            nc.tensor.transpose(ps[:, X[3], 0:ROWS], param_rows[0:ROWS, :], ident[0:ROWS, 0:ROWS]).then_inc(params_T, 1)
            def turn(t, k):
                banks = BANKS[t // 4]
                mm = nc.tensor.transpose(ps[:, banks[k], (t % 4) * P:(t % 4 + 1) * P],
                                         xs[:, t, k * P:(k + 1) * P], ident[:])
                if t % 4 == 3:
                    mm.then_inc(x_turned, 1)

            def turn_tile(t, features):
                pe.wait_ge(x_norm, t + 1)
                table = BANKS[0].index(X[3])
                for k in [k for k in range(features) if t or k != table]:
                    turn(t, k)
                if t == 0:
                    pe.wait_ge(params_ready, 1)
                    turn(t, table)

            for t in range(4):
                turn_tile(t, KT)
            def gate_tile(b, lo, hi):
                if b == 0 and lo == 0:
                    pe.wait_ge(w_split, GATES + 1)
                for m in range(lo, hi):
                    mm = nc.tensor.matmul(ps[:, 2 * slot(GATES) + b, :], w_hi[slot(GATES)][:, m // 2, :],
                                          (hT_hi, hT_lo)[m % 2][:, m // 2, b * BANK:(b + 1) * BANK],
                                          start=(m == 0), stop=(m == 2 * KT - 1))
                if b == 1 and hi == 2 * KT:
                    mm.then_inc(tile_done, 1)

            dense(0, 0, 0, MMS // 2, gate=hT_lo_ready)
            gate_tile(0, 0, 6)
            pe.wait_ge(hT_lo_ready, KT)
            turn_tile(4, FRESH)
            turn_tile(5, FRESH)
            gate_tile(0, 6, 10)
            turn_tile(6, FRESH)
            turn_tile(7, FRESH)
            gate_tile(0, 10, 2 * KT)
            for k in range(FRESH, KT):
                pe.wait_ge(hT_lo_ready, KT + BANKS[1].index(BANKS[1][k]) + 1)
                for t in range(4, NB):
                    turn(t, k)
            pe.wait_ge(hT_lo_ready, KT + BANKS[1].index(1) + 1)
            dense(0, 0, MMS // 2, MMS, gate=hT_lo_ready, halves=True)
            gate_tile(1, 0, 2 * KT)
            for t in range(2, S2):
                dense(t, slot(t), 0, MMS)

            def turn_gates():
                pe.wait_ge(g_exp, 1)
                pe.wait_ge(v_ready, 2)
                for c in range(NB):
                    nc.tensor.transpose(ps[:, X[c // 4], (c % 4) * P:(c % 4 + 1) * P],
                                        g_t4[:, c * P:(c + 1) * P], ident[:])
                nc.tensor.matmul(ps[:, X[2], 0:PAIRS * NB], parity_sel,
                                 decay_rows[:].rearrange("h a b -> h (a b)"), start=True, stop=True)\
                    .then_inc(g_turned, 1)

            def turn_attention_v(n):
                pe.wait_ge(tile_out, 4 + n)
                for c in range(NB):
                    mm = nc.tensor.transpose(ps[:, X[2 * n + c // 4], (c % 4) * P:(c % 4 + 1) * P],
                                             ev[1 - n][:, c * P:(c + 1) * P], ident[:])
                mm.then_inc(v_turned, 1)

            turn_attention_v(0)


            def scores(n):
                first = max(n - 1, 0)
                for h in range(GR):
                    o = ps[:, X[h // 2], (h % 2) * 2 * P + (P if n == 0 else 0):(h % 2 + 1) * 2 * P]
                    for part in (k_hi, k_lo):
                        mm = nc.tensor.matmul(o, q_split[:, h, n * P:(n + 1) * P], part[:, first * P:(n + 1) * P],
                                              start=(part is k_hi), stop=(part is k_lo))
                return mm

            def attention_step(g):
                t0 = S2 + 6 * g
                dense(t0, 1, 0, MMS)
                if not later(g):
                    turn_attention_v(1)
                dense(t0 + 1, 0, 0, MMS // 2)
                if not later(g):
                    turn_gates()
                dense(t0 + 1, 0, MMS // 2, MMS)
                done = [0]

                def more(hi):
                    lo = done[0]
                    for j in range(4):
                        a, b = max(lo, j * MMS), min(hi, (j + 1) * MMS)
                        if a < b:
                            dense(t0 + 2 + j, slot(S2 + j), a - j * MMS, b - j * MMS)
                    done[0] = hi

                more(lead)
                for n in range(NB + 2):
                    if n < NB:
                        if n == 0:
                            pe.wait_ge(kv_head_ready, g + 1)
                            pe.wait_ge(tile_out, t0 + 2)
                            if not later(g):
                                pe.wait_ge(g_ready, 1)
                        else:
                            pe.wait_ge(cur_copied, NB * g + n)
                            pe.wait_ge(max_ready, NB * g + n)
                        scores(n).then_inc(scores_done, 1)
                    if n <= NB:
                        more(lead + (4 * MMS - lead - tail) * (2 * n + 1) // (2 * NB + 2))
                    if n >= 2:
                        m = n - 2
                        pe.wait_ge(pT_ready, NB * g + m + 1)
                        if 1 <= m <= COPIED:
                            pe.wait_ge(attn_ready, COPIED * g + m)
                        if m > COPIED:
                            pe.wait_ge(attn_gated, (NB - 1 - COPIED) * g + m - COPIED)
                        for r in range(2):
                            o = ps[64 * r:64 * r + 64, X[3], 0:2 * P]
                            mm = nc.tensor.matmul(o, v_head[:, m, :], pT_cur[:, r:GR:2, :], start=True, stop=(m == 0))
                            if m:
                                mm = nc.tensor.matmul(o, v_head[:, m - 1, :], pT_prev[:, r:GR:2, :], start=False, stop=True)
                        mm.then_inc(pv_done, 1)
                    if 1 <= n <= NB:
                        pe.wait_ge(probs_ready, NB * g + n)
                        for h in range(GR):
                            mm = nc.tensor.transpose(ps[:, X[2], h * P:(h + 1) * P], probs[(n - 1) % 2][:, h, :], ident[:])
                        mm.then_inc(probs_turned, 1)
                    if n <= NB:
                        more(lead + (4 * MMS - lead - tail) * (n + 1) // (NB + 1))
                more(4 * MMS)

            lead = 18
            tail = 24
            looped(pe, KV, attention_step)

            def branch_a_step(i):
                for j in range(2):
                    dense(S3 + j + 2 * i, slot(S3 + j), 0, MMS, u_hi, u_lo, gate=u_split if j == 0 else None)

            looped(pe, KT // 2, branch_a_step)

            def mlstm_step(p):
                t0 = S4 + 10 * p
                for j in range(4):
                    dense(t0 + j, slot(S4 + j), 0, MMS)
                done = [0]

                def more(hi):
                    lo = done[0]
                    for j in range(6):
                        a, b = max(lo, j * MMS), min(hi, (j + 1) * MMS)
                        if a < b:
                            dense(t0 + 4 + j, slot(S4 + j), a - j * MMS, b - j * MMS, half_way=h_half_used if j == 5 else None)
                    done[0] = hi

                def turn_v(j):
                    pe.wait_ge(tile_out, t0 + 3 + j)
                    for c in range(NB):
                        mm = nc.tensor.transpose(ps[:, X[2 * j + c // 4], (c % 4) * P:(c % 4 + 1) * P],
                                                 ev[j][:, c * P:(c + 1) * P], ident[:])
                    mm.then_inc(m_v_turned, 1)

                if later(p):
                    pe.wait_ge(u_ready, KV + p)
                turn_v(0)
                more(12)
                turn_v(1)
                more(24)
                pe.wait_ge(m_qk, 2 * (p + 1))
                pe.wait_ge(m_tabs, p + 1)
                pe.wait_ge(m_v_ready, 2 * (p + 1))
                each = (5 * MMS - 24) // (2 * NB)
                for c in range(NB):
                    tok = slice(c * P, (c + 1) * P)
                    if c:
                        pe.wait_ge(m_inter, 7 * p + c - 1) if c > 1 else None
                        pe.wait_ge(m_decay, 8 * p + c)
                        pe.wait_ge(m_state, 8 * p + c)
                    nc.tensor.matmul(ps[:, X[0], 0:2 * P], ones_r[:], c_heads[:, :, tok], start=True, stop=False)
                    nc.tensor.matmul(ps[:, X[0], 0:2 * P], ident_b[:],
                                     causal[:].unsqueeze(1).to_broadcast([P, 2, P]), start=False, stop=True)
                    nc.tensor.matmul(ps[:, X[1], 0:2 * P], mk_T[:, tok], mq_pad[:, :, tok], start=True, stop=True)
                    mm = nc.tensor.transpose(ps[:, X[1], 2 * P:3 * P], mk_T[:, tok], ident[:])
                    if c:
                        for j in range(2):
                            mm = nc.tensor.matmul(ps[:, X[3], j * (MV + 1):(j + 1) * (MV + 1)], mq_pad[:, j, tok],
                                                  state[:], start=True, stop=True)
                    mm.then_inc(m_scores, 1)
                    more(24 + each * (2 * c + 1))
                    pe.wait_ge(m_sT, 8 * p + c + 1)
                    for j in range(2):
                        mm = nc.tensor.matmul(ps[:, X[2], j * (MV + 1):(j + 1) * (MV + 1)], s_T[:, j, :], v1[:, c, j, :],
                                              start=True, stop=True)
                    if c < NB - 1:
                        for j in range(2):
                            mm = nc.tensor.matmul(ps[64 * j:64 * j + 64, X[2], 2 * (MV + 1):3 * (MV + 1)], k_w[:, j, :],
                                                  v1[:, c, j, :], start=True, stop=True)
                    mm.then_inc(m_prod, 1)
                    more(24 + each * (2 * c + 2))
                more(6 * MMS - 14)
                pe.wait_ge(m_h, p + 1)
                for j in range(2):
                    for c in range(NB):
                        mm = nc.tensor.transpose(ps[:, X[2 * j + c // 4], (c % 4) * P:(c % 4 + 1) * P],
                                                 h_tok[:, c, j, 0:MV], ident[:])
                mm.then_inc(m_h_turned, 1)
                more(6 * MMS)

            looped(pe, PAIRS, mlstm_step)

            gate_from = KT

            def branch_m_step(i):
                dense(S5 + 2 * i, 1, 0, MMS, gate=u_split, halves=True)
                dense(S5 + 1 + 2 * i, 0, 0, MMS)

            looped(pe, KT // 2, branch_m_step)

            pe.wait_ge(wo_split, KT)

            def out_step(i):
                for j in range(2):
                    s = slot(S6 + j)
                    first = not later(i) and j == 0
                    if first:
                        pe.wait_ge(mt_ready, 1)
                        orders = [(0, KT - 1), (KT - 1, KT)]
                    else:
                        pe.wait_ge(mt_hi_ready, 2 * i + j + 2)
                        orders = [(0, KT)]
                    pe.wait_ge(tile_out, S6 - 1 + 2 * i + j)
                    for b in range(2):
                        o = ps[:, 2 * s + b, :]
                        part = slice(b * BANK, (b + 1) * BANK)
                        for lo, hi in orders:
                            if first and b == 0 and lo:
                                pe.wait_ge(mt_ready, 2)
                            for k in range(lo, hi):
                                nc.tensor.matmul(o, mt_hi[j][:, k, :], wo_hi[:, k, part], start=(k == 0), stop=False)
                                nc.tensor.matmul(o, mt_hi[j][:, k, :], wo_lo[:, k, part], start=False, stop=False)
                            if not first and b == 0:
                                pe.wait_ge(mt_ready, 2 * i + j + 2)
                            for k in range(lo, hi):
                                mm = nc.tensor.matmul(o, mt_lo[j][:, k, :], wo_hi[:, k, part], start=False, stop=(k == KT - 1))
                        mm.then_inc(half_done if b == 0 else tile_done, 1)

            looped(pe, NB // 2, out_step)

        @block.scalar
        def _(act):
            A = nc.scalar.activation

            def squares_of(t):
                act.wait_ge(x_in[t], 16)
                act.drain()
                A(ev[0][:], xs[:, t, :], ACT.Square, accum_out=sumsq[:, t:t + 1]).then_inc(x_sumsq, 1)

            def root(t):
                act.wait_ge(x_var, t + 1)
                A(rstd[:, t:t + 1], rstd[:, t:t + 1], ACT.Sqrt).then_inc(x_root, 1)

            def squares_and_roots(half):
                for t in range(4 * half, 4 * half + 4):
                    squares_of(t)
                    if t % 4:
                        root(t - 1)
                    if t == 2:
                        act.wait_ge(params_T, 1)
                        A(par[:], ps[:, X[3], 0:ROWS], ACT.Copy)
                        A(par_half[:], ps[:, X[3], 0:ROWS], ACT.Copy, scale=0.5).then_inc(params_ready, 1)
                root(4 * half + 3)

            def high_parts(half):
                for k in range(KT):
                    act.wait_ge(x_turned, KT * half + k + 1)
                    A(hT_hi[:, k, half * BANK:(half + 1) * BANK], ps[:, BANKS[half][k], :], ACT.Copy,
                      scale=par[:, R_NORM + k:R_NORM + k + 1]).then_inc(hT_hi_ready, 1)

            act.wait_ge(gate_slot_clear, 1)
            A(rstd[:, 0:1], sumsq[:, 0:1], ACT.Sqrt)
            for half in range(2):
                squares_and_roots(half)
                high_parts(half)

            def k_tile(t):
                act.wait_ge(tile_done, t + 1)
                for half in range(2):
                    for r in range(2):
                        ins = A(k_dup[64 * r:64 * r + 64, t + half, :], dense_ps(t)[64 * half:64 * half + 64, :],
                                ACT.Identity, bias=par[64 * half:64 * half + 64, R_K + t // 2:R_K + t // 2 + 1])
                ins.then_inc(tile_out, 1)

            k_tile(0)
            act.wait_ge(tile_done, GATES + 1)
            act.wait_ge(bias_in, 16 * 3)
            A(g_i[0:8, :], dense_ps(GATES)[0:8, :], ACT.Identity, bias=gate_bias[0:8, :])
            A(g_f[0:8, :], dense_ps(GATES)[32:40, :], ACT.Identity, bias=gate_bias[32:40, :]).then_inc(g_parts, 1)
            act.wait_ge(g_sum, 1)
            act.sem_inc(tile_out, 1)
            A(g_t1[0:8, :], g_f[0:8, :], ACT.Abs)
            act.drain()
            A(g_t1[0:8, :], g_t1[0:8, :], ACT.Exp, scale=-1.0)
            act.drain()
            A(g_t1[0:8, :], g_t1[0:8, :], ACT.Ln, bias=1.0).then_inc(g_log, 1)
            k_tile(2)
            act.wait_ge(g_rows, 1)
            A(g_t4[32:40, :], g_f[0:8, :], ACT.Exp)
            A(g_t4[64:72, :], g_t2[0:8, :], ACT.Exp)
            A(g_t4[96:104, :], g_t3[0:8, :], ACT.Exp, scale=-1.0)
            A(decay[:], g_f[0:8, :].rearrange("h (c n) -> h c n", n=P)[:, :, P - 1], ACT.Exp)
            act.drain()
            for q in range(PAIRS):
                ins = A(decay_rows[:, q, :], decay[:], ACT.Copy, scale=pair_mask[:, q, 0:1])
            ins.then_inc(g_exp, 1)
            for t in (3, 4):
                act.wait_ge(tile_done, t + 1)
                A(ev[t % 2][:], dense_ps(t), ACT.Identity, bias=par[:, R_V + t - 3:R_V + t - 2]).then_inc(tile_out, 1)

            def gate_tables():
                act.wait_ge(g_turned, 1)
                for b in range(2):
                    for c in range(4):
                        A(gate_T[:, 4 * b + c],
                          ps[:, X[b], c * P:(c + 1) * P].rearrange("p (q h) -> p q h", h=32)[:, :, 0:MH], ACT.Copy)
                A(decay_tab[:].rearrange("p a b -> p (a b)"), ps[:, X[2], 0:PAIRS * NB], ACT.Copy).then_inc(g_ready, 1)

            def ga_tile(g, j):
                act.wait_ge(tile_done, S2 + 5 + j + 6 * g)
                act.wait_ge(z_used, 2 * g + j + 1)
                A(ev[j][:], dense_ps(S2 + j), ACT.Tanh, scale=0.5, bias=par_half[:, ds(R_GA + j + 2 * g, 1)])\
                    .then_inc(tile_out, 1)
                act.drain()
                act.dma_start(scr_a[ds(2 * g + j, 1)].rearrange("a p n -> p (a n)"), ev[j][:]).then_inc(ga_out[j], 16)

            def attention_step(g):
                t0 = S2 + 6 * g
                if later(g):
                    ga_tile(g - 1, 1)
                for j in range(2):
                    act.wait_ge(tile_done, t0 + 1 + j)
                    for r in range(2):
                        rows = slice(64 * r, 64 * r + 64)
                        A(q_split[0:64, 2 * j + r, :], dense_ps(S2 + j)[rows, :], ACT.Identity,
                          bias=par[rows, ds(R_Q + j + 2 * g, 1)]).then_inc(q_hi_ready, 1)
                    act.wait_ge(q_split_ready, GR * g + 2 * j + 2)
                    act.sem_inc(tile_out, 1)
                    if not later(g) and j == 0:
                        gate_tables()

                def z_tile(j):
                    act.wait_ge(tile_done, t0 + 3 + j)
                    if later(g):
                        act.wait_ge(u_ready, g)
                        act.wait_ge(ga_out[j], 16 * g)
                    else:
                        act.wait_ge(v_turned, 2)
                    A(silu_z[:, j, :], dense_ps(S2 + j), ACT.Identity, bias=par[:, ds(R_Z + j + 2 * g, 1)]).then_inc(tile_out, 1)

                def tanh_z(j):
                    act.drain()
                    A(ev[j][:], silu_z[:, j, :], ACT.Tanh, scale=0.5).then_inc(z_tanh, 1)

                for n in range(NB + 2):
                    if n < NB:
                        pr = probs[n % 2]
                        act.wait_ge(scores_done, NB * g + n + 1)
                        if n >= 2:
                            act.wait_ge(probs_turned, NB * g + n - 1)
                        A(pr[:], both_blocks[:, :, 1, :], ACT.Copy).then_inc(cur_copied, 1)
                        act.wait_ge(max_ready, NB * g + n + 1)
                        for h in range(GR):
                            A(pr[:, h, :], pr[:, h, :], ACT.Exp, scale=HD ** -0.5, bias=neg_max[:, h:h + 1],
                              accum_out=row_sum[:, h:h + 1])
                        A(sink_exp[:], sink_in[:], ACT.Exp).then_inc(exp_ready, 1)
                    if 2 <= n < COPIED + 2:
                        m = n - 2
                        act.wait_ge(pv_done, NB * g + m + 1)
                        A(U[:, ds(2 * g, 2), m * P:(m + 1) * P], ps[:, X[3], 0:2 * P].rearrange("p (j n) -> p j n", j=2),
                          ACT.Copy).then_inc(attn_ready, 1)
                    if n in (2, 5):
                        z_tile(n // 3)
                    if n in (3, 6):
                        tanh_z(n // 3 - 1)
                ga_tile(g, 0)

            looped(act, KV, attention_step)

            act.wait_ge(pv_done, KV * NB)
            for k in range(KT):
                if k % 2 == 0:
                    act.wait_ge(u_ready, k // 2 + 1)
                A(u_hi[:, k, :], U[:, k, :], ACT.Copy).then_inc(u_hi_ready, 1)
            ga_tile(KV - 1, 1)

            def branch_a_step(i):
                for j in range(2):
                    if later(i):
                        act.wait_ge(branch_a_out[j], 16 * i)
                    else:
                        act.wait_ge(ga_out[j], 16 * KV)
                    act.dma_start(ev[j][:], scr_a[ds(2 * i + j, 1)].rearrange("a p n -> p (a n)")).then_inc(ga_in[j], 16)
                for j in range(2):
                    act.wait_ge(branch_a, 2 * i + j + 1)
                    act.sem_inc(tile_out, 1)
                    act.dma_start(scr_a[ds(2 * i + j, 1)].rearrange("a p n -> p (a n)"), ev[j][:])\
                        .then_inc(branch_a_out[j], 16)

            looped(act, KT // 2, branch_a_step)

            def gm_tile(p, j):
                act.wait_ge(tile_done, S4 + 9 + j + 10 * p)
                act.wait_ge(m_v_turned, 2 * p + 1 + j)
                A(ev[j][:], dense_ps(S4 + j), ACT.Tanh, scale=0.5,
                  bias=par_half[:, ds(R_GM + j + 2 * p, 1)]).then_inc(tile_out, 1)
                act.drain()
                act.dma_start(scr_g[ds(2 * p + j, 1)].rearrange("a p n -> p (a n)"), ev[j][:]).then_inc(gm_out[j], 16)

            def mlstm_step(p):
                t0 = S4 + 10 * p
                if later(p):
                    gm_tile(p - 1, 1)
                for j, (raw, row) in enumerate(((raw_q, R_MQ), (raw_k, R_MK))):
                    act.wait_ge(tile_done, t0 + 1 + j)
                    A(raw[:, 3:], dense_ps(S4 + j), ACT.Identity, bias=par[:, ds(row + p, 1)]).then_inc(tile_out, 1)
                act.wait_ge(m_conv, 2 * p + 1)
                if later(p):
                    act.wait_ge(mz_used, 2 * p)
                A(tanh_buf[:], z_buf[:], ACT.Tanh, scale=0.5).then_inc(m_tanh, 1)

                def v_tile(j):
                    act.wait_ge(tile_done, t0 + 3 + j)
                    if not later(p):
                        act.wait_ge(branch_a_out[j], 16 * (KT // 2))
                    else:
                        act.wait_ge(gm_out[j], 16 * p)
                    A(ev[j][:], dense_ps(S4 + j), ACT.Identity, bias=par[:, ds(R_MV + j + 2 * p, 1)]).then_inc(tile_out, 1)

                v_tile(0)
                act.wait_ge(m_conv, 2 * p + 2)
                act.wait_ge(m_qk, 2 * p + 1)
                A(tanh_buf[:], mk_T[:], ACT.Tanh, scale=0.5).then_inc(m_tanh, 1)
                v_tile(1)

                def o_tile(j):
                    act.wait_ge(tile_done, t0 + 5 + j)
                    if later(p):
                        act.wait_ge(u_ready, KV + p)
                    A(gates[:, j, :], dense_ps(S4 + j), ACT.Tanh, scale=0.5,
                      bias=par_half[:, ds(R_O + j + 2 * p, 1)]).then_inc(tile_out, 1)

                def z_tile(j):
                    act.wait_ge(tile_done, t0 + 7 + j)
                    if j == 0:
                        act.wait_ge(m_qk, 2 * p + 2)
                    else:
                        act.wait_ge(mz_used, 2 * p + 1)
                    A(z_buf[:], dense_ps(S4 + j), ACT.Identity, bias=par[:, ds(R_MZ + j + 2 * p, 1)]).then_inc(tile_out, 1)
                    act.drain()
                    A(tanh_buf[:], z_buf[:], ACT.Tanh, scale=0.5).then_inc(mz_tanh, 1)

                def sum_squares(c):
                    act.drain()
                    act.wait_ge(m_den, 8 * p + c + 1)
                    for j in range(2):
                        if j:
                            act.drain()
                        ins = A(junk[:], h_tok[:, c, j, 0:MV], ACT.Square, scale=den_inv[:, c, j:j + 1],
                                accum_out=sumsq[:, 2 * c + j:2 * c + j + 1])
                    return ins

                for c in range(NB):
                    act.wait_ge(m_scores, 8 * p + c + 1)
                    if c >= 1:
                        act.wait_ge(m_sT, 8 * p + c)
                    for j in range(2):
                        ins = A(dmat[:, j, :], ps[:, X[0], j * P:(j + 1) * P], ACT.Exp, bias=tok_gate[:, c, 0, j:j + 1])
                    ins.then_inc(m_decay, 1)
                    if c:
                        act.wait_ge(m_state, 8 * p + c)
                        for j in range(2):
                            ins = A(inter[:, j, :], ps[:, X[3], j * (MV + 1):(j + 1) * (MV + 1)], ACT.Copy,
                                    scale=tok_gate[:, c, 1, j:j + 1])
                        ins.then_inc(m_inter, 1)
                        sum_squares(c - 1)
                    if c == 1:
                        o_tile(0)
                    if c == 3:
                        o_tile(1)
                    if c == 5:
                        z_tile(0)
                    if c == 7:
                        z_tile(1)
                gm_tile(p, 0)
                sum_squares(NB - 1).then_inc(m_sumsq, 1)
                act.wait_ge(m_var, p + 1)
                A(rstd[:], rstd[:], ACT.Sqrt).then_inc(m_root, 1)

            looped(act, PAIRS, mlstm_step)

            for half in range(2):
                if half == 0:
                    act.wait_ge(h_half_used, PAIRS)
                else:
                    act.wait_ge(tile_done, S5)
                part = slice(half * BANK, (half + 1) * BANK)
                for k in range(KT):
                    if half == 0 and k % 2 == 0:
                        act.wait_ge(u_ready, KV + k // 2 + 1)
                    A(hT_hi[:, k, part], U[:, k, part], ACT.Copy).then_inc(u_hi_ready, 1)
            gm_tile(PAIRS - 1, 1)
            act.wait_ge(u_split, 3 * KT)

            def branch_m_step(i):
                for j in range(2):
                    last = isinstance(i, int) and i == KT // 2 - 1 and j == 1
                    if not last:
                        act.wait_ge(branch_m, 2 * i + j + 1)
                        act.sem_inc(tile_out, 1)
                    act.wait_ge(wo_in[j], 16 * (i + 1))
                    row = ds(2 * i + j, 1)
                    A(wo_hi[:, row, :], wo_raw[:, row, :], ACT.Copy).then_inc(wo_hi_ready, 1)
                    if last:
                        act.wait_ge(merged_ready, KT - 1)
                        act.wait_ge(tile_done, S6 - 1)
                        A(mt_hi[0][:, 0:KT - 1, :], merged[:, 0:KT - 1, 0:P], ACT.Copy).then_inc(mt_hi_ready, 1)

            branch_m_step(0)
            with act.Fori(1, KT // 2 - 1) as i:
                branch_m_step(i)
            branch_m_step(KT // 2 - 1)

            act.wait_ge(merged_ready, KT)
            A(mt_hi[0][:, KT - 1:KT, :], merged[:, KT - 1:KT, 0:P], ACT.Copy).then_inc(mt_hi_ready, 1)
            act.wait_ge(tile_done, S6)

            def token_tile(n, j):
                A(mt_hi[j], merged[:, :, ds(P * n, P)], ACT.Copy).then_inc(mt_hi_ready, 1)

            token_tile(1, 1)
            act.wait_ge(branch_m, KT)
            act.sem_inc(tile_out, 1)
            act.wait_ge(merged_rest, 1)

            def out_step(i):
                for j in range(2):
                    for half in range(2):
                        part = slice(half * BANK, (half + 1) * BANK)
                        act.wait_ge(res_ready, 4 * i + 2 * j + half + 1)
                        if half == 1:
                            act.sem_inc(tile_out, 1)
                        A(squares[:, part], ev[j][:, part], ACT.Square, accum_out=sumsq[:, 2 * j + half:2 * j + half + 1])\
                            .then_inc(res_sumsq, 1)
                    if not (isinstance(i, int) and i == NB // 2 - 1):
                        token_tile(2 * (i + 1) + j, j)
                    act.wait_ge(res_var, 2 * i + j + 1)
                    A(rstd[:, j:j + 1], rstd[:, j:j + 1], ACT.Sqrt).then_inc(res_root, 1)

            out_step(0)
            with act.Fori(1, NB // 2 - 1) as i:
                out_step(i)
            out_step(NB // 2 - 1)

        @block.vector
        def _(dve):
            V = nc.vector

            def variance(t):
                dve.wait_ge(x_sumsq, t + 1)
                V.tensor_scalar(rstd[:, t:t + 1], sumsq[:, t:t + 1], 1.0 / D, EPS, ALU.mult, ALU.add).then_inc(x_var, 1)

            def normalised(t):
                dve.wait_ge(x_root, t + 1)
                V.reciprocal(rstd[:, t:t + 1], rstd[:, t:t + 1])
                dve.drain()
                V.tensor_scalar(xs[:, t, :], xs[:, t, :], rstd[:, t:t + 1], None, ALU.mult).then_inc(x_norm, 1)

            for half in range(2):
                variance(4 * half)
                for t in range(4 * half, 4 * half + 4):
                    if t % 4 < 3:
                        variance(t + 1)
                    normalised(t)
                for k in range(KT):
                    part = slice(half * BANK, (half + 1) * BANK)
                    dve.wait_ge(hT_hi_ready, KT * half + k + 1)
                    V.scalar_tensor_tensor(hT_lo[:, k, part], ps[:, BANKS[half][k], :], par[:, R_NORM + k:R_NORM + k + 1],
                                           hT_hi[:, k, part].bitcast(F32), ALU.mult, ALU.subtract).then_inc(hT_lo_ready, 1)

            i_, f_ = g_i[0:8, :], g_f[0:8, :]
            chunks = lambda a: a.rearrange("h (c n) -> h c n", n=P)
            logf, m_, b_ = g_t2[0:8, :], g_t3[0:8, :], g_t5[0:8, :]
            dve.wait_ge(g_parts, 1)
            V.tensor_tensor(i_, i_, dense_ps(GATES)[64:72, :], ALU.add)
            V.tensor_tensor(f_, f_, dense_ps(GATES)[96:104, :], ALU.add).then_inc(g_sum, 1)
            dve.drain()
            dve.wait_ge(g_log, 1)
            V.tensor_scalar(logf, f_, 0.0, None, ALU.min)
            V.memset(g_t4[:], 0.0)
            V.memset(c_split[:], 0.0)
            V.memset(m_before[:], NEG)
            dve.drain()
            V.tensor_tensor(logf, logf, g_t1[0:8, :], ALU.subtract)
            dve.drain()
            V.tensor_tensor_scan(m_, logf, i_, NEG, ALU.add, ALU.max)
            for c in range(NB):
                V.tensor_tensor_scan(b_[:, c * P:(c + 1) * P], ones8, logf[:, c * P:(c + 1) * P], 0.0, ALU.mult, ALU.add)
            dve.drain()
            V.tensor_tensor(g_t4[0:8, :], i_, b_, ALU.subtract)
            V.tensor_tensor(b_, b_, m_, ALU.subtract)
            V.tensor_copy(m_before[:, 1:NB], chunks(m_)[:, 0:NB - 1, P - 1])
            dve.drain()
            V.tensor_tensor(chunks(f_), chunks(b_), m_before[:].unsqueeze(2).to_broadcast([MH, NB, P]), ALU.add)
            V.tensor_tensor(chunks(logf), chunks(g_t4[0:8, :]),
                            chunks(b_)[:, :, P - 1:P].to_broadcast([MH, NB, P]), ALU.add).then_inc(g_rows, 1)
            V.tensor_copy(c_hi[0:8, :], b_)
            dve.drain()
            V.tensor_tensor(c_split[32:40, :], b_, c_hi[0:8, :].bitcast(F32), ALU.subtract)
            V.tensor_copy(c_split[0:8, :], c_hi[0:8, :].bitcast(F32))
            for n in range(2):
                dve.wait_ge(v_turned, n + 1)
                for b in range(2):
                    ins = V.tensor_copy(v_tok[:, 4 * b:4 * b + 4, n * P:(n + 1) * P],
                                        ps[:, X[2 * n + b], :].rearrange("p (c n) -> p c n", n=P))
                ins.then_inc(v_ready, 1)

            def attention_step(g):
                dve.drain()
                until(dve, pv_done, NB * g)
                k_g = k_dup[:, ds(g, 1), :].rearrange("p a n -> p (a n)")
                V.tensor_copy(k_hi[:], k_g)
                dve.drain()
                V.tensor_tensor(k_lo[:], k_g, k_hi[:].bitcast(F32), ALU.subtract)
                V.tensor_copy(v_head[:], v_tok[:, :, ds(HD * g, HD)]).then_inc(kv_head_ready, 1)

                for h in range(GR):
                    j, r = divmod(h, 2)
                    rows = slice(64 * r, 64 * r + 64)
                    dve.wait_ge(q_hi_ready, GR * g + h + 1)
                    V.scalar_tensor_tensor(q_split[64:128, h, :], dense_ps(S2 + j)[rows, :], par[rows, ds(R_Q + j + 2 * g, 1)],
                                           q_split[0:64, h, :].bitcast(F32), ALU.add, ALU.subtract).then_inc(q_split_ready, 1)

                def combine(n):
                    pr = probs[n % 2]
                    dve.wait_ge(cur_copied, NB * g + n + 1)
                    dve.sem_inc(passed, 1)
                    if n:
                        V.copy_predicated(pr[:], from_prev[:].unsqueeze(1).to_broadcast([P, GR, P]),
                                          both_blocks[:, :, 0, :])
                    else:
                        V.copy_predicated(pr[:], from_prev[:].unsqueeze(1).to_broadcast([P, GR, P]),
                                          neg_col[:].unsqueeze(1).to_broadcast([P, GR, P]))
                    dve.drain()
                    V.tensor_reduce(row_max[:], pr[:], AXX, ALU.max)
                    dve.drain()
                    sink = sink_tab[:, ds(GR * g, GR)]
                    V.scalar_tensor_tensor(row_max[:], row_max[:], HD ** -0.5, sink, ALU.mult, ALU.max)
                    dve.drain()
                    V.tensor_tensor(sink_in[:], sink, row_max[:], ALU.subtract)
                    V.tensor_scalar(neg_max[:], row_max[:], -1.0, None, ALU.mult).then_inc(max_ready, 1)

                def normalise(n):
                    pr = probs[n % 2]
                    dve.wait_ge(exp_ready, NB * g + n + 1)
                    V.tensor_tensor(row_inv[:], row_sum[:], sink_exp[:], ALU.add)
                    dve.drain()
                    V.tensor_scalar(row_inv[:], row_inv[:], 2.0, None, ALU.mult)
                    dve.drain()
                    V.reciprocal(row_inv[:], row_inv[:])
                    dve.drain()
                    V.tensor_tensor(pr[:], pr[:], row_inv[:].unsqueeze(2).to_broadcast([P, GR, P]), ALU.mult)\
                        .then_inc(probs_ready, 1)

                def select(n):
                    dve.wait_ge(probs_turned, NB * g + n + 1)
                    if n:
                        dve.wait_ge(pv_done, NB * g + n)
                    src = ps[:, X[2], :].rearrange("p (h n) -> p h n", n=P)
                    ins = V.tensor_tensor(pT_cur[:], src, cur_T[:].unsqueeze(1).to_broadcast([P, GR, P]), ALU.mult)
                    if n:
                        ins = V.tensor_tensor(pT_prev[:], src, prev_T[:].unsqueeze(1).to_broadcast([P, GR, P]), ALU.mult)
                    ins.then_inc(pT_ready, 1)

                def silu(j):
                    dve.wait_ge(z_tanh, 2 * g + j + 1)
                    V.scalar_tensor_tensor(silu_z[:, j, :], ev[j][:], 1.0, silu_z[:, j, :], ALU.add, ALU.mult)\
                        .then_inc(z_used, 1)

                for n in range(NB + 2):
                    if n < NB:
                        combine(n)
                    if 1 <= n <= NB:
                        select(n - 1)
                    if n >= COPIED + 2:
                        m = n - 2
                        dve.wait_ge(pv_done, NB * g + m + 1)
                        ins = V.tensor_tensor(U[:, ds(2 * g, 2), m * P:(m + 1) * P],
                                              ps[:, X[3], 0:2 * P].rearrange("p (j n) -> p j n", j=2),
                                              silu_z[:, :, m * P:(m + 1) * P], ALU.mult)
                        ins.then_inc(u_ready if m == NB - 1 else attn_gated, 1)
                    if n < NB:
                        normalise(n)
                    if n == 4:
                        silu(0)
                    if n == COPIED + 1:
                        silu(1)
                        dve.drain()
                    if n == NB:
                        dve.wait_ge(attn_ready, COPIED * (g + 1))
                        copied = U[:, ds(2 * g, 2), 0:COPIED * P]
                        V.tensor_tensor(copied, copied, silu_z[:, :, 0:COPIED * P], ALU.mult)

            looped(dve, KV, attention_step)

            dve.drain()
            for k in range(KT):
                dve.wait_ge(u_hi_ready, k + 1)
                V.tensor_tensor(u_lo[:, k, :], U[:, k, :], u_hi[:, k, :].bitcast(F32), ALU.subtract).then_inc(u_split, 1)

            def branch_a_step(i):
                for j in range(2):
                    dve.wait_ge(ga_in[j], 16 * (i + 1))
                    dve.wait_ge(tile_done, S3 + 1 + j + 2 * i)
                    V.scalar_tensor_tensor(ev[j][:], ev[j][:], 1.0, dense_ps(S3 + j), ALU.add, ALU.mult)\
                        .then_inc(branch_a, 1)

            looped(dve, KT // 2, branch_a_step)

            dve.wait_ge(tile_done, S4)
            V.memset(v1[:, :, :, MV:MV + 1], 1.0)
            for raw in (raw_q, raw_k):
                V.memset(raw[:, 0:3], 0.0)
            for r in range(2):
                V.memset(mq_pad[64 * (1 - r):64 * (1 - r) + 64, r, :], 0.0)

            def mlstm_step(p):
                t0 = S4 + 10 * p
                dve.drain()
                dve.wait_ge(tile_out, t0 + 1)
                V.tensor_copy(tok_gate[:], gate_T[:, :, :, ds(2 * p, 2)])
                V.tensor_copy(pair_decay[:], decay_tab[:, ds(p, 1), :].rearrange("p a c -> p (a c)"))
                V.tensor_copy(pair_norm[:], par[:, ds(R_MNORM + 2 * p, 2)])
                for j in range(2):
                    V.tensor_scalar(c_heads[:, j, :], c_split[:], head_col[:, ds(2 * p + j, 1)], None, ALU.mult)
                dve.drain()
                V.tensor_scalar(tok_gate[:, :, 1, :], tok_gate[:, :, 1, :], 0.5 * MK ** -0.5, None, ALU.mult)
                V.tensor_scalar(pair_norm[:], pair_norm[:], 0.25, None, ALU.mult).then_inc(m_tabs, 1)
                for j, (raw, dst) in enumerate(((raw_q, z_buf), (raw_k, mk_T))):
                    dve.wait_ge(tile_out, t0 + 1 + j)
                    tap = lambda n: par[:, ds(R_CONVW + 8 * n + 4 * j + p, 1)]
                    V.tensor_scalar(dst[:], raw[:, 3:T + 3], tap(3), par[:, ds(R_CONVB + 4 * j + p, 1)], ALU.mult, ALU.add)
                    for n in range(3):
                        dve.drain()
                        ins = V.scalar_tensor_tensor(dst[:], raw[:, n:T + n], tap(n), dst[:], ALU.mult, ALU.add)
                    ins.then_inc(m_conv, 1)
                    dve.wait_ge(m_tanh, 2 * p + j + 1)
                    if j == 0:
                        for r in range(2):
                            rows = slice(64 * r, 64 * r + 64)
                            ins = V.scalar_tensor_tensor(mq_pad[rows, r, :], tanh_buf[rows, :], 1.0, z_buf[rows, :],
                                                         ALU.add, ALU.mult)
                    else:
                        ins = V.scalar_tensor_tensor(mk_T[:], tanh_buf[:], 1.0, mk_T[:], ALU.add, ALU.mult)
                    ins.then_inc(m_qk, 1)
                for j in range(2):
                    dve.wait_ge(m_v_turned, 2 * p + j + 1)
                    for b in range(2):
                        ins = V.tensor_copy(v1[:, 4 * b:4 * b + 4, j, 0:MV],
                                            ps[:, X[2 * j + b], :].rearrange("p (c n) -> p c n", n=P))
                    ins.then_inc(m_v_ready, 1)

                def z_part(j):
                    dve.wait_ge(mz_tanh, 2 * p + j + 1)
                    V.scalar_tensor_tensor(gates[:, j, :], gates[:, j, :], 1.0, z_buf[:], ALU.add, ALU.mult)
                    dve.drain()
                    V.scalar_tensor_tensor(gates[:, j, :], tanh_buf[:], 1.0, gates[:, j, :], ALU.add, ALU.mult)\
                        .then_inc(mz_used, 1)

                for c in range(NB):
                    dve.wait_ge(m_decay, 8 * p + c + 1)
                    for j in range(2):
                        V.scalar_tensor_tensor(s_T[:, j, :], ps[:, X[1], j * P:(j + 1) * P], 0.25 * MK ** -0.5,
                                               dmat[:, j, :], ALU.mult, ALU.mult)
                    for j in range(2):
                        ins = V.tensor_scalar(k_w[:, j, :], ps[:, X[1], 2 * P + MK * j:2 * P + MK * (j + 1)],
                                              tok_gate[:, c, 2, j:j + 1], 0.5, ALU.mult, ALU.mult)
                    ins.then_inc(m_sT, 1)
                    dve.wait_ge(m_prod, 8 * p + c + 1)
                    num = ps[:, X[2], 0:2 * (MV + 1)]
                    h_c = h_tok[:, c].rearrange("p j n -> p (j n)")
                    new = ps[:, X[2], 2 * (MV + 1):3 * (MV + 1)]
                    if c == 0:
                        V.tensor_copy(h_c, num)
                        V.tensor_copy(state[:], new).then_inc(m_state, 1)
                    else:
                        if c < NB - 1:
                            V.scalar_tensor_tensor(state[:], state[:], pair_decay[:, c:c + 1], new, ALU.mult, ALU.add)
                        dve.wait_ge(m_inter, 7 * p + c)
                        V.tensor_tensor(h_c, num, inter[:].rearrange("p j n -> p (j n)"), ALU.add).then_inc(m_state, 1)
                    dve.drain()
                    d = h_tok[:, c, :, MV]
                    V.scalar_tensor_tensor(den[:], d, -1.0, d, ALU.mult, ALU.max)
                    dve.drain()
                    V.tensor_tensor(den[:], den[:], tok_gate[:, c, 3, :], ALU.max)
                    dve.drain()
                    V.reciprocal(den_inv[:, c, :], den[:]).then_inc(m_den, 1)
                    if c == 6:
                        z_part(0)
                z_part(1)
                dve.wait_ge(m_sumsq, p + 1)
                V.tensor_scalar(rstd[:], sumsq[:], 1.0 / MV, EPS, ALU.mult, ALU.add).then_inc(m_var, 1)
                dve.wait_ge(m_root, p + 1)
                V.reciprocal(rstd[:], rstd[:])
                dve.drain()
                V.tensor_tensor(rstd[:], rstd[:], den_inv[:].rearrange("p c j -> p (c j)"), ALU.mult)
                dve.drain()
                hv = h_tok[:].rearrange("p c j n -> p (c j) n")[:, :, 0:MV]
                V.tensor_tensor(hv, hv, rstd[:].unsqueeze(2).to_broadcast([P, 2 * NB, MV]), ALU.mult).then_inc(m_h, 1)
                dve.wait_ge(m_h_turned, p + 1)
                for j in range(2):
                    for b in range(2):
                        part = slice(b * BANK, (b + 1) * BANK)
                        ins = V.scalar_tensor_tensor(U[:, ds(j + 2 * p, 1), part].rearrange("p a n -> p (a n)"),
                                                     ps[:, X[2 * j + b], :], pair_norm[:, j:j + 1], gates[:, j, part],
                                                     ALU.mult, ALU.mult)
                ins.then_inc(u_ready, 1)

            looped(dve, PAIRS, mlstm_step)

            dve.drain()
            for half in range(2):
                part = slice(half * BANK, (half + 1) * BANK)
                for k in range(KT):
                    dve.wait_ge(u_hi_ready, KT * (half + 1) + k + 1)
                    V.tensor_tensor(hT_lo[:, k, part], U[:, k, part], hT_hi[:, k, part].bitcast(F32), ALU.subtract)\
                        .then_inc(u_split, 1)

            def branch_m_step(i):
                for j in range(2):
                    row = ds(2 * i + j, 1)
                    last = isinstance(i, int) and i == KT // 2 - 1 and j == 1

                    def split_wo():
                        dve.wait_ge(wo_hi_ready, 2 * i + j + 1)
                        V.tensor_tensor(wo_lo[:, row, :], wo_raw[:, row, :], wo_hi[:, row, :].bitcast(F32), ALU.subtract)\
                            .then_inc(wo_split, 1)

                    if last:
                        split_wo()
                        dve.wait_ge(mt_hi_ready, 1)
                        V.tensor_tensor(mt_lo[0][:, 0:KT - 1, :], merged[:, 0:KT - 1, 0:P],
                                        mt_hi[0][:, 0:KT - 1, :].bitcast(F32), ALU.subtract).then_inc(mt_ready, 1)
                    if later(i):
                        dve.drain()
                    else:
                        dve.wait_ge(gm_out[j], 16 * PAIRS)
                    dve.wait_ge(th_in[j], 16 * (i + 1))
                    dve.wait_ge(merged_in[j], 16 * (i + 1))
                    dve.wait_ge(tile_done, S5 + 1 + 2 * i + j)
                    for part in (slice(0, 2 * P), slice(2 * P, T)) if last else (slice(0, T),):
                        ins = V.scalar_tensor_tensor(ev[j][:, part], th_gm[j][:, part], 1.0, dense_ps(S5 + j)[:, part],
                                                     ALU.add, ALU.mult)
                        if part.stop == T:
                            ins.then_inc(branch_m, 1)
                        dve.drain()
                        piece = merged[:, row, part].rearrange("p a n -> p (a n)")
                        V.tensor_tensor(piece, piece, ev[j][:, part], ALU.add)\
                            .then_inc(merged_rest if last and part.stop == T else merged_ready, 1)
                        if part.stop == 2 * P:
                            dve.wait_ge(mt_hi_ready, 2)
                            V.tensor_tensor(mt_lo[0][:, KT - 1:KT, :], merged[:, KT - 1:KT, 0:P],
                                            mt_hi[0][:, KT - 1:KT, :].bitcast(F32), ALU.subtract).then_inc(mt_ready, 1)
                    if not last:
                        split_wo()

            branch_m_step(0)
            with dve.Fori(1, KT // 2 - 1) as i:
                branch_m_step(i)
            branch_m_step(KT // 2 - 1)

            def token_tile(n, j):
                dve.wait_ge(mt_hi_ready, n + 2)
                V.tensor_tensor(mt_lo[j], merged[:, :, ds(P * n, P)], mt_hi[j].bitcast(F32), ALU.subtract).then_inc(mt_ready, 1)

            token_tile(1, 1)
            dve.wait_ge(fn_in, 16)

            def out_step(i):
                for j in range(2):
                    dve.wait_ge(x_again[j], 16 * (i + 1))
                    if later(i):
                        dve.wait_ge(y_out[j], 16 * i)
                    for half in range(2):
                        part = slice(half * BANK, (half + 1) * BANK)
                        if half == 0:
                            dve.wait_ge(half_done, 2 * i + j + 1)
                        else:
                            dve.wait_ge(tile_done, S6 + 1 + 2 * i + j)
                        V.scalar_tensor_tensor(ev[j][:, part], dense_ps(S6 + j)[:, part], 0.5, th_gm[j][:, part],
                                               ALU.mult, ALU.add).then_inc(res_ready, 1)
                    r = rstd[:, j:j + 1]
                    dve.wait_ge(res_sumsq, 4 * i + 2 * j + 2)
                    V.tensor_tensor(r, sumsq[:, 2 * j:2 * j + 1], sumsq[:, 2 * j + 1:2 * j + 2], ALU.add)
                    dve.drain()
                    V.tensor_scalar(r, r, 1.0 / D, EPS, ALU.mult, ALU.add).then_inc(res_var, 1)
                    if not (isinstance(i, int) and i == NB // 2 - 1):
                        token_tile(2 * (i + 1) + j, j)
                    dve.wait_ge(res_root, 2 * i + j + 1)
                    V.reciprocal(r, r)
                    dve.drain()
                    last = isinstance(i, int) and i == NB // 2 - 1 and j == 1
                    for part in (slice(0, BANK), slice(BANK, D)) if last else (slice(0, D),):
                        V.scalar_tensor_tensor(ev[j][:, part], ev[j][:, part], r, fnw[:, part], ALU.mult, ALU.mult)\
                            .then_inc(y_ready, 1)

            out_step(0)
            with dve.Fori(1, NB // 2 - 1) as i:
                out_step(i)
            out_step(NB // 2 - 1)


def kernel(x, norm_w, w_in, b_in, attn_sinks, conv_w, conv_b, mlstm_norm_w, w_branch_attn, w_branch_mlstm,
           w_out, final_norm_w):
    import numpy as np
    import concourse.bacc as bacc
    from concourse.bass_utils import run_bass_kernel_spmd

    ins = {"x": x[0], "norm_w": norm_w[0], "w_in": w_in[0], "b_in": b_in[0], "attn_sinks": attn_sinks[0],
           "conv_w": conv_w[0], "conv_b": conv_b[0], "mlstm_norm_w": mlstm_norm_w[0],
           "w_branch_attn": w_branch_attn[0], "w_branch_mlstm": w_branch_mlstm[0], "w_out": w_out[0],
           "final_norm_w": final_norm_w}
    nc = bacc.Bacc("TRN2", target_bir_lowering=False, num_devices=1)
    arrays, args = {}, []
    for name, a in ins.items():
        a = np.ascontiguousarray(a)
        arrays[f"in_{name}"] = a
        args.append(nc.dram_tensor(f"in_{name}", a.shape, mybir.dt.from_np(a.dtype), kind="ExternalInput").ap())
    args.append(nc.dram_tensor("out", (T, D), F32, kind="ExternalOutput").ap())
    build(nc, *args)
    r = run_bass_kernel_spmd(nc, [arrays], core_ids=[0])
    return r.results[0]["out"].reshape(1, T, D)
```
